# Optimizing a Trainium2 kernel written in Bass

```python
import math, functools
import jax, jax.numpy as jnp
from jax import lax
import numpy as np

D_MODEL = 1024
BATCH = 1
SEQ = 512
DEPTH = 1
DEC_BATCH = 8
DEC_SEQ = 8
PAST_LEN = 2048
PAGE_SIZE = 128

D_INNER = 2 * D_MODEL
SSD_HEAD_DIM = 64
SSD_HEADS = D_INNER // SSD_HEAD_DIM
SSD_GROUPS = 8
SSD_STATE = 128
SSD_CONV = 4
SSD_CHUNK = 128
CONV_DIM = D_INNER + 2 * SSD_GROUPS * SSD_STATE
ATT_HEADS = 16
ATT_HEAD_DIM = 64
KV_HEADS = 4
GQA_REP = ATT_HEADS // KV_HEADS
ATT_WIDTH = ATT_HEADS * ATT_HEAD_DIM
KV_WIDTH = KV_HEADS * ATT_HEAD_DIM
MOBA_BLOCK = 256
MOBA_TOPK = 3
Q_BLOCK = 128
ROT_DIM = ATT_HEAD_DIM // 4
ROPE_THETA = 500000.0
MEM_TOKENS = 256
MEM_HEADS = 4
MEM_HEAD_DIM = 256
MEM_WIDTH = MEM_HEADS * MEM_HEAD_DIM
D_FF = 2816
FFN_CONV = 3
N_BRANCH = 3
RMS_EPS = 1e-6
NEG_INF = -1e30
IN_SPLITS = (D_INNER, CONV_DIM, SSD_HEADS, ATT_WIDTH, KV_WIDTH, KV_WIDTH, MEM_WIDTH, N_BRANCH * D_MODEL)
D_IN_PROJ = D_INNER + CONV_DIM + SSD_HEADS + ATT_WIDTH + 2 * KV_WIDTH + MEM_WIDTH + N_BRANCH * D_MODEL

kernel_name = "hybrid_ssd_moba_mem_convffn_step"

def _rmsnorm(x, w):
    xf = x.astype(jnp.float32)
    y = xf * lax.rsqrt(jnp.mean(xf * xf, axis=-1, keepdims=True) + RMS_EPS)
    return (y * w.astype(jnp.float32)).astype(x.dtype)

def _gated_group_rmsnorm(y, z, w, out_dtype):
    g = y.astype(jnp.float32) * jax.nn.silu(z.astype(jnp.float32))
    shp = g.shape
    g = g.reshape(*shp[:-1], SSD_GROUPS, D_INNER // SSD_GROUPS)
    g = g * lax.rsqrt(jnp.mean(g * g, axis=-1, keepdims=True) + RMS_EPS)
    return (g.reshape(shp) * w.astype(jnp.float32)).astype(out_dtype)

def _split_cols(x, sizes):
    out, start = [], 0
    for s in sizes:
        out.append(x[..., start:start + s])
        start += s
    return out

def _causal_dwconv(x, buf, w, b):
    k = w.shape[0]
    l = x.shape[1]
    xp = jnp.concatenate([buf.astype(x.dtype), x], axis=1)
    y = xp[:, 0:l] * w[0]
    for i in range(1, k):
        y = y + xp[:, i:i + l] * w[i]
    return y + b, xp[:, xp.shape[1] - (k - 1):]

def _partial_rope(x, pos):
    half = ROT_DIM // 2
    inv = ROPE_THETA ** (-jnp.arange(half, dtype=jnp.float32) * 2.0 / ROT_DIM)
    ang = pos.astype(jnp.float32)[:, None] * inv[None, :]
    cos = jnp.cos(ang)[None, :, None, :]
    sin = jnp.sin(ang)[None, :, None, :]
    xf = x.astype(jnp.float32)
    x1, x2 = xf[..., :half], xf[..., half:ROT_DIM]
    out = jnp.concatenate([x1 * cos - x2 * sin, x2 * cos + x1 * sin, xf[..., ROT_DIM:]], axis=-1)
    return out.astype(x.dtype)

def _ssd_chunked(x, dt, a, bmat, cmat, init_state, chunk):
    f32 = jnp.float32
    b, l, h, p = x.shape
    g, n = bmat.shape[2], bmat.shape[3]
    r = h // g
    c = l // chunk
    cs = jnp.cumsum((dt * a).reshape(b, c, chunk, h), axis=2)
    xdt = (x.astype(f32) * dt[..., None]).reshape(b, c, chunk, g, r, p)
    bc = bmat.astype(f32).reshape(b, c, chunk, g, n)
    cc = cmat.astype(f32).reshape(b, c, chunk, g, n)
    causal = jnp.tril(jnp.ones((chunk, chunk), dtype=bool))
    seg = cs[:, :, :, None, :] - cs[:, :, None, :, :]
    lmat = jnp.exp(jnp.where(causal[None, None, :, :, None], seg, -jnp.inf)).reshape(b, c, chunk, chunk, g, r)
    cb = jnp.einsum("bcign,bcjgn->bcijg", cc, bc)
    y_diag = jnp.einsum("bcijgr,bcjgrp->bcigrp", cb[..., None] * lmat, xdt)
    decay_to_end = jnp.exp(cs[:, :, -1:, :] - cs).reshape(b, c, chunk, g, r)
    states = jnp.einsum("bcjgn,bcjgrp->bcgrpn", bc, decay_to_end[..., None] * xdt)
    chunk_decay = jnp.exp(cs[:, :, -1, :]).reshape(b, c, g, r)

    def step(s, inp):
        st, dec = inp
        return s * dec[..., None, None] + st, s

    s_final, s_start = lax.scan(step, init_state.astype(f32).reshape(b, g, r, p, n),
                                (jnp.moveaxis(states, 1, 0), jnp.moveaxis(chunk_decay, 1, 0)))
    s_start = jnp.moveaxis(s_start, 0, 1)
    y_off = jnp.einsum("bcign,bcgrpn->bcigrp", cc, s_start) * jnp.exp(cs).reshape(b, c, chunk, g, r)[..., None]
    y = (y_diag + y_off).reshape(b, l, h, p)
    return y, s_final.reshape(b, h, p, n)

def _moba_core(q, k_sel, v_sel, sel_ok, k_own, v_own, own_ok):
    f32 = jnp.float32
    h, nq, hd = q.shape
    qs = q.astype(f32) * (hd ** -0.5)
    s_own = jnp.einsum("grqd,gkd->grqk", qs.reshape(KV_HEADS, GQA_REP, nq, hd), k_own.astype(f32)).reshape(h, nq, -1)
    s_own = jnp.where(own_ok[None], s_own, NEG_INF)
    n_own = s_own.shape[-1]
    if k_sel is None:
        p = jax.nn.softmax(s_own, axis=-1)
        out = 0.0
    else:
        s_sel = jnp.where(sel_ok, jnp.einsum("hqd,hqkd->hqk", qs, k_sel.astype(f32)), NEG_INF)
        n_sel = s_sel.shape[-1]
        p = jax.nn.softmax(jnp.concatenate([s_sel, s_own], axis=-1), axis=-1)
        out = jnp.einsum("hqk,hqkd->hqd", p[..., :n_sel], v_sel.astype(f32))
        p = p[..., n_sel:]
    out = out + jnp.einsum("grqk,gkd->grqd", p.reshape(KV_HEADS, GQA_REP, nq, n_own), v_own.astype(f32)).reshape(h, nq, hd)
    return out.transpose(1, 0, 2).astype(q.dtype)

def _moba_prompt(q, k, v):
    b, s, h, hd = q.shape
    nb = -(-s // MOBA_BLOCK)
    pad = nb * MOBA_BLOCK - s
    nqb = s // Q_BLOCK
    topk = min(MOBA_TOPK, nb - 1)
    padw = ((0, 0), (0, pad), (0, 0), (0, 0))
    k_blk = jnp.pad(k, padw).reshape(b, nb, MOBA_BLOCK, KV_HEADS, hd).transpose(0, 3, 1, 2, 4)
    v_blk = jnp.pad(v, padw).reshape(b, nb, MOBA_BLOCK, KV_HEADS, hd).transpose(0, 3, 1, 2, 4)
    own_blk = jnp.arange(s) // MOBA_BLOCK
    q_b = q.reshape(b, nqb, Q_BLOCK, h, hd).transpose(0, 1, 3, 2, 4).reshape(b * nqb, h, Q_BLOCK, hd)
    sel_b, ok_b = None, None
    if topk > 0:
        k_mean = jnp.mean(k_blk.astype(jnp.float32), axis=3)
        gate = jnp.einsum("bsgrd,bgnd->bgrsn", q.astype(jnp.float32).reshape(b, s, KV_HEADS, GQA_REP, hd), k_mean).reshape(b, h, s, nb)
        gate = jnp.where(jnp.arange(nb)[None, :] < own_blk[:, None], gate, NEG_INF)
        _, sel = lax.top_k(gate, topk)
        ok = sel < own_blk[None, None, :, None]
        sel_b = sel.reshape(b, h, nqb, Q_BLOCK, topk).transpose(0, 2, 1, 3, 4).reshape(b * nqb, h, Q_BLOCK, topk)
        ok_b = ok.reshape(b, h, nqb, Q_BLOCK, topk).transpose(0, 2, 1, 3, 4).reshape(b * nqb, h, Q_BLOCK, topk)
    bidx = jnp.arange(b * nqb) // nqb
    qidx = jnp.arange(b * nqb) % nqb
    head_kv = jnp.arange(h) // GQA_REP

    def body(inp):
        qb, selq, okq, bi, qi = inp
        kb, vb = k_blk[bi], v_blk[bi]
        ob = qi * Q_BLOCK // MOBA_BLOCK
        k_own = lax.dynamic_index_in_dim(kb, ob, axis=1, keepdims=False)
        v_own = lax.dynamic_index_in_dim(vb, ob, axis=1, keepdims=False)
        qpos = qi * Q_BLOCK + jnp.arange(Q_BLOCK)
        kpos = ob * MOBA_BLOCK + jnp.arange(MOBA_BLOCK)
        own_ok = kpos[None, :] <= qpos[:, None]
        if selq is None:
            return _moba_core(qb, None, None, None, k_own, v_own, own_ok)
        k_sel = kb[head_kv[:, None, None], selq].reshape(h, Q_BLOCK, topk * MOBA_BLOCK, hd)
        v_sel = vb[head_kv[:, None, None], selq].reshape(h, Q_BLOCK, topk * MOBA_BLOCK, hd)
        sel_ok = jnp.repeat(okq, MOBA_BLOCK, axis=-1)
        return _moba_core(qb, k_sel, v_sel, sel_ok, k_own, v_own, own_ok)

    out = lax.map(body, (q_b, sel_b, ok_b, bidx, qidx))
    return out.reshape(b, s, h, hd)

def _moba_sample(q, k, v, cache_k, cache_v, page_table, layer):
    db, t, h, hd = q.shape
    n_pages = page_table.shape[1]
    past = n_pages * PAGE_SIZE
    n_full = past // MOBA_BLOCK
    own_start = n_full * MOBA_BLOCK
    topk = min(MOBA_TOPK, n_full)
    ppb = MOBA_BLOCK // PAGE_SIZE
    head_kv = jnp.arange(h) // GQA_REP
    row = jnp.arange(PAGE_SIZE)
    qpos = past + jnp.arange(t)
    kpos = own_start + jnp.arange(past - own_start + t)
    own_ok = kpos[None, :] <= qpos[:, None]

    def body(inp):
        qb, kb, vb, pt = inp
        k_past = cache_k[layer, pt].reshape(past, KV_HEADS, hd)
        v_tail = cache_v[layer, pt[own_start // PAGE_SIZE:]].reshape(-1, KV_HEADS, hd)
        k_own = jnp.concatenate([k_past[own_start:], kb.astype(k_past.dtype)], axis=0).transpose(1, 0, 2)
        v_own = jnp.concatenate([v_tail, vb.astype(v_tail.dtype)], axis=0).transpose(1, 0, 2)
        qh = qb.transpose(1, 0, 2)
        if topk == 0:
            return _moba_core(qh, None, None, None, k_own, v_own, own_ok)
        k_mean = jnp.mean(k_past[:own_start].astype(jnp.float32).reshape(n_full, MOBA_BLOCK, KV_HEADS, hd), axis=1)
        gate = jnp.einsum("grtd,ngd->grtn", qh.astype(jnp.float32).reshape(KV_HEADS, GQA_REP, t, hd), k_mean).reshape(h, t, n_full)
        _, sel = lax.top_k(gate, topk)
        phys = pt[sel[..., None] * ppb + jnp.arange(ppb)]
        gi = head_kv[:, None, None, None, None]
        k_sel = cache_k[layer, phys[..., None], row, gi].reshape(h, t, topk * MOBA_BLOCK, hd)
        v_sel = cache_v[layer, phys[..., None], row, gi].reshape(h, t, topk * MOBA_BLOCK, hd)
        sel_ok = jnp.ones((h, t, topk * MOBA_BLOCK), dtype=bool)
        return _moba_core(qh, k_sel, v_sel, sel_ok, k_own, v_own, own_ok)

    return lax.map(body, (q, k, v, page_table))

def _mem_attend(qm, mem_k, mem_v):
    b, l, _ = qm.shape
    q = qm.astype(jnp.float32).reshape(b, l, MEM_HEADS, MEM_HEAD_DIM) * (MEM_HEAD_DIM ** -0.5)
    s = jnp.einsum("blhd,bmhd->bhlm", q, mem_k.astype(jnp.float32))
    p = jax.nn.softmax(s, axis=-1)
    out = jnp.einsum("bhlm,bmhd->blhd", p, mem_v.astype(jnp.float32))
    return out.reshape(b, l, MEM_WIDTH).astype(qm.dtype)

def _layer(x, pos, mem_k, mem_v, ssm_init, conv_buf, ffn_buf, attend, lw):
    b, l, _ = x.shape
    xn = _rmsnorm(x, lw["norm1_w"])
    z, xbc, dt_raw, q, k, v, qm, gates = _split_cols(xn @ lw["w_in"], IN_SPLITS)
    xbc, conv_new = _causal_dwconv(xbc, conv_buf, lw["ssd_conv_w"], lw["ssd_conv_b"])
    xbc = jax.nn.silu(xbc)
    xs, bm, cm = _split_cols(xbc, (D_INNER, SSD_GROUPS * SSD_STATE, SSD_GROUPS * SSD_STATE))
    xs = xs.reshape(b, l, SSD_HEADS, SSD_HEAD_DIM)
    bm = bm.reshape(b, l, SSD_GROUPS, SSD_STATE)
    cm = cm.reshape(b, l, SSD_GROUPS, SSD_STATE)
    dt = jax.nn.softplus(dt_raw.astype(jnp.float32) + lw["dt_bias"].astype(jnp.float32))
    a = -jnp.exp(lw["a_log"].astype(jnp.float32))
    y, ssm_final = _ssd_chunked(xs, dt, a, bm, cm, ssm_init, math.gcd(l, SSD_CHUNK))
    y = y + lw["d_skip"].astype(jnp.float32)[:, None] * xs.astype(jnp.float32)
    y_ssd = _gated_group_rmsnorm(y.reshape(b, l, D_INNER), z, lw["ssd_norm_w"], x.dtype)
    q = _partial_rope(q.reshape(b, l, ATT_HEADS, ATT_HEAD_DIM), pos)
    k = _partial_rope(k.reshape(b, l, KV_HEADS, ATT_HEAD_DIM), pos)
    v = v.reshape(b, l, KV_HEADS, ATT_HEAD_DIM)
    y_att = attend(q, k, v).reshape(b, l, ATT_WIDTH)
    y_mem = _mem_attend(qm, mem_k, mem_v)
    gs = jax.nn.sigmoid(gates.astype(jnp.float32).reshape(b, l, N_BRANCH, D_MODEL)).astype(x.dtype)
    merged = (gs[:, :, 0] * (y_ssd @ lw["w_ssd_out"]) + gs[:, :, 1] * (y_att @ lw["w_attn_out"])
              + gs[:, :, 2] * (y_mem @ lw["w_mem_out"]))
    h = x + merged @ lw["w_o"]
    u = _rmsnorm(h, lw["norm2_w"]) @ lw["w_up"]
    uc, ffn_new = _causal_dwconv(u, ffn_buf, lw["ffn_conv_w"], lw["ffn_conv_b"])
    ug, uv = uc[..., :D_FF], uc[..., D_FF:]
    h = h + (jax.nn.silu(ug) * uv) @ lw["w_down"]
    return h, k, v, ssm_final.astype(x.dtype), conv_new, ffn_new

def setup_inputs(seed: int = 0) -> dict:
    key = jax.random.key(seed)
    keys = list(jax.random.split(key, 40))
    f32 = jnp.float32

    def nrm(shape, scale=1.0):
        return scale * jax.random.normal(keys.pop(), shape, f32)

    n_pages = PAST_LEN // PAGE_SIZE
    n_used = DEC_BATCH * n_pages
    n_phys = n_used + n_used // 4
    page_table = jax.random.permutation(keys.pop(), n_phys)[:n_used].reshape(DEC_BATCH, n_pages).astype(jnp.int32)
    dt0 = jnp.exp(jax.random.uniform(keys.pop(), (DEPTH, SSD_HEADS), f32, math.log(1e-3), math.log(1e-1)))
    dt_bias = dt0 + jnp.log(-jnp.expm1(-dt0))
    a_log = jnp.log(jax.random.uniform(keys.pop(), (DEPTH, SSD_HEADS), f32, 1.0, 16.0))
    return {
        "x_prompt": nrm((BATCH, SEQ, D_MODEL)),
        "x_sample": nrm((DEC_BATCH, DEC_SEQ, D_MODEL)),
        "cache_k": nrm((DEPTH, n_phys, PAGE_SIZE, KV_HEADS, ATT_HEAD_DIM)),
        "cache_v": nrm((DEPTH, n_phys, PAGE_SIZE, KV_HEADS, ATT_HEAD_DIM)),
        "cache_mem_k": nrm((DEPTH, DEC_BATCH, MEM_TOKENS, MEM_HEADS, MEM_HEAD_DIM)),
        "cache_mem_v": nrm((DEPTH, DEC_BATCH, MEM_TOKENS, MEM_HEADS, MEM_HEAD_DIM)),
        "state_ssm": nrm((DEPTH, DEC_BATCH, SSD_HEADS, SSD_HEAD_DIM, SSD_STATE), 0.3),
        "state_conv": nrm((DEPTH, DEC_BATCH, SSD_CONV - 1, CONV_DIM)),
        "state_ffn_conv": nrm((DEPTH, DEC_BATCH, FFN_CONV - 1, 2 * D_FF)),
        "page_table": page_table,
        "mem_prompt": nrm((BATCH, MEM_TOKENS, D_MODEL)),
        "norm1_w": 1.0 + nrm((DEPTH, D_MODEL), 0.02),
        "w_in": nrm((DEPTH, D_MODEL, D_IN_PROJ), D_MODEL ** -0.5),
        "ssd_conv_w": nrm((DEPTH, SSD_CONV, CONV_DIM), SSD_CONV ** -0.5),
        "ssd_conv_b": nrm((DEPTH, CONV_DIM), 0.01),
        "dt_bias": dt_bias,
        "a_log": a_log,
        "d_skip": 1.0 + nrm((DEPTH, SSD_HEADS), 0.1),
        "ssd_norm_w": 1.0 + nrm((DEPTH, D_INNER), 0.02),
        "mem_norm_w": 1.0 + nrm((DEPTH, D_MODEL), 0.02),
        "w_mem_kv": nrm((DEPTH, D_MODEL, 2 * MEM_WIDTH), D_MODEL ** -0.5),
        "w_ssd_out": nrm((DEPTH, D_INNER, D_MODEL), D_INNER ** -0.5),
        "w_attn_out": nrm((DEPTH, ATT_WIDTH, D_MODEL), ATT_WIDTH ** -0.5),
        "w_mem_out": nrm((DEPTH, MEM_WIDTH, D_MODEL), MEM_WIDTH ** -0.5),
        "w_o": nrm((DEPTH, D_MODEL, D_MODEL), D_MODEL ** -0.5),
        "norm2_w": 1.0 + nrm((DEPTH, D_MODEL), 0.02),
        "w_up": nrm((DEPTH, D_MODEL, 2 * D_FF), D_MODEL ** -0.5),
        "ffn_conv_w": nrm((DEPTH, FFN_CONV, 2 * D_FF), FFN_CONV ** -0.5),
        "ffn_conv_b": nrm((DEPTH, 2 * D_FF), 0.01),
        "w_down": nrm((DEPTH, D_FF, D_MODEL), D_FF ** -0.5),
        "final_norm_w": 1.0 + nrm((D_MODEL,), 0.02),
    }

def reference(x_prompt, x_sample, cache_k, cache_v, cache_mem_k, cache_mem_v, state_ssm, state_conv,
              state_ffn_conv, page_table, mem_prompt, norm1_w, w_in, ssd_conv_w, ssd_conv_b, dt_bias, a_log,
              d_skip, ssd_norm_w, mem_norm_w, w_mem_kv, w_ssd_out, w_attn_out, w_mem_out, w_o, norm2_w, w_up,
              ffn_conv_w, ffn_conv_b, w_down, final_norm_w):
    b_p, s_p, _ = x_prompt.shape
    n_mem = mem_prompt.shape[1]
    pos_p = jnp.arange(s_p, dtype=jnp.int32)
    pos_s = page_table.shape[1] * PAGE_SIZE + jnp.arange(x_sample.shape[1], dtype=jnp.int32)
    hp, hs = x_prompt, x_sample
    kp_l, vp_l, mkp_l, mvp_l, sp_l, cp_l, fp_l = [], [], [], [], [], [], []
    ks_l, vs_l, ss_l, cs_l, fs_l = [], [], [], [], []
    for l in range(DEPTH):
        lw = {"norm1_w": norm1_w[l], "w_in": w_in[l], "ssd_conv_w": ssd_conv_w[l], "ssd_conv_b": ssd_conv_b[l],
              "dt_bias": dt_bias[l], "a_log": a_log[l], "d_skip": d_skip[l], "ssd_norm_w": ssd_norm_w[l],
              "w_ssd_out": w_ssd_out[l], "w_attn_out": w_attn_out[l], "w_mem_out": w_mem_out[l], "w_o": w_o[l],
              "norm2_w": norm2_w[l], "w_up": w_up[l], "ffn_conv_w": ffn_conv_w[l], "ffn_conv_b": ffn_conv_b[l],
              "w_down": w_down[l]}
        mkv = (_rmsnorm(mem_prompt, mem_norm_w[l]) @ w_mem_kv[l]).reshape(b_p, n_mem, 2, MEM_HEADS, MEM_HEAD_DIM)
        mk_p, mv_p = mkv[:, :, 0], mkv[:, :, 1]
        ssm0 = jnp.zeros((b_p, SSD_HEADS, SSD_HEAD_DIM, SSD_STATE), x_prompt.dtype)
        conv0 = jnp.zeros((b_p, SSD_CONV - 1, CONV_DIM), x_prompt.dtype)
        ffn0 = jnp.zeros((b_p, FFN_CONV - 1, 2 * D_FF), x_prompt.dtype)
        hp, kp, vp, sp, cp, fp = _layer(hp, pos_p, mk_p, mv_p, ssm0, conv0, ffn0, _moba_prompt, lw)
        attend_s = functools.partial(_moba_sample, cache_k=cache_k, cache_v=cache_v, page_table=page_table, layer=l)
        hs, ks, vs, ss, cs, fs = _layer(hs, pos_s, cache_mem_k[l], cache_mem_v[l], state_ssm[l], state_conv[l],
                                        state_ffn_conv[l], attend_s, lw)
        kp_l.append(kp); vp_l.append(vp); mkp_l.append(mk_p); mvp_l.append(mv_p)
        sp_l.append(sp); cp_l.append(cp); fp_l.append(fp)
        ks_l.append(ks); vs_l.append(vs); ss_l.append(ss); cs_l.append(cs); fs_l.append(fs)
    y_prompt = _rmsnorm(hp, final_norm_w)
    y_sample = _rmsnorm(hs, final_norm_w)
    return (y_prompt, y_sample, jnp.stack(kp_l), jnp.stack(vp_l), jnp.stack(mkp_l), jnp.stack(mvp_l),
            jnp.stack(sp_l), jnp.stack(cp_l), jnp.stack(fp_l), jnp.stack(ks_l), jnp.stack(vs_l),
            jnp.stack(ss_l), jnp.stack(cs_l), jnp.stack(fs_l))


_drawn_inputs = setup_inputs


def setup_inputs(seed=0):
    import zlib

    import numpy as np

    out = dict(_drawn_inputs(seed))
    spreads = {}
    factors = {'ssd_conv_b': 3.426,
     'ssd_norm_w': 5.296,
     'mem_norm_w': 8.732,
     'norm2_w': 2.778,
     'ffn_conv_b': 8.0,
     'final_norm_w': 8.046,
     'cache_k': 4.396,
     'cache_v': 4.098,
     'cache_mem_k': 3.01}
    for name, (base, spread) in spreads.items():
        noise = np.random.default_rng([zlib.crc32(name.encode()), seed]).standard_normal(out[name].shape)
        drawn = base * np.exp(spread * noise) if base else spread * noise
        out[name] = __import__('jax').numpy.asarray(drawn.astype(out[name].dtype))
    for name, factor in factors.items():
        out[name] = (out[name] * factor).astype(out[name].dtype)
    return out
```

```python
from contextlib import ExitStack

import numpy as np

import concourse.bass as bass
from concourse import mybir

F32 = mybir.dt.float32
F32R = mybir.dt.float32r
ALU = mybir.AluOpType
ACT = mybir.ActivationFunctionType
AX = mybir.AxisListType.X

P = 128
D = 1024
KT = D // P
SEQ = 512
NB, DT = 8, 8
TS = NB * DT
T = SEQ + TS
HALF = T // 2
CH = SEQ // P
HEADS = 32
GROUPS = 8
GH = HEADS // GROUPS
SCONV, FCONV = 4, 3
NCV = 32
FT = 22
PAD = SCONV - 1
PBUF = SEQ + PAD
SB1 = DT + PAD
CW = PBUF + NB * SB1
FPAD = FCONV - 1
FPB = SEQ + FPAD
FSB = DT + FPAD
FW = FPB + NB * FSB
PAST, PAGE = 2048, 128
NPG = PAST // PAGE
MEM = 256
EPS = 1e-6
NEG = -1e30


def offsets(parts):
    at, out = 0, {}
    for name, width in parts:
        out[name] = (at, width)
        at += width
    return out, at


CST, CST_W = offsets([
    ("ident", P), ("ones", P), ("upto_p", P), ("after_p", P), ("upto_s", TS), ("after_s", TS),
    ("same_b", NB), ("rot", P), ("swap", P), ("causal", P), ("own", DT), ("blk_lt", 64),
    ("cos", T), ("sin", T)])
FEA, FEA_W = offsets([
    ("norm1", KT), ("norm2", KT), ("memn", KT), ("final", KT), ("ssdn", 16), ("dskip", 16),
    ("dtb", 1), ("alog", 1), ("convw", NCV * SCONV), ("convb", NCV), ("hist", NCV * NB * PAD),
    ("fconvw", 2 * FT * FCONV), ("fconvb", 2 * FT), ("fhist", 2 * FT * NB * FPAD)])

N_DT = 1
N_GRP = 6
FFN_PIECES = (8, 8, 6)


class Chain:

    def __init__(self, eng, sem):
        self.e, self.sem, self.base, self.i, self.per, self.local = eng, sem, 0, None, 0, 0

    def value(self):
        v = self.base + self.local
        return v if self.i is None else self.i * self.per + v

    def __call__(self, ins):
        ins.then_inc(self.sem, 1)
        self.local += 1
        self.e.wait_ge(self.sem, self.value())

    def enter(self, i, per):
        self.base, self.local, self.i, self.per = self.base + self.local, 0, i, per

    def leave(self, trips):
        assert self.local == self.per, f"links of a turn: {self.local}, not {self.per}"
        self.base, self.local, self.i = self.base + trips * self.per, 0, None


def build_program(nc, io):
    ctx = ExitStack()
    with ctx:
        def sb(name, shape, dt=F32):
            return ctx.enter_context(nc.sbuf_tensor(name, shape, dt))

        def stage_sb(stack, name, shape, dt=F32):
            return stack.enter_context(nc.sbuf_tensor(name, shape, dt))

        def sem(name):
            return ctx.enter_context(nc.semaphore(name))

        cst = sb("cst", [P, CST_W])
        fea = sb("fea", [P, FEA_W])
        xn_hi, xn_lo = sb("xn_hi", [P, KT, T], F32R), sb("xn_lo", [P, KT, T], F32R)
        y_hi, y_lo = sb("y_hi", [P, KT, T], F32R), sb("y_lo", [P, KT, T], F32R)
        merged = sb("merged", [P, KT, T])
        w_raw = sb("w_raw", [P, 2, D])
        w_hi, w_lo = sb("w_hi", [P, 2, D], F32R), sb("w_lo", [P, 2, D], F32R)
        dt_tok = sb("dt_tok", [P, 2, CH + 1, HEADS])
        dec = sb("dec", [P, CH + 1, HEADS])
        tot = sb("tot", [P, CH * HEADS + NB * HEADS])

        tails = sb("tails", [P, NCV, PAD + NB * PAD])
        w_taken = sem("w_taken")
        vown = sb("vown", [DT, 256])
        pad1 = sb("pad1", [P, 1])
        ftails = sb("ftails", [P, 2 * FT, FPAD + NB * FPAD])

        def c_(name, p=P):
            at, w = CST[name]
            return cst[0:p, at:at + w]

        def f_(name, i=0, n=1, p=P):
            at, _ = FEA[name]
            return fea[0:p, at + i * n:at + i * n + n]

        ident, ones = c_("ident"), c_("ones")

        dps = ctx.enter_context(nc.psum_tensor("dps", [P, 2, 2, 512], F32))
        psA = ctx.enter_context(nc.psum_tensor("psA", [P, 512], F32))
        psLE = ctx.enter_context(nc.psum_tensor("psLE", [P, 2, 512], F32))
        psL, psE = psLE[:, 0, :], psLE[:, 1, :]
        psY = ctx.enter_context(nc.psum_tensor("psY", [P, 512], F32))

        w_landed = [sem("w_landed0"), sem("w_landed1")]
        w_hi_done = sem("w_hi_done")
        w_split = [sem("w_split0"), sem("w_split1")]
        dense_full = [sem("dense_full0"), sem("dense_full1")]
        dense_free = [sem("dense_free0"), sem("dense_free1")]
        const_in, x_in = sem("const_in"), sem("x_in")
        out_done = sem("out_done")
        dve_step, act_step = sem("dve_step"), sem("act_step")
        stage_done, passed = [sem("pe_stage"), sem("act_stage"), sem("dve_stage")], [0]

        pe_prog, act_prog, dve_prog = [], [], []
        chains = {}

        def edge(name):
            passed[0] += 1
            count = passed[0]

            def side(own):
                def f(e):
                    e.drain().then_inc(stage_done[own], 1)
                    for k in range(3):
                        e.wait_ge(stage_done[k], count)
                return f
            pe_prog.append(side(0)); act_prog.append(side(1)); dve_prog.append(side(2))

        def halves(ps, par, width=T):
            return ps[:, par, :, 0:HALF]

        def two(ap):
            return ap.rearrange("p (h c) -> p h c", h=2)

        def slot(n0, u, i=0, nb=0):
            return (n0 + u) % 2, (n0 + u) // 2 + i * (nb // 2)

        def pe_dense(pe, tile, hi, lo, nk=KT, width=T):
            par, k0 = tile
            pe.wait_ge(w_split[par], k0 + 1)
            pe.wait_ge(dense_free[par], k0)
            spans = [(0, 0, width)] if width <= 512 and width != T else [(0, 0, HALF), (1, HALF, HALF)]
            for k in range(nk):
                wh, wl = w_hi[:, par, k * P:(k + 1) * P], w_lo[:, par, k * P:(k + 1) * P]
                for j, (w, a) in enumerate(((wh, hi), (wh, lo), (wl, hi))):
                    for b, c0, cw in spans:
                        mm = pe.matmul(dps[:, par, b, 0:cw], w, a[:, k, c0:c0 + cw],
                                       start=(k == 0 and j == 0), stop=(k == nk - 1 and j == 2))
            mm.then_inc(dense_full[par], 1)

        final_waits = []
        nstream = [0]

        def take(count):
            n = nstream[0]
            nstream[0] += count
            return n

        norm_sems = [sem(f"norm_{k}") for k in ("sq_ready", "sq_used", "mean", "root", "t_ready", "hi_ready")]
        norm_count = [0]

        def norm_stage(name, src, wname, hi, lo, width=T, kts=KT, ready=(), half_in=1.0, plain=None):
            st = ExitStack()
            sq = stage_sb(st, f"{name}_sq", [P, 2, width])
            rs = stage_sb(st, f"{name}_rs", [P, width])
            t = stage_sb(st, f"{name}_t", [P, 2, width])
            st.close()
            sq_ready, sq_used, mean_ready, root_ready, t_ready, hi_ready = norm_sems
            norms = norm_count[0]
            norm_count[0] += 1
            done = norms * kts
            if width == T:
                sp = lambda ap: two(ap)
                ps = dps[:, 0, :, 0:HALF]
                spans = [(0, 0, HALF), (1, HALF, HALF)]
            else:
                sp = lambda ap: ap
                ps = dps[:, 0, 0, 0:width]
                spans = [(0, 0, width)]

            def pe_f(pe):
                for k in range(kts):
                    pe.wait_ge(sq_ready, done + k + 1)
                    for b, c0, cw in spans:
                        mm = pe.matmul(dps[:, 0, b, 0:cw], ones, sq[:, k % 2, c0:c0 + cw],
                                       start=(k == 0), stop=(k == kts - 1))
                    mm.then_inc(sq_used, 1)

            def act_f(act):
                for s, v in ready:
                    act.wait_ge(s, v)
                for k in range(kts):
                    if k >= 2:
                        act.wait_ge(sq_used, done + k - 1)
                    act.activation(sq[:, k % 2, :], src[:, k, :], ACT.Square).then_inc(sq_ready, 1)
                act.wait_ge(mean_ready, norms + 1)
                act.activation(rs[:], rs[:], ACT.Sqrt).then_inc(root_ready, 1)
                if hi is not None:
                    for k in range(kts):
                        act.wait_ge(t_ready, done + k + 1)
                        act.activation(hi[:, k, 0:width], t[:, k % 2, :], ACT.Copy).then_inc(hi_ready, 1)

            def dve_f(dve):
                link = chains["dve"]
                for s, v in ready:
                    dve.wait_ge(s, v)
                dve.wait_ge(sq_used, done + kts)
                dve.tensor_scalar(sp(rs[:]), ps, 1.0 / D, EPS, ALU.mult, ALU.add).then_inc(mean_ready, 1)
                dve.wait_ge(root_ready, norms + 1)
                link(dve.reciprocal(rs[:], rs[:]))
                for k in range(kts):
                    if hi is None:
                        dve.scalar_tensor_tensor(plain[:, k, :], src[:, k, :], f_(wname, k), rs[:],
                                                 ALU.mult, ALU.mult).then_inc(t_ready, 1)
                        continue
                    if k >= 2:
                        dve.wait_ge(hi_ready, done + k - 1)
                    dve.scalar_tensor_tensor(t[:, k % 2, :], src[:, k, :], f_(wname, k), rs[:],
                                             ALU.mult, ALU.mult).then_inc(t_ready, 1)
                    dve.wait_ge(hi_ready, done + k + 1)
                    link(dve.tensor_tensor(lo[:, k, 0:width], t[:, k % 2, :], hi[:, k, 0:width].bitcast(F32),
                                           ALU.subtract))
            pe_prog.append(pe_f); act_prog.append(act_f); dve_prog.append(dve_f)
            return done + kts

        s0 = ExitStack()
        x_t = stage_sb(s0, "x_t", [P, KT, T])

        def act_load(act):
            act.dma_start(cst[:], io["cst"]).then_inc(const_in, 16)
            act.dma_start(fea[:], io["fea"]).then_inc(const_in, 16)
            act.dma_start(x_t[:], io["x_t"]).then_inc(x_in, 16)

        act_prog.append(act_load)
        pe_prog.append(lambda pe: pe.wait_ge(const_in, 32))

        def dve_scale(dve):
            link = chains["dve"]
            dve.wait_ge(const_in, 32)
            for name, w in (("convw", NCV * SCONV), ("convb", NCV), ("ssdn", 16),
                            ("fconvw", FT * FCONV), ("fconvb", FT)):
                a, _ = FEA[name]
                link(dve.tensor_scalar(fea[:, a:a + w], fea[:, a:a + w], 0.5, None, ALU.mult))
        dve_prog.append(dve_scale)
        norm_stage("norm1", x_t, "norm1", xn_hi, xn_lo, ready=((const_in, 32), (x_in, 16)))
        s0.close()
        edge("edge_norm1")

        s1 = ExitStack()
        n0 = take(N_DT)
        dtv = [stage_sb(s1, f"dtv{i}", [HEADS, T]) for i in range(6)]
        acol = stage_sb(s1, "acol", [HEADS, 1])
        da_b = stage_sb(s1, "da_b", [TS, NB, HEADS])
        dt_x, dt_e, dt_l, dt_t, dt_f = (sem(f"dt_{k}") for k in ("x", "exp", "ln", "tr", "full"))
        dt_n, dt_u, a_neg, dt_tokd = sem("dt_n"), sem("dt_u"), sem("dt_a"), sem("dt_tokd")
        dtx, dtr, dtn, dte, dtu, dtl = dtv

        def pe_dt(pe):
            pe_dense(pe, slot(n0, 0), xn_hi, xn_lo)
            pe.wait_ge(dt_f, 1)
            for j, v in enumerate((dtx, dtr)):
                for c in range(CH + 1):
                    m = P if c < CH else TS
                    o = (j * (CH + 1) + c) * HEADS
                    tr = pe.transpose(psA[0:m, o:o + HEADS], v[:, c * P:c * P + m], cst[0:HEADS, CST["ident"][0]:CST["ident"][0] + HEADS])
            tr.then_inc(dt_t, 1)
            pe.wait_ge(dt_tokd, 1)
            da = dt_tok[:, 1, 0:CH, :].rearrange("p c h -> p (c h)")
            pe.matmul(psL[:, 0:CH * HEADS], c_("after_p"), da, start=True, stop=True)
            pe.matmul(psL[0:TS, 128:160], c_("after_s", TS), dt_tok[0:TS, 1, CH, :], start=True, stop=True)
            pe.matmul(psE[:, 0:CH * HEADS], ones, da, start=True, stop=True)
            pe.matmul(psE[:, 128:384], cst[0:TS, CST["ones"][0]:CST["ones"][0] + P],
                      da_b[:].rearrange("p b h -> p (b h)"), start=True, stop=True).then_inc(dt_t, 1)

        def act_dt(act):
            link = chains["act"]
            act.wait_ge(dense_full[0], 1)
            act.activation(two(dtx[:]), dps[0:HEADS, 0, :, 0:HALF], ACT.Identity, bias=f_("dtb", p=HEADS)).then_inc(dense_free[0], 1)
            act.activation(acol[:], f_("alog", p=HEADS), ACT.Exp).then_inc(a_neg, 1)
            act.wait_ge(dt_n, 1)
            act.activation(dte[:], dtn[:], ACT.Exp).then_inc(dt_e, 1)
            act.wait_ge(dt_u, 1)
            act.activation(dtl[:], dtu[:], ACT.Ln).then_inc(dt_l, 1)
            act.wait_ge(dt_t, 2)
            link(act.activation(dec[:, 0:CH, :].rearrange("p c h -> p (c h)"), psL[:, 0:128], ACT.Exp))
            link(act.activation(dec[0:TS, CH, :], psL[0:TS, 128:160], ACT.Exp))
            link(act.activation(tot[:], psE[:, 0:384], ACT.Exp))

        def dve_dt(dve):
            link = chains["dve"]
            tt = lambda o, a, b, op: link(dve.tensor_tensor(o, a, b, op))
            ts = lambda o, a, s, op: link(dve.tensor_scalar(o, a, s, None, op))
            dve.wait_ge(dense_free[0], 1)
            ts(dtr[:], dtx[:], 0.0, ALU.max)
            ts(dtn[:], dtx[:], -1.0, ALU.mult)
            dve.tensor_tensor(dtn[:], dtn[:], dtx[:], ALU.min).then_inc(dt_n, 1)
            dve.wait_ge(dt_e, 1)
            dve.tensor_scalar(dtu[:], dte[:], 1.0, None, ALU.add).then_inc(dt_u, 1)
            dve.wait_ge(dt_l, 1)
            ts(dtu[:], dtu[:], 1.0, ALU.subtract)
            ts(dtn[:], dtu[:], 0.0, ALU.is_equal)
            tt(dtl[:], dtl[:], dtn[:], ALU.add)
            tt(dtu[:], dtu[:], dtn[:], ALU.add)
            link(dve.reciprocal(dtu[:], dtu[:]))
            tt(dtl[:], dtl[:], dtu[:], ALU.mult)
            tt(dtl[:], dtl[:], dte[:], ALU.mult)
            tt(dtx[:], dtl[:], dtr[:], ALU.add)
            dve.wait_ge(a_neg, 1)
            link(dve.tensor_scalar(acol[:], acol[:], -1.0, None, ALU.mult))
            dve.tensor_scalar(dtr[:], dtx[:], acol[:], None, ALU.mult).then_inc(dt_f, 1)
            dve.wait_ge(dt_t, 1)
            link(dve.tensor_copy(dt_tok[:, :, 0:CH, :], psA[:, 0:320].rearrange("p (j c h) -> p j c h", j=2, c=CH + 1)[:, :, 0:CH, :]))
            link(dve.tensor_copy(dt_tok[0:TS, :, CH, :], psA[0:TS, 0:320].rearrange("p (j c h) -> p j c h", j=2, c=CH + 1)[:, :, CH, :]))
            dve.tensor_tensor(da_b[:], dt_tok[0:TS, 1:2, CH, :].to_broadcast([TS, NB, HEADS]),
                              c_("same_b", TS).rearrange("p (b o) -> p b o", o=1).to_broadcast([TS, NB, HEADS]),
                              ALU.mult).then_inc(dt_tokd, 1)

        pe_prog.append(pe_dt); act_prog.append(act_dt); dve_prog.append(dve_dt)
        s1.close()
        edge("edge_dt")

        ssd_stack = ExitStack()
        ss = lambda n, s, d=F32: stage_sb(ssd_stack, n, s, d)
        cbuf = ss("cbuf", [P, 2, CW])
        cout = ss("cout", [P, 2, CW])
        cth = ss("cth", [P, 2, CW])
        xg = ss("xg", [P, 2, T])
        bg, cg = ss("bg", [P, T]), ss("cg", [P, T])
        zg = ss("zg", [P, 2, T])
        yg = ss("yg", [P, 2, T])
        rhs_a = ss("rhs_a", [P, GH, P])
        cbm = ss("cbm", [P, P])
        btok = ss("btok", [P, P])
        xdt, xdtd = ss("xdt", [P, 256]), ss("xdtd", [P, 256])
        l_exp, e_exp = ss("l_exp", [P, 512]), ss("e_exp", [P, 512])
        state = ss("state", [P, 256])
        st_in = ss("st_in", [P, NB, 256])
        bm = ss("bm", [TS, NB, P])
        rstd = ss("rstd", [P, T])
        ssd_stack.close()

        cin_ready, conv_ready = sem("cin_ready"), sem("conv_ready")
        th_ready, feat_ready = sem("th_ready"), sem("feat_ready")
        zth_ready = sem("zth_ready")
        a_full, a_free, le_full, exp_ready = sem("a_full"), sem("a_free"), sem("le_full"), sem("exp_ready")
        rhs_ready, m_ready, y_full, y_free = sem("rhs_ready"), sem("m_ready"), sem("y_full"), sem("y_free")
        n_full, n_free = sem("n_full"), sem("n_free")
        st_landed, st_new = sem("st_landed"), sem("st_new")
        gsq_ready, gsum_full, gmean_ready, groot_ready = sem("gsq_ready"), sem("gsum_full"), sem("gmean_ready"), sem("groot_ready")
        gt_ready, ghi_ready = sem("gt_ready"), sem("ghi_ready")
        st_read = sem("st_read")
        ssm_ready = sem("ssm_ready")
        ssm_out = sem("ssm_out")

        def ssd_half(half):
            n0 = take(4 * N_GRP)
            p0 = n0 % 2
            CW_, CB_ = FEA["convw"][0], FEA["convb"][0]

            def dyn(ap2, off, w):
                return ap2[:, bass.ds(off, w)]

            def pe_f(pe):
                with pe.Fori(0, 4) as i:
                    G = i + 4 * half
                    for u in range(N_GRP):
                        pe_dense(pe, slot(n0, u, i, N_GRP), xn_hi, xn_lo)
                    pe.wait_ge(feat_ready, G * 4 + 4)
                    for c in range(CH + 1):
                        m = P if c < CH else TS
                        lo_, hi_ = c * P, c * P + m
                        last = c == CH
                        pe.wait_ge(a_free, G * 5 + c)
                        pe.matmul(psA[0:m, 384:384 + m], bg[:, lo_:hi_], cg[:, lo_:hi_], start=True, stop=True)
                        for q in range(2):
                            pe.transpose(psA[0:m, q * P:(q + 1) * P], xg[:, q, lo_:hi_], ident)
                        pe.transpose(psA[0:m, 256:384], bg[:, lo_:hi_], ident).then_inc(a_full, 1)
                        pe.wait_ge(rhs_ready, G * 5 + c + 1)
                        rows = P if not last else TS
                        rv = rhs_a[0:rows, :, 0:m]
                        aft = c_("after_p") if not last else c_("after_s", TS)
                        if c > 0:
                            pe.matmul(psE[:, 0:GH * m].rearrange("p (h i) -> p h i", h=GH),
                                      cst[0:rows, CST["ones"][0]:CST["ones"][0] + P], rv, start=True, stop=True)
                        mm = pe.matmul(psL[0:m, 0:GH * m].rearrange("p (h i) -> p h i", h=GH), aft, rv, start=True, stop=True)
                        mm.then_inc(le_full, 1)
                        pe.wait_ge(m_ready, G * 5 + c + 1)
                        pe.wait_ge(y_free, G * 5 + c)
                        lv = l_exp[0:rows, 0:GH * m].rearrange("p (h i) -> p h i", h=GH)
                        ev = e_exp[:, 0:GH * m].rearrange("p (h i) -> p h i", h=GH)
                        if last:
                            pe.wait_ge(st_landed, G * 16 + 16)
                            for b in range(NB):
                                for q in range(2):
                                    o = 2 * m + (b * 2 + q) * 16
                                    pe.matmul(psY[:, o:o + 16].rearrange("p (h t) -> p h t", h=2),
                                              st_in[:, b, q * P:(q + 1) * P], ev[:, 2 * q:2 * q + 2, b * DT:(b + 1) * DT],
                                              start=True, stop=True)
                        for q in range(2):
                            for hh in range(2):
                                h = 2 * q + hh
                                o = psY[hh * 64:hh * 64 + 64, q * m:(q + 1) * m]
                                mid = 0 < c < CH
                                mm = pe.matmul(o, xdt[0:rows, h * 64:h * 64 + 64], lv[:, h, :], start=True, stop=not mid)
                                if mid:
                                    pe.matmul(o, state[:, h * 64:h * 64 + 64], ev[:, h, :], start=False, stop=True)
                        if not last:
                            pe.matmul(psY[:, 256:512], btok[:], xdtd[:], start=True, stop=True).then_inc(y_full, 1)
                            continue
                        mm.then_inc(y_full, 1)
                        for r in range(4):
                            pe.wait_ge(n_free, G * 4 + r - 1) if r > 1 else None
                            bank = psL if r % 2 == 0 else psE
                            for b in (2 * r, 2 * r + 1):
                                mm = pe.matmul(bank[:, (b % 2) * 256:(b % 2) * 256 + 256], bm[:, b, :], xdtd[0:TS, :],
                                               start=True, stop=True)
                            mm.then_inc(n_full, 1)
                    pe.wait_ge(gsq_ready, G + 1)
                    for hf, bank in ((0, psL), (1, psE)):
                        for q in range(2):
                            mm = pe.matmul(bank[:, 0:HALF], ones, zg[:, q, hf * HALF:(hf + 1) * HALF], start=(q == 0), stop=(q == 1))
                    mm.then_inc(gsum_full, 1)

            def act_f(act):
                link = chains["act"]
                with act.Fori(0, 4) as i:
                    link.enter(i, 0)
                    G = i + 4 * half
                    act.wait_ge(ssm_out, G * 32)
                    act.dma_start(st_in[:], io["state_t"][bass.ds(G * P, P), :].rearrange("n (b q) -> n b q", b=NB)).then_inc(st_landed, 16)
                    for u in range(4):
                        par, k0 = slot(n0, u, i, N_GRP)
                        act.wait_ge(dense_full[par], k0 + 1)
                        if u >= 2:
                            act.wait_ge(conv_ready, G * 4 + u - 1)
                        cb = cbuf[:, u % 2, :]
                        tl = dyn(tails[:].rearrange("p n k -> p (n k)"), tail_at(G, u) * 27, 27)
                        act.activation(cb[:, PAD:PAD + HALF], dps[:, par, 0, 0:HALF], ACT.Copy)
                        act.activation(cb[:, PAD + HALF:PBUF], dps[:, par, 1, 0:SEQ - HALF], ACT.Copy)
                        act.activation(tl[:, PAD:27].rearrange("p (b k) -> p b k", b=NB),
                                       dps[:, par, 1, SEQ - HALF:HALF].rearrange("p (b t) -> p b t", b=NB)[:, :, DT - PAD:DT], ACT.Copy)
                        act.activation(tl[:, 0:PAD], dps[:, par, 1, SEQ - HALF - PAD:SEQ - HALF], ACT.Copy)
                        act.activation(cb[:, PBUF:CW].rearrange("p (b k) -> p b k", b=NB)[:, :, PAD:SB1],
                                       dps[:, par, 1, SEQ - HALF:HALF].rearrange("p (b t) -> p b t", b=NB), ACT.Copy).then_inc(dense_free[par], 1)
                        if u >= 1:
                            th_of(act, G, u - 1)
                    th_of(act, G, 3)
                    for q in range(2):
                        par, k0 = slot(n0, 4 + q, i, N_GRP)
                        act.wait_ge(dense_full[par], k0 + 1)
                        act.activation(two(zg[:, q, :]), dps[:, par, :, 0:HALF], ACT.Tanh, scale=0.5).then_inc(zth_ready, 1)
                    for c in range(CH + 1):
                        act.wait_ge(le_full, G * 5 + c + 1)
                        m = P if c < CH else TS
                        ins = act.activation(l_exp[0:m, 0:GH * m], psL[0:m, 0:GH * m], ACT.Exp)
                        if c > 0:
                            ins = act.activation(e_exp[:, 0:GH * m], psE[:, 0:GH * m], ACT.Exp)
                        ins.then_inc(exp_ready, 1)
                    act.wait_ge(gt_ready, G * 3 + 1)
                    for q in range(2):
                        ins = act.activation(zg[:, q, :], yg[:, q, :], ACT.Square)
                    ins.then_inc(gsq_ready, 1)
                    act.wait_ge(gmean_ready, G + 1)
                    act.activation(rstd[:], rstd[:], ACT.Sqrt).then_inc(groot_ready, 1)
                    for q in range(2):
                        act.wait_ge(gt_ready, G * 3 + 2 + q)
                        yh = dyn(y_hi[:].rearrange("p k t -> p (k t)"), (i * 2 + q) * T, T)
                        act.activation(yh, zg[:, q, :], ACT.Copy).then_inc(ghi_ready, 1)
                    act.wait_ge(ssm_ready, G + 1)
                    act.dma_start(io["ssm_s"][bass.ds(G * P, P), :].rearrange("n (b q) -> n b q", b=NB), st_in[:]).then_inc(ssm_out, 16)
                    act.dma_start(io["ssm_p"][bass.ds(G * P, P), :], state[:]).then_inc(ssm_out, 16)
                link.leave(4)

            def th_of(act, G, u):
                act.wait_ge(conv_ready, G * 4 + u + 1)
                if u >= 2:
                    act.wait_ge(feat_ready, G * 4 + u - 1)
                act.activation(cth[:, u % 2, 0:CW - PAD], cout[:, u % 2, 0:CW - PAD], ACT.Tanh).then_inc(th_ready, 1)

            def tail_at(G, u):
                return G * 2 + u if u < 2 else G + (16 if u == 2 else 24)

            def dve_f(dve):
                link = chains["dve"]
                with dve.Fori(0, 4) as i:
                    link.enter(i, 58)
                    G = i + 4 * half
                    for u in range(4):
                        tix = tail_at(G, u)
                        cb, co = cbuf[:, u % 2, :], cout[:, u % 2, 0:CW - PAD]
                        h0 = FEA["hist"][0]
                        par, k0 = slot(n0, u, i, N_GRP)
                        dve.wait_ge(dense_free[par], k0 + 1)
                        link(dve.tensor_copy(cb[:, PBUF:CW].rearrange("p (b k) -> p b k", b=NB)[:, :, 0:PAD],
                                             dyn(fea[:], tix * (NB * PAD) + h0, NB * PAD).rearrange("p (b k) -> p b k", b=NB)))
                        wv = lambda j: dyn(fea[:], tix * SCONV + (CW_ + j), 1)
                        if u >= 2:
                            dve.wait_ge(th_ready, G * 4 + u - 1)
                        link(dve.tensor_scalar(co, cb[:, 0:CW - PAD], wv(0), dyn(fea[:], tix + CB_, 1), ALU.mult, ALU.add))
                        for j in range(1, SCONV):
                            ins = dve.scalar_tensor_tensor(co, cb[:, j:j + CW - PAD], wv(j), co, ALU.mult, ALU.add)
                            if j < SCONV - 1:
                                link(ins)
                        ins.then_inc(conv_ready, 1)
                        dve.wait_ge(conv_ready, G * 4 + u + 1)
                        if u >= 1:
                            silu_of(dve, link, G, u - 1)
                    silu_of(dve, link, G, 3)
                    for q in range(2):
                        dve.wait_ge(zth_ready, G * 2 + q + 1)
                        par, k0 = slot(n0, 4 + q, i, N_GRP)
                        dve.scalar_tensor_tensor(two(zg[:, q, :]), two(zg[:, q, :]), 1.0, dps[:, par, :, 0:HALF],
                                                 ALU.add, ALU.mult).then_inc(dense_free[par], 1)
                        dve.wait_ge(dense_free[par], k0 + 1)
                    for c in range(CH + 1):
                        last = c == CH
                        m = P if not last else TS
                        lo_, hi_ = c * P, c * P + m
                        up = c_("upto_p") if not last else c_("upto_s", TS)
                        hd = lambda t3: dyn(t3, G * GH, GH)
                        dve.tensor_tensor(rhs_a[0:m, :, 0:m], up.rearrange("p (o i) -> p o i", o=1).to_broadcast([m, GH, m]),
                                          hd(dt_tok[0:m, 1, c, :]).rearrange("p (h o) -> p h o", o=1).to_broadcast([m, GH, m]),
                                          ALU.mult).then_inc(rhs_ready, 1)
                        dve.wait_ge(a_full, G * 5 + c + 1)
                        bc = lambda ap: ap.rearrange("p (h o) -> p h o", o=1).to_broadcast([m, GH, 64])
                        x4 = lambda ap: ap.rearrange("p (h d) -> p h d", h=GH)
                        link(dve.tensor_tensor(x4(xdt[0:m, :]), x4(psA[0:m, 0:256]), bc(hd(dt_tok[0:m, 0, c, :])), ALU.mult))
                        link(dve.tensor_copy(btok[0:m, :], psA[0:m, 256:384]))
                        dve.tensor_tensor(cbm[0:m, 0:m], psA[0:m, 384:384 + m], up, ALU.mult).then_inc(a_free, 1)
                        dve.wait_ge(a_free, G * 5 + c + 1)
                        link(dve.tensor_tensor(x4(xdtd[0:m, :]), x4(xdt[0:m, :]), bc(hd(dec[0:m, c, :])), ALU.mult))
                        if last:
                            link(dve.tensor_tensor(bm[:], btok[0:TS, :].rearrange("p (o n) -> p o n", o=1).to_broadcast([TS, NB, P]),
                                                   c_("same_b", TS).rearrange("p (b o) -> p b o", o=1).to_broadcast([TS, NB, P]), ALU.mult))
                        dve.wait_ge(exp_ready, G * 5 + c + 1)
                        lv = l_exp[0:m, 0:GH * m].rearrange("p (h i) -> p h i", h=GH)
                        ev = e_exp[:, 0:GH * m].rearrange("p (h i) -> p h i", h=GH)
                        ins = dve.tensor_tensor(lv, lv, cbm[0:m, 0:m].rearrange("p (o i) -> p o i", o=1).to_broadcast([m, GH, m]), ALU.mult)
                        if c > 0:
                            ins = dve.tensor_tensor(ev, ev, cg[:, lo_:hi_].rearrange("p (o i) -> p o i", o=1).to_broadcast([P, GH, m]), ALU.mult)
                        ins.then_inc(m_ready, 1)
                        dve.wait_ge(m_ready, G * 5 + c + 1)
                        dve.wait_ge(y_full, G * 5 + c + 1)
                        for q in range(2):
                            dsk = dyn(fea[:], G * 2 + (FEA["dskip"][0] + q), 1)
                            link(dve.scalar_tensor_tensor(yg[:, q, lo_:hi_], xg[:, q, lo_:hi_], dsk, psY[:, q * m:(q + 1) * m], ALU.mult, ALU.add))
                        if not last:
                            if c > 0:
                                tv = dyn(tot[:], G * GH + c * HEADS, GH).rearrange("p (h o) -> p h o", o=1).to_broadcast([P, GH, 64])
                                link(dve.tensor_tensor(x4(state[:]), x4(state[:]), tv, ALU.mult))
                                ins = dve.tensor_tensor(state[:], state[:], psY[:, 256:512], ALU.add)
                            else:
                                dve.wait_ge(ssm_out, G * 32)
                                ins = dve.tensor_copy(state[:], psY[:, 256:512])
                            ins.then_inc(y_free, 1)
                            dve.wait_ge(y_free, G * 5 + c + 1)
                            continue
                        for hh in range(2):
                            r0, r1 = hh * 64, hh * 64 + 64
                            yv = yg[r0:r1, :, SEQ:T].rearrange("p q (b t) -> p b q t", b=NB)
                            ov = psY[r0:r1, 128:384].rearrange("p (b q h t) -> p b q h t", b=NB, q=2, h=2)[:, :, :, hh, :]
                            ins = dve.tensor_tensor(yv, yv, ov, ALU.add)
                            if hh == 0:
                                link(ins)
                        ins.then_inc(y_free, 1)
                        dve.wait_ge(y_free, G * 5 + c + 1)
                        tv = tot[:, CH * HEADS:].rearrange("p (b h) -> p b h", b=NB)
                        tg = tot[:, bass.ds(G * GH + CH * HEADS, (NB - 1) * HEADS + GH)]
                        for b in range(NB):
                            tb = dyn(tot[:], G * GH + (CH + b) * HEADS, GH).rearrange("p (h o) -> p h o", o=1).to_broadcast([P, GH, 64])
                            link(dve.tensor_tensor(x4(st_in[:, b, :]), x4(st_in[:, b, :]), tb, ALU.mult))
                        for r in range(4):
                            bank = psL if r % 2 == 0 else psE
                            dve.wait_ge(n_full, G * 4 + r + 1)
                            sv = st_in[:, 2 * r:2 * r + 2, :].rearrange("p b q -> p (b q)")
                            dve.tensor_tensor(sv, sv, bank, ALU.add).then_inc(n_free, 1)
                        dve.wait_ge(n_free, G * 4 + 4)
                        dve.sem_inc(ssm_ready, 1)
                    ins = dve.tensor_tensor(yg[:], yg[:], zg[:], ALU.mult)
                    ins.then_inc(gt_ready, 1)
                    dve.wait_ge(gt_ready, G * 3 + 1)
                    dve.wait_ge(gsum_full, G + 1)
                    link(dve.tensor_scalar(rstd[:, 0:HALF], psL[:, 0:HALF], 1.0 / 1024, EPS, ALU.mult, ALU.add))
                    dve.tensor_scalar(rstd[:, HALF:T], psE[:, 0:HALF], 1.0 / 1024, EPS, ALU.mult, ALU.add).then_inc(gmean_ready, 1)
                    dve.wait_ge(groot_ready, G + 1)
                    link(dve.reciprocal(rstd[:], rstd[:]))
                    for q in range(2):
                        wv = dyn(fea[:], G * 2 + (FEA["ssdn"][0] + q), 1)
                        dve.scalar_tensor_tensor(zg[:, q, :], yg[:, q, :], wv, rstd[:], ALU.mult, ALU.mult).then_inc(gt_ready, 1)
                        dve.wait_ge(ghi_ready, G * 2 + q + 1)
                        off = (i * 2 + q) * T
                        link(dve.tensor_tensor(dyn(y_lo[:].rearrange("p k t -> p (k t)"), off, T), zg[:, q, :],
                                               dyn(y_hi[:].rearrange("p k t -> p (k t)"), off, T).bitcast(F32), ALU.subtract))
                link.leave(4)

            def silu_of(dve, link, G, u):
                dst = (xg[:, 0, :], xg[:, 1, :], bg[:], cg[:])[u]
                co, th = cout[:, u % 2, :], cth[:, u % 2, :]
                sample = lambda a: a[:, PBUF:CW].rearrange("p (b k) -> p b k", b=NB)[:, :, 0:DT]
                dve.wait_ge(th_ready, G * 4 + u + 1)
                dve.scalar_tensor_tensor(dst[:, 0:SEQ], th[:, 0:SEQ], 1.0, co[:, 0:SEQ], ALU.add, ALU.mult)
                dve.scalar_tensor_tensor(dst[:, SEQ:T].rearrange("p (b t) -> p b t", b=NB), sample(th), 1.0, sample(co),
                                         ALU.add, ALU.mult).then_inc(feat_ready, 1)
                dve.wait_ge(feat_ready, G * 4 + u + 1)

            pe_prog.append(pe_f); act_prog.append(act_f); dve_prog.append(dve_f)

        dve_prog.append(lambda dve: chains["dve"](dve.memset(cbuf[:, :, 0:PAD], 0.0)))
        edge("edge_zero")
        ssd_half(0)
        edge("edge_ssd0")

        def evac_stage(n0, count, hi, lo, evac, nb=2):
            def pe_f(pe):
                with pe.Fori(0, count // nb) as i:
                    for u in range(nb):
                        pe_dense(pe, slot(n0, u, i, nb), hi(u), lo(u))
            pe_prog.append(pe_f)

        n0c = take(8)
        evac_stage(n0c, 8, lambda u: y_hi, lambda u: y_lo, None)

        def act_c(act):
            with act.Fori(0, 4) as i:
                for u in range(2):
                    par, k0 = slot(n0c, u, i, 2)
                    act.wait_ge(dense_full[par], k0 + 1)
                    act.activation(two(merged[:].rearrange("p k t -> p (k t)")[:, bass.ds((i * 2 + u) * T, T)]),
                                   dps[:, par, :, 0:HALF], ACT.Copy).then_inc(dense_free[par], 1)
        act_prog.append(act_c)
        edge("edge_out0")
        ssd_half(1)
        act_prog.append(lambda act: act.wait_ge(ssm_out, GROUPS * 32))
        edge("edge_ssd1")

        merged_done, merges = sem("merged_done"), [0]

        def merge_stage(name, first):
            st = ExitStack()
            gth = stage_sb(st, f"{name}_gth", [P, 2, T])
            tmp = stage_sb(st, f"{name}_tmp", [P, 2, T])
            st.close()
            n0 = take(2 * KT)
            before = merges[0] * KT
            merges[0] += 1

            def pe_f(pe):
                with pe.Fori(0, KT // 2) as i:
                    for u in range(4):
                        gate = u % 2 == 0
                        pe_dense(pe, slot(n0, u, i, 4), xn_hi if gate else y_hi, xn_lo if gate else y_lo)

            def act_f(act):
                with act.Fori(0, KT // 2) as i:
                    for u in (0, 2):
                        par, k0 = slot(n0, u, i, 4)
                        act.wait_ge(merged_done, i * 2 + before)
                        act.wait_ge(dense_full[par], k0 + 1)
                        act.activation(two(gth[:, u // 2, :]), dps[:, par, :, 0:HALF], ACT.Tanh, scale=0.5).then_inc(dense_free[par], 1)

            def dve_f(dve):
                link = chains["dve"]
                with dve.Fori(0, KT // 2) as i:
                    link.enter(i, 2)
                    for j in range(2):
                        gp, gk = slot(n0, 2 * j, i, 4)
                        par, k0 = slot(n0, 2 * j + 1, i, 4)
                        mv = merged[:].rearrange("p k t -> p (k t)")[:, bass.ds((i * 2 + j) * T, T)]
                        dve.wait_ge(dense_free[gp], gk + 1)
                        dve.wait_ge(dense_full[par], k0 + 1)
                        ps = dps[:, par, :, 0:HALF]
                        if first:
                            dve.tensor_tensor(two(tmp[:, j, :]), two(mv), ps, ALU.add).then_inc(dense_free[par], 1)
                            dve.wait_ge(dense_free[par], k0 + 1)
                            dve.scalar_tensor_tensor(mv, gth[:, j, :], 1.0, tmp[:, j, :], ALU.add, ALU.mult).then_inc(merged_done, 1)
                            link(dve.memset(pad1[:], 0.0))
                        else:
                            dve.scalar_tensor_tensor(two(tmp[:, j, :]), two(gth[:, j, :]), 1.0, ps, ALU.add, ALU.mult).then_inc(dense_free[par], 1)
                            dve.wait_ge(dense_free[par], k0 + 1)
                            link(dve.tensor_tensor(mv, mv, tmp[:, j, :], ALU.add))
                            dve.sem_inc(merged_done, 1)
                link.leave(KT // 2)
            pe_prog.append(pe_f); act_prog.append(act_f); dve_prog.append(dve_f)

        merge_stage("m0", True)
        edge("edge_m0")

        att = ExitStack()
        as_ = lambda n, s, d=F32: stage_sb(att, n, s, d)
        ks = as_("ks", [P, 2, T])
        vs = as_("vs", [P, 2, T])
        v_new = as_("v_new", [DT, NB, 256])
        qbd = as_("qbd", [P, 2, NB, P])
        ys = as_("ys", [P, 2, 4, TS])
        pro = ExitStack()
        ps_ = lambda n, s, d=F32: stage_sb(pro, n, s, d)
        ksw = ps_("ksw", [P, 2, T])
        v_tok = ps_("v_tok", [P, CH, 256])
        raw, ropet = ps_("raw", [P, T]), ps_("ropet", [P, T])
        qk = ps_("qk", [P, T])
        kcur, vcur = ps_("kcur", [P, SEQ]), ps_("vcur", [P, CH, 64])
        prob = ps_("prob", [P, 2, SEQ])
        prob_t = ps_("prob_t", [P, CH, SEQ])
        nmax, psum_, prec = ps_("nmax", [P, 2]), ps_("psum_", [P, 2]), ps_("prec", [P, 2])
        pro.close()

        raw_ready, rot_full, rope_done = sem("raw_ready"), sem("rot_full"), sem("rope_done")
        sw_full, sw_copied = sem("sw_full"), sem("sw_copied")
        vt_full, vt_copied = sem("vt_full"), sem("vt_copied")
        kv_out = sem("kv_out")
        n_kv = take(4)

        def rope(dve, link, dst, n_done, n_rot):
            dve.wait_ge(rot_full, n_rot)
            dve.tensor_tensor(two(ropet[:]), two(c_("sin")), psLE[:, :, 0:HALF], ALU.mult)
            link(dve.tensor_tensor(dst, raw[:], c_("cos"), ALU.mult))
            dve.tensor_tensor(dst, dst, ropet[:], ALU.add).then_inc(rope_done, 1)
            dve.wait_ge(rope_done, n_done)

        def pe_rot(pe, src, mat, done):
            for b in range(2):
                mm = pe.matmul(psLE[:, b, 0:HALF], mat, src[:, b * HALF:(b + 1) * HALF], start=True, stop=True)
            mm.then_inc(done, 1)

        def pe_kv(pe):
            for u in range(2):
                pe_dense(pe, slot(n_kv, u), xn_hi, xn_lo)
            for j in range(2):
                pe.wait_ge(raw_ready, j + 1)
                pe_rot(pe, raw, c_("rot"), rot_full)
                pe.wait_ge(rope_done, j + 1)
            for u in range(2, 4):
                pe_dense(pe, slot(n_kv, u), xn_hi, xn_lo)
            for j in range(2):
                if j:
                    pe.wait_ge(sw_copied, 1)
                pe_rot(pe, ks[:, j, :], c_("swap"), sw_full)
            par, k0 = slot(n_kv, 3)
            pe.wait_ge(dense_free[par], k0 + 1)
            for c in range(CH):
                bank = psA if c < 2 else psY
                for j in range(2):
                    mm = pe.transpose(bank[:, (c % 2) * 256 + j * P:(c % 2) * 256 + (j + 1) * P], vs[:, j, c * P:(c + 1) * P], ident)
            mm.then_inc(vt_full, 1)
            for r in range(4):
                if r == 0:
                    pe.wait_ge(vt_copied, 1)
                if r == 2:
                    pe.wait_ge(vt_copied, 3)
                bank = psA if r % 2 == 0 else psY
                for b in (2 * r, 2 * r + 1):
                    for j in range(2):
                        o = (b % 2) * 256 + j * P
                        mm = pe.transpose(bank[0:DT, o:o + P], vs[:, j, SEQ + b * DT:SEQ + (b + 1) * DT], ident)
                mm.then_inc(vt_full, 1)

        def act_kv(act):
            for u in range(4):
                par, k0 = slot(n_kv, u)
                act.wait_ge(dense_full[par], k0 + 1)
                if u == 0:
                    act.activation(two(raw[:]), dps[:, par, :, 0:HALF], ACT.Copy).then_inc(dense_free[par], 1)
                    act.wait_ge(dense_free[par], k0 + 1)
                    act.sem_inc(raw_ready, 1)
                elif u == 1:
                    act.wait_ge(rope_done, 1)
                    act.activation(two(raw[:]), dps[:, par, :, 0:HALF], ACT.Copy).then_inc(dense_free[par], 1)
                    act.wait_ge(dense_free[par], k0 + 1)
                    act.sem_inc(raw_ready, 1)
                else:
                    act.activation(two(vs[:, u - 2, :]), dps[:, par, :, 0:HALF], ACT.Copy).then_inc(dense_free[par], 1)
            act.wait_ge(dense_free[par], k0 + 1)
            act.dma_start(io["kv_t"][:, 2:4, :], vs[:]).then_inc(kv_out, 16)
            for j in range(2):
                act.wait_ge(sw_full, j + 1)
                act.activation(two(ksw[:, j, :]), psLE[:, :, 0:HALF], ACT.Copy).then_inc(sw_copied, 1)
            act.wait_ge(rope_done, 2)
            act.dma_start(io["kv_t"][:, 0:2, :], ks[:]).then_inc(kv_out, 16)

        def dve_kv(dve):
            link = chains["dve"]
            dve.memset(qbd[:], 0.0)
            for j in range(2):
                dve.wait_ge(raw_ready, j + 1)
                rope(dve, link, ks[:, j, :], j + 1, j + 1)
            dve.wait_ge(vt_full, 1)
            dve.tensor_copy(v_tok[:, 0:2, :], psA[:].rearrange("p (c f) -> p c f", c=2))
            dve.tensor_copy(v_tok[:, 2:4, :], psY[:].rearrange("p (c f) -> p c f", c=2)).then_inc(vt_copied, 1)
            for r in range(4):
                dve.wait_ge(vt_full, r + 2)
                bank = psA if r % 2 == 0 else psY
                dve.tensor_copy(v_new[:, 2 * r:2 * r + 2, :], bank[0:DT, :].rearrange("p (b f) -> p b f", b=2)).then_inc(vt_copied, 1)
        pe_prog.append(pe_kv); act_prog.append(act_kv); dve_prog.append(dve_kv)
        edge("edge_kv")

        n_q = take(KT)
        s_full, s_max, s_exp, p_norm = sem("s_full"), sem("s_max"), sem("s_exp"), sem("p_norm")
        t_full, t_copied, pv_full = sem("t_full"), sem("t_copied"), sem("pv_full")
        yhi_ready, ylo_ready, qsw_full, qbd_done, kv_cur = sem("yhi_ready"), sem("ylo_ready"), sem("qsw_full"), sem("qbd_done"), sem("kv_cur")

        def pe_q(pe):
            with pe.Fori(0, 2) as j:
                for tt in range(4):
                    t = j * 4 + tt
                    pe_dense(pe, slot(n_q, tt, j, 4), xn_hi, xn_lo)
                    pe.wait_ge(raw_ready, t + 3)
                    pe_rot(pe, raw, c_("rot"), rot_full)
                    pe.wait_ge(rope_done, t + 3)
                    pe.matmul(psA[:, 0:TS], c_("swap"), qk[:, SEQ:T], start=True, stop=True).then_inc(qsw_full, 1)
                    pe.wait_ge(qbd_done, t + 1)
                    if tt % 2 == 0:
                        pe.wait_ge(kv_cur, j * 2 + (tt // 2 + 1))

                    def scores(r):
                        hh, i = r // 4, r % 4
                        s = t * 8 + r
                        pe.wait_ge(s_exp, s + 1)
                        rows = slice(hh * 64, hh * 64 + 64)
                        o = psLE[:, r % 2, 0:(i + 1) * P]
                        pe.matmul(o, qk[rows, i * P:(i + 1) * P], kcur[rows, 0:(i + 1) * P], start=True, stop=False)
                        pe.matmul(psLE[:, r % 2, i * P:(i + 1) * P], ident, c_("causal"), start=False, stop=True).then_inc(s_full, 1)
                    scores(0)
                    for r in range(8):
                        hh, i = r // 4, r % 4
                        s = t * 8 + r
                        if r < 7:
                            scores(r + 1)
                        pe.wait_ge(t_copied, s)
                        pe.wait_ge(p_norm, s + 1)
                        for kt in range(i + 1):
                            mm = pe.transpose(psA[:, kt * P:(kt + 1) * P], prob[:, r % 2, kt * P:(kt + 1) * P], ident)
                        mm.then_inc(t_full, 1)
                        if i == 3:
                            if hh == 0:
                                pe.wait_ge(ylo_ready, t)
                            pe.wait_ge(t_copied, s + 1)
                            for kt in range(CH):
                                mm = pe.matmul(psY[hh * 64:hh * 64 + 64, kt * P:SEQ], vcur[:, kt, :], prob_t[:, kt, kt * P:SEQ],
                                               start=(kt == 0), stop=(kt == CH - 1))
                            mm.then_inc(pv_full, 1)

        def act_q(act):
            act.sem_inc(s_exp, 2)
            with act.Fori(0, 2) as j:
                for tt in range(4):
                    t = j * 4 + tt
                    par, k0 = slot(n_q, tt, j, 4)
                    act.wait_ge(dense_full[par], k0 + 1)
                    act.wait_ge(rope_done, t + 2)
                    act.activation(two(raw[:]), dps[:, par, :, 0:HALF], ACT.Copy, scale=0.125).then_inc(dense_free[par], 1)
                    act.wait_ge(dense_free[par], k0 + 1)
                    act.sem_inc(raw_ready, 1)
                    if tt % 2 == 0:
                        gpar = tt // 2
                        act.wait_ge(pv_full, t * 2)
                        flat = lambda a: a[:].rearrange("p k t -> p (k t)")
                        for hf in range(2):
                            src = ks if hf == gpar else ksw
                            rows = slice(hf * 64, hf * 64 + 64)
                            act.activation(kcur[rows, :], flat(src)[rows, bass.ds(j * T, SEQ)], ACT.Copy)
                        act.activation(vcur[:], v_tok[:, :, bass.ds(j * P + gpar * 64, 64)], ACT.Copy).then_inc(kv_cur, 1)

                    def exp_(r):
                        i, s = r % 4, t * 8 + r
                        w = (i + 1) * P
                        act.wait_ge(s_max, s + 1)
                        act.activation(prob[:, r % 2, 0:w], psLE[:, r % 2, 0:w], ACT.Exp, bias=nmax[:, r % 2:r % 2 + 1],
                                       accum_out=psum_[:, r % 2:r % 2 + 1]).then_inc(s_exp, 1)
                    exp_(0)
                    for r in range(8):
                        hh, i = r // 4, r % 4
                        s = t * 8 + r
                        if r < 7:
                            exp_(r + 1)
                        act.wait_ge(t_full, s + 1)
                        if i == 0:
                            act.wait_ge(pv_full, t * 2 + hh)
                        act.activation(prob_t[:, 0:i + 1, i * P:(i + 1) * P], psA[:, 0:(i + 1) * P].rearrange("p (k q) -> p k q", q=P),
                                       ACT.Copy).then_inc(t_copied, 1)
                    act.wait_ge(pv_full, t * 2 + 2)
                    act.activation(y_hi[:].rearrange("p k t -> p (k t)")[:, bass.ds(t * T, SEQ)], psY[:], ACT.Copy).then_inc(yhi_ready, 1)

        def dve_q(dve):
            link = chains["dve"]
            with dve.Fori(0, 2) as j:
                link.enter(j, PER_Q)
                for tt in range(4):
                    t = j * 4 + tt
                    gpar, r0 = tt // 2, (tt % 2) * 2
                    rope(dve, link, qk[:], t + 3, t + 3)
                    dve.wait_ge(qsw_full, t + 1)
                    rows = slice(gpar * 64, gpar * 64 + 64)
                    for hf in range(2):
                        src = qk[rows, SEQ:T] if hf == gpar else psA[rows, 0:TS]
                        col = gpar * 32 + (r0 + hf) * DT
                        ap = qbd[rows, bass.ds(j, 1), :, bass.ds(j * 64 + col, DT)].rearrange("p o b c -> p (o b) c")
                        ins = dve.tensor_copy(ap, src.rearrange("p (b t) -> p b t", b=NB))
                    ins.then_inc(qbd_done, 1)

                    def max_(r):
                        i, s = r % 4, t * 8 + r
                        dve.wait_ge(s_full, s + 1)
                        dve.wait_ge(s_exp, s + 1)
                        dve.tensor_reduce(nmax[:, r % 2:r % 2 + 1], psLE[:, r % 2, 0:(i + 1) * P], AX, ALU.max, negate=True).then_inc(s_max, 1)
                    max_(0)
                    for r in range(8):
                        hh, i = r // 4, r % 4
                        s = t * 8 + r
                        w = (i + 1) * P
                        if r < 7:
                            max_(r + 1)
                        dve.wait_ge(s_exp, s + 3)
                        link(dve.reciprocal(prec[:, r % 2:r % 2 + 1], psum_[:, r % 2:r % 2 + 1]))
                        dve.tensor_scalar(prob[:, r % 2, 0:w], prob[:, r % 2, 0:w], prec[:, r % 2:r % 2 + 1], None, ALU.mult).then_inc(p_norm, 1)
                    dve.wait_ge(yhi_ready, t + 1)
                    yl, yh = (a[:].rearrange("p k t -> p (k t)")[:, bass.ds(t * T, SEQ)] for a in (y_lo, y_hi))
                    dve.tensor_tensor(yl, psY[:], yh.bitcast(F32), ALU.subtract).then_inc(ylo_ready, 1)
                    dve.wait_ge(ylo_ready, t + 1)
            link.leave(2)

        PER_Q = 36
        pe_prog.append(pe_q); act_prog.append(act_q); dve_prog.append(dve_q)
        edge("edge_q")

        n_pages_at = nstream[0]
        sam = ExitStack()
        sa = lambda n, s, d=F32: stage_sb(sam, n, s, d)
        ptab = sa("ptab", [1, NB * NPG], mybir.dt.int32)
        kpg = sa("kpg", [P, 2, 4, 256])
        vpg = sa("vpg", [P, 2, 4, 256])
        sc = sa("sc", [P, PAST + DT])
        pt_s = sa("pt_s", [P, NPG, P])
        pt_own = sa("pt_own", [DT, P])
        qb = sa("qb", [P, 2, P])
        gs, bmx, cmp1, cmp2 = sa("gs", [P, 8]), sa("bmx", [P, 9]), sa("cmp1", [P, 8, 8]), sa("cmp2", [P, 8, 8])
        rank, bias, nm, ssum = sa("rank", [P, 8]), sa("bias", [P, 9]), sa("nm", [P, 1]), sa("ssum", [P, 9])
        yf = sa("yf", [P, KT, TS])
        sam.close(); att.close()
        k_landed, v_landed = [sem("k_landed0"), sem("k_landed1")], [sem("v_landed0"), sem("v_landed1")]
        pt_in, b_qb, b_s, b_sc, b_own, b_bias, b_exp, b_norm = (sem(f"b_{k}") for k in ("pt", "qb", "s", "sc", "own", "bias", "exp", "norm"))
        b_t, b_tc, b_pv, b_ys, b_vused = (sem(f"b_{k}") for k in ("t", "tc", "pv", "ys", "vused"))
        sw_s, sw_y = sem("sw_s"), sem("sw_y")
        sam_start = sem("sam_start")

        def sp_load_pages(sp):
            sp.wait_ge(sam_start, 1)
            sp.dma_start(ptab[:], io["page_table"]).then_inc(pt_in, 16)
            sp.wait_ge(pt_in, 16)
            n_phys = io["k_pages"].shape[0]
            with sp.Fori(0, NB) as b:
                for kind in range(2):
                    for c in range(4):
                        pages = [sp.value_load(ptab[0:1, bass.ds(b * NPG + (c * 4 + k), 1)], min_val=0, max_val=n_phys - 1)
                                 for k in range(4)]
                        if kind == 0:
                            buf, src, landed = kpg, io["k_pages"], k_landed
                            sp.wait_ge(b_s, b * 5 + (c - 1)) if c >= 2 else sp.wait_ge(b_s, b * 5)
                        else:
                            buf, src, landed = vpg, io["v_pages"], v_landed
                            sp.wait_ge(b_vused, b * 4 + (c - 1)) if c >= 2 else sp.wait_ge(b_vused, b * 4)
                        for k in range(4):
                            sp.dma_start(buf[:, c % 2, k, :], src[bass.ds(pages[k], 1), :, :].rearrange("o p f -> (o p) f")).then_inc(landed[c % 2], 16)

        sp_pages = [sp_load_pages ]

        def pe_s(pe):
            with pe.Fori(0, NB) as b:
                pe.wait_ge(b_qb, b + 1)
                for c in range(4):
                    pe.wait_ge(k_landed[c % 2], b * 128 + (c // 2 + 1) * 64)
                    if c < 2:
                        pe.wait_ge(b_sc, b * 4)
                    else:
                        pe.wait_ge(b_sc, b * 4 + (c - 1))
                    for m in range(2):
                        mm = pe.matmul(psLE[:, c % 2, :].rearrange("p (k t) -> p k t", k=4), qb[:, m, :],
                                       kpg[:, c % 2, :, m * P:(m + 1) * P], start=(m == 0), stop=(m == 1))
                    mm.then_inc(b_s, 1)
                pe.wait_ge(b_own, b)
                for m in range(2):
                    mm = pe.matmul(psY[:, 0:DT], qb[:, m, :], ks[:].rearrange("p k t -> p (k t)")[:, bass.ds(b * DT + (m * T + SEQ), DT)],
                                   start=(m == 0), stop=(m == 1))
                mm.then_inc(b_s, 1)
                pe.wait_ge(b_norm, b + 1)
                for c in range(4):
                    if c >= 2:
                        pe.wait_ge(b_tc, b * 5 + (c - 1))
                    else:
                        pe.wait_ge(b_tc, b * 5)
                    bank = psA if c % 2 == 0 else psY
                    for k in range(4):
                        mm = pe.transpose(bank[:, k * P:(k + 1) * P], sc[:, (c * 4 + k) * P:(c * 4 + k + 1) * P], ident)
                    mm.then_inc(b_t, 1)
                pe.wait_ge(b_tc, b * 5 + 3)
                pe.transpose(psA[0:DT, 0:P], sc[:, PAST:PAST + DT], ident).then_inc(b_t, 1)
                pe.wait_ge(b_ys, b * 2)
                for c in range(4):
                    pe.wait_ge(v_landed[c % 2], b * 128 + (c // 2 + 1) * 64)
                    pe.wait_ge(b_tc, b * 5 + (c + 1))
                    for k in range(4):
                        for m in range(2):
                            mm = pe.matmul(dps[:, m, 0, 0:64], vpg[:, c % 2, k, m * P:(m + 1) * P], pt_s[:, c * 4 + k, m * 64:m * 64 + 64],
                                           start=(c == 0 and k == 0), stop=False)
                    mm.then_inc(b_vused, 1)
                pe.wait_ge(b_tc, b * 5 + 5)
                for m in range(2):
                    mm = pe.matmul(dps[:, m, 0, 0:64], vown[:, m * P:(m + 1) * P], pt_own[:, m * 64:m * 64 + 64], start=False, stop=True)
                mm.then_inc(b_pv, 1)
            pe.wait_ge(b_ys, 2 * NB)
            pe.matmul(psL, c_("swap"), ys[:].rearrange("p m r t -> p (m r t)"), start=True, stop=True).then_inc(sw_s, 1)

        def act_s(act):
            act.sem_inc(sam_start, 1)
            with act.Fori(0, NB) as b:
                for c in range(4):
                    act.wait_ge(b_s, b * 5 + (c + 1))
                    if c == 0:
                        act.wait_ge(b_t, b * 5)
                    act.activation(sc[:, c * 512:(c + 1) * 512], psLE[:, c % 2, :], ACT.Copy).then_inc(b_sc, 1)
                act.wait_ge(b_bias, b + 1)
                for n in range(8):
                    act.activation(sc[:, n * 256:(n + 1) * 256], sc[:, n * 256:(n + 1) * 256], ACT.Exp, bias=bias[:, n:n + 1],
                                   accum_out=ssum[:, n:n + 1])
                act.activation(sc[:, PAST:], sc[:, PAST:], ACT.Exp, bias=nm[:, 0:1], accum_out=ssum[:, 8:9]).then_inc(b_exp, 1)
                for c in range(4):
                    act.wait_ge(b_t, b * 5 + (c + 1))
                    bank = psA if c % 2 == 0 else psY
                    if c == 0:
                        act.wait_ge(b_pv, b)
                    act.activation(pt_s[:, 4 * c:4 * c + 4, :], bank[:].rearrange("p (k r) -> p k r", k=4), ACT.Copy).then_inc(b_tc, 1)
                act.wait_ge(b_t, b * 5 + 5)
                act.activation(pt_own[:], psA[0:DT, 0:P], ACT.Copy)
                act.activation(vown[:], v_new[:].rearrange("p b f -> p (b f)")[:, bass.ds(b * 256, 256)], ACT.Copy).then_inc(b_tc, 1)
            act.wait_ge(sw_y, 1)
            act.activation(y_hi[:, :, SEQ:T], yf[:], ACT.Copy).then_inc(yhi_ready, 1)
            act.wait_ge(kv_out, 32)

        def dve_s(dve):
            link = chains["dve"]
            with dve.Fori(0, NB) as b:
                link.enter(b, PER_S)
                dve.wait_ge(b_s, b * 5)
                dve.tensor_copy(qb[:], qbd[:].rearrange("p m b c -> p m (b c)")[:, :, bass.ds(b * P, P)]).then_inc(b_qb, 1)
                for c in range(4):
                    dve.wait_ge(b_sc, b * 4 + (c + 1))
                    blk = sc[:, c * 512:(c + 1) * 512].rearrange("p (n k) -> p n k", n=2)
                    link(dve.tensor_reduce(gs[:, 2 * c:2 * c + 2], blk, AX, ALU.add))
                    link(dve.tensor_reduce(bmx[:, 2 * c:2 * c + 2], blk, AX, ALU.max))
                dve.wait_ge(b_s, b * 5 + 5)
                dve.tensor_tensor(sc[:, PAST:], psY[:, 0:DT], c_("own"), ALU.add).then_inc(b_own, 1)
                dve.wait_ge(b_own, b + 1)
                link(dve.tensor_reduce(bmx[:, 8:9], sc[:, PAST:], AX, ALU.max))
                gm = gs[:].rearrange("p (o m) -> p o m", o=1).to_broadcast([P, 8, 8])
                gn = gs[:].rearrange("p (n o) -> p n o", o=1).to_broadcast([P, 8, 8])
                link(dve.tensor_tensor(cmp1[:], gm, gn, ALU.is_gt))
                link(dve.tensor_tensor(cmp2[:], gm, gn, ALU.is_equal))
                link(dve.tensor_tensor(cmp2[:], cmp2[:], c_("blk_lt").rearrange("p (n m) -> p n m", n=8), ALU.mult))
                link(dve.tensor_tensor(cmp1[:], cmp1[:], cmp2[:], ALU.add))
                link(dve.tensor_reduce(rank[:], cmp1[:], AX, ALU.add))
                link(dve.tensor_scalar(bias[:, 0:8], rank[:], 3.0, NEG, ALU.is_ge, ALU.mult))
                link(dve.tensor_tensor(bmx[:, 0:8], bmx[:, 0:8], bias[:, 0:8], ALU.add))
                link(dve.tensor_reduce(nm[:], bmx[:], AX, ALU.max, negate=True))
                dve.tensor_scalar(bias[:, 0:8], bias[:, 0:8], nm[:, 0:1], None, ALU.add).then_inc(b_bias, 1)
                dve.wait_ge(b_exp, b + 1)
                link(dve.tensor_reduce(rank[:, 0:1], ssum[:], AX, ALU.add))
                link(dve.reciprocal(rank[:, 1:2], rank[:, 0:1]))
                dve.tensor_scalar(sc[:], sc[:], rank[:, 1:2], None, ALU.mult).then_inc(b_norm, 1)
                dve.wait_ge(b_pv, b + 1)
                for p in range(2):
                    rows = slice(p * 64, p * 64 + 64)
                    dve.tensor_copy(ys[rows, :, :, bass.ds(b * DT, DT)],
                                    dps[rows, :, 0, p * 32:p * 32 + 32].rearrange("p m (r t) -> p m r t", r=4)).then_inc(b_ys, 1)
            link.leave(NB)
            dve.wait_ge(b_ys, 2 * NB)
            dve.wait_ge(sw_s, 1)
            swp = psL.rearrange("p (m r t) -> p m r t", m=2, r=4)
            for rp in range(2):
                rows = slice(rp * 64, rp * 64 + 64)
                for p in range(2):
                    src = ys[:] if p == rp else swp
                    dst = yf[rows].rearrange("p (m q r) t -> p m q r t", m=2, q=2)[:, :, p, :, :]
                    ins = dve.tensor_copy(dst, src[rows].rearrange("p m (r s) t -> p m r s t", s=2)[:, :, :, rp, :])
            ins.then_inc(sw_y, 1)
            dve.wait_ge(sw_y, 1)
            dve.wait_ge(yhi_ready, KT + 1)
            link(dve.tensor_tensor(y_lo[:, :, SEQ:T], yf[:], y_hi[:, :, SEQ:T].bitcast(F32), ALU.subtract))

        PER_S = 19
        pe_prog.append(pe_s); act_prog.append(act_s); dve_prog.append(dve_s)
        edge("edge_s")
        merge_stage("m1", False)
        edge("edge_m1")

        mm_ = ExitStack()
        ms = lambda n, s, d=F32: stage_sb(mm_, n, s, d)
        km = ms("km", [P, KT, MEM])
        vm = ms("vm", [P, 2, D])
        mk = ExitStack()
        memx = stage_sb(mk, "memx", [P, KT, MEM])
        vmt = stage_sb(mk, "vmt", [P, KT, MEM])
        mem_in, memkv_out = sem("mem_in"), sem("memkv_out")
        act_prog.append(lambda act: act.dma_start(memx[:], io["mem_t"]).then_inc(mem_in, 16))
        norm_stage("normm", memx, "memn", y_hi, y_lo, width=MEM, ready=((mem_in, 16),))
        mk.close()
        edge("edge_normm")
        n_mem = take(2 * KT)
        vmt_full, vmt_copied = sem("vmt_full"), sem("vmt_copied")

        def pe_mem(pe):
            with pe.Fori(0, KT) as i:
                for u in range(2):
                    pe_dense(pe, slot(n_mem, u, i, 2), y_hi, y_lo, width=MEM)
            for par in range(2):
                pe.wait_ge(dense_free[par], (n_mem + 2 * KT) // 2 if (n_mem % 2 == 0) else (n_mem + 2 * KT + 1 - par) // 2)
            for kt in range(2):
                for j in range(KT):
                    r = kt * 2 + j // 4
                    if j % 4 == 0 and r >= 2:
                        pe.wait_ge(vmt_copied, r - 1)
                    bank = psA if r % 2 == 0 else psY
                    mm = pe.transpose(bank[:, (j % 4) * P:(j % 4 + 1) * P], vmt[:, j, kt * P:(kt + 1) * P], ident)
                    if j % 4 == 3:
                        mm.then_inc(vmt_full, 1)

        def act_mem(act):
            for dst in (km, vmt):
                base = n_mem if dst is km else n_mem + KT
                with act.Fori(0, KT // 2) as i:
                    for u in range(2):
                        par, k0 = slot(base, u, i, 2)
                        act.wait_ge(dense_full[par], k0 + 1)
                        act.activation(dst[:].rearrange("p k t -> p (k t)")[:, bass.ds((i * 2 + u) * MEM, MEM)],
                                       dps[:, par, 0, 0:MEM], ACT.Copy).then_inc(dense_free[par], 1)
            for par in range(2):
                act.wait_ge(dense_free[par], (n_mem + 2 * KT + 1 - par) // 2)
            act.dma_start(io["memkv_t"][:, 0:KT, :], km[:]).then_inc(memkv_out, 16)
            act.dma_start(io["memkv_t"][:, KT:2 * KT, :], vmt[:]).then_inc(memkv_out, 16)
            act.wait_ge(memkv_out, 32)

        def dve_mem(dve):
            for r in range(4):
                dve.wait_ge(vmt_full, r + 1)
                bank = psA if r % 2 == 0 else psY
                dve.tensor_copy(vm[:, r // 2, (r % 2) * 512:(r % 2) * 512 + 512], bank[:]).then_inc(vmt_copied, 1)
        pe_prog.append(pe_mem); act_prog.append(act_mem); dve_prog.append(dve_mem)
        edge("edge_mem")

        mh = ExitStack()
        ms2 = lambda n, s, d=F32: stage_sb(mh, n, s, d)
        kc = ms2("kc", [P, NB, 2, MEM])
        vc = ms2("vc", [P, NB, 2, MEM])
        qh = ms2("qh", [P, 2, T])
        vh = ms2("vh", [P, 2, MEM])
        mp = ms2("mp", [P, 2, MEM])
        mpt = ms2("mpt", [P, 2, T])
        mst = ms2("mst", [P, 2, TS])
        mfix = ms2("mfix", [P, 2, TS])
        mnm, msum, mrc = ms2("mnm", [P, 2]), ms2("msum", [P, 2]), ms2("mrc", [P, 2])
        mh.close(); mm_.close()
        n_qm = take(KT)
        h_q, h_s, h_max, h_exp, h_norm, h_a, h_ac = (sem(f"h_{k}") for k in ("q", "s", "max", "exp", "norm", "a", "ac"))
        h_pv, h_hi, h_lo, kc_in, vc_in = (sem(f"h_{k}") for k in ("pv", "hi", "lo", "kc", "vc"))
        NQ = CH + 1

        def pe_h(pe):
            with pe.Fori(0, 4) as h:
                for u in range(2):
                    pe_dense(pe, slot(n_qm, u, h, 2), xn_hi, xn_lo)
                pe.wait_ge(h_q, h + 1)
                pe.wait_ge(kc_in, h * 16 + 16)
                pe.wait_ge(h_ac, h * 7)
                for kk in range(2):
                    for b in range(NB):
                        for kt in range(2):
                            mm = pe.matmul(psA[:, kk * TS + b * DT:kk * TS + (b + 1) * DT], kc[:, b, kt, kk * P:(kk + 1) * P],
                                           qh[:, kt, SEQ + b * DT:SEQ + (b + 1) * DT], start=(kt == 0), stop=(kt == 1))
                mm.then_inc(h_a, 1)
                for i in range(NQ):
                    m = P if i < CH else TS
                    bank = psLE[:, i % 2, :]
                    if i == 0:
                        pe.wait_ge(h_exp, h * 5)
                    elif i >= 2:
                        pe.wait_ge(h_exp, h * 5 + (i - 1))
                    if i < CH:
                        for kt in range(2):
                            mm = pe.matmul(bank[:, 0:MEM], qh[:, kt, i * P:(i + 1) * P],
                                           km[:].rearrange("p k t -> p (k t)")[:, bass.ds(h * (2 * MEM) + kt * MEM, MEM)],
                                           start=(kt == 0), stop=(kt == 1))
                    else:
                        pe.wait_ge(h_ac, h * 7 + 1)
                        for kk in range(2):
                            mm = pe.matmul(bank[0:TS, kk * P:(kk + 1) * P], mst[:, kk, :], ident, start=True, stop=True)
                    mm.then_inc(h_s, 1)
                    if i >= 1:
                        turn(pe, h, i - 1)
                turn(pe, h, CH)
                pe.wait_ge(h_ac, h * 7 + 6)
                for dt in range(2):
                    pe.wait_ge(h_lo, h * 2 + dt)
                    for kt in range(2):
                        mm = pe.matmul(psY[:], vh[:, kt, dt * P:(dt + 1) * P], mpt[:, kt, 0:SEQ], start=(kt == 0), stop=(kt == 1))
                    mm.then_inc(h_pv, 1)
                pe.wait_ge(vc_in, h * 16 + 16)
                for dt in range(2):
                    for b in range(NB):
                        for kt in range(2):
                            o = dt * TS + b * DT
                            mm = pe.matmul(psA[:, o:o + DT], vc[:, b, kt, dt * P:(dt + 1) * P],
                                           mpt[:, kt, SEQ + b * DT:SEQ + (b + 1) * DT], start=(kt == 0), stop=(kt == 1))
                mm.then_inc(h_a, 1)

        def turn(pe, h, i):
            m = P if i < CH else TS
            pe.wait_ge(h_ac, h * 7 + (i + 1))
            pe.wait_ge(h_norm, h * 5 + (i + 1))
            for kk in range(2):
                mm = pe.matmul(psA[:, kk * P:kk * P + m], mp[0:m, i % 2, kk * P:(kk + 1) * P],
                               cst[0:m, CST["ident"][0]:CST["ident"][0] + m], start=True, stop=True)
            mm.then_inc(h_a, 1)

        def act_h(act):
            with act.Fori(0, 4) as h:
                act.wait_ge(h_a, h * 7)
                act.dma_start(kc[:], io["mem_kt"][bass.ds(h * P, P), :].rearrange("p (b k t) -> p b k t", b=NB, k=2)).then_inc(kc_in, 16)
                act.dma_start(vc[:], io["mem_v"][bass.ds(h * P, P), :].rearrange("p (b k t) -> p b k t", b=NB, k=2)).then_inc(vc_in, 16)
                for u in range(2):
                    par, k0 = slot(n_qm, u, h, 2)
                    act.wait_ge(dense_full[par], k0 + 1)
                    act.activation(two(qh[:, u, :]), dps[:, par, :, 0:HALF], ACT.Copy, scale=0.0625).then_inc(dense_free[par], 1)
                act.activation(vh[:], vm[:, :, bass.ds(h * MEM, MEM)], ACT.Copy).then_inc(h_q, 1)
                act.wait_ge(h_a, h * 7 + 1)
                act.activation(mst[:], psA[:, 0:2 * TS].rearrange("p (k t) -> p k t", k=2), ACT.Copy).then_inc(h_ac, 1)
                for i in range(NQ):
                    m = P if i < CH else TS
                    act.wait_ge(h_max, h * 5 + (i + 1))
                    act.activation(mp[0:m, i % 2, :], psLE[0:m, i % 2, 0:MEM], ACT.Exp, bias=mnm[0:m, i % 2:i % 2 + 1],
                                   accum_out=msum[0:m, i % 2:i % 2 + 1]).then_inc(h_exp, 1)
                    if i >= 1:
                        untile(act, h, i - 1)
                untile(act, h, CH)
                for dt in range(2):
                    act.wait_ge(h_pv, h * 2 + (dt + 1))
                    act.activation(y_hi[:].rearrange("p k t -> p (k t)")[:, bass.ds((h * 2 + dt) * T, SEQ)], psY[:], ACT.Copy).then_inc(h_hi, 1)
                act.wait_ge(h_a, h * 7 + 7)
                act.activation(mfix[:], psA[:, 0:2 * TS].rearrange("p (k t) -> p k t", k=2), ACT.Copy).then_inc(h_ac, 1)
                act.wait_ge(h_ac, h * 7 + 7)
                for dt in range(2):
                    act.activation(y_hi[:].rearrange("p k t -> p (k t)")[:, bass.ds((h * 2 + dt) * T + SEQ, TS)], mfix[:, dt, :], ACT.Copy).then_inc(h_hi2, 1)

        def untile(act, h, i):
            m = P if i < CH else TS
            act.wait_ge(h_a, h * 7 + (i + 2))
            act.activation(mpt[:, :, i * P:i * P + m], psA[:, 0:2 * P].rearrange("p (k q) -> p k q", k=2)[:, :, 0:m], ACT.Copy).then_inc(h_ac, 1)

        def dve_h(dve):
            link = chains["dve"]
            yl, yh = (a[:].rearrange("p k t -> p (k t)") for a in (y_lo, y_hi))
            with dve.Fori(0, 4) as h:
                link.enter(h, 7)

                def max_(i):
                    m = P if i < CH else TS
                    dve.wait_ge(h_s, h * 5 + (i + 1))
                    if i >= 2:
                        dve.wait_ge(h_exp, h * 5 + (i - 1))
                    dve.tensor_reduce(mnm[0:m, i % 2:i % 2 + 1], psLE[0:m, i % 2, 0:MEM], AX, ALU.max, negate=True).then_inc(h_max, 1)
                max_(0)
                for i in range(NQ):
                    m = P if i < CH else TS
                    if i < CH:
                        max_(i + 1)
                    dve.wait_ge(h_exp, h * 5 + (i + 1))
                    link(dve.reciprocal(mrc[0:m, i % 2:i % 2 + 1], msum[0:m, i % 2:i % 2 + 1]))
                    dve.tensor_scalar(mp[0:m, i % 2, :], mp[0:m, i % 2, :], mrc[0:m, i % 2:i % 2 + 1], None, ALU.mult).then_inc(h_norm, 1)
                for dt in range(2):
                    dve.wait_ge(h_hi, h * 2 + (dt + 1))
                    o = (h * 2 + dt) * T
                    dve.tensor_tensor(yl[:, bass.ds(o, SEQ)], psY[:], yh[:, bass.ds(o, SEQ)].bitcast(F32), ALU.subtract).then_inc(h_lo, 1)
                for dt in range(2):
                    dve.wait_ge(h_hi2, h * 2 + (dt + 1))
                    o = (h * 2 + dt) * T + SEQ
                    link(dve.tensor_tensor(yl[:, bass.ds(o, TS)], mfix[:, dt, :], yh[:, bass.ds(o, TS)].bitcast(F32), ALU.subtract))
            link.leave(4)
        h_hi2 = sem("h_hi2")
        pe_prog.append(pe_h); act_prog.append(act_h); dve_prog.append(dve_h)
        edge("edge_h")
        merge_stage("m2", False)
        edge("edge_m2")

        hs = ExitStack()
        h_res = stage_sb(hs, "h_res", [P, KT, T])
        h_in, mg_hi, wo_done = sem("h_in"), sem("mg_hi"), sem("wo_done")
        n_wo = take(KT)

        def residual_stage(n0, hi, lo, nk, done, k_done):
            def pe_f(pe):
                with pe.Fori(0, KT // 2) as i:
                    for u in range(2):
                        pe_dense(pe, slot(n0, u, i, 2), hi, lo, nk=nk)

            def dve_f(dve):
                with dve.Fori(0, KT // 2) as i:
                    for u in range(2):
                        par, k0 = slot(n0, u, i, 2)
                        dve.wait_ge(dense_full[par], k0 + 1)
                        hv = two(h_res[:].rearrange("p k t -> p (k t)")[:, bass.ds((i * 2 + u) * T, T)])
                        dve.tensor_tensor(hv, hv, dps[:, par, :, 0:HALF], ALU.add).then_inc(dense_free[par], 1)
            pe_prog.append(pe_f); dve_prog.append(dve_f)

        def act_wo(act):
            act.dma_start(h_res[:], io["x_t"]).then_inc(h_in, 16)
            for k in range(KT):
                act.activation(xn_hi[:, k, :], merged[:, k, :], ACT.Copy, scale=0.5).then_inc(mg_hi, 1)

        def dve_wo(dve):
            link = chains["dve"]
            for k in range(KT):
                dve.wait_ge(mg_hi, k + 1)
                dve.scalar_tensor_tensor(xn_lo[:, k, :], merged[:, k, :], 0.5, xn_hi[:, k, :].bitcast(F32), ALU.mult, ALU.subtract).then_inc(wo_done, 1)
            dve.wait_ge(h_in, 16)
        act_prog.append(act_wo); dve_prog.append(dve_wo)
        pe_prog.append(lambda pe: pe.wait_ge(wo_done, KT))
        residual_stage(n_wo, xn_hi, xn_lo, KT, None, None)
        edge("edge_wo")

        norm_stage("norm2", h_res, "norm2", xn_hi, xn_lo)
        edge("edge_norm2")
        fs = ExitStack()
        ff = lambda n, s, d=F32: stage_sb(fs, n, s, d)
        fin = ff("fin", [P, 2, FW])
        fout = ff("fout", [P, 2, FW])
        fth = ff("fth", [P, FW])
        fg = ff("fg", [P, FW])
        fa = ff("fa", [P, T])
        fs.close()
        f_in, f_conv, f_th, f_a, f_hi = sem("f_in"), sem("f_conv"), sem("f_th"), sem("f_a"), sem("f_hi")
        dve_prog.append(lambda dve: chains["dve"](dve.memset(fin[:, :, 0:FPAD], 0.0)))
        FO = FW - FPAD

        def ffn_piece(j0, count):
            n0 = take(2 * count)

            def pe_f(pe):
                with pe.Fori(0, count) as i:
                    for u in range(2):
                        pe_dense(pe, slot(n0, u, i, 2), xn_hi, xn_lo)

            def act_f(act):
                with act.Fori(0, count) as i:
                    j = i + j0
                    for u in range(2):
                        par, k0 = slot(n0, u, i, 2)
                        act.wait_ge(dense_full[par], k0 + 1)
                        act.wait_ge(f_conv, j * 2 + u)
                        fb = fin[:, u, :]
                        k = FPAD + NB * FPAD
                        tl = ftails[:].rearrange("p n k -> p (n k)")[:, bass.ds(j * k + u * FT * k, k)]
                        smp = dps[:, par, 1, SEQ - HALF:HALF].rearrange("p (b t) -> p b t", b=NB)
                        act.activation(fb[:, FPAD:FPAD + HALF], dps[:, par, 0, 0:HALF], ACT.Copy)
                        act.activation(fb[:, FPAD + HALF:FPB], dps[:, par, 1, 0:SEQ - HALF], ACT.Copy)
                        act.activation(tl[:, FPAD:k].rearrange("p (b k) -> p b k", b=NB), smp[:, :, DT - FPAD:DT], ACT.Copy)
                        act.activation(tl[:, 0:FPAD], dps[:, par, 1, SEQ - HALF - FPAD:SEQ - HALF], ACT.Copy)
                        act.activation(fb[:, FPB:FW].rearrange("p (b k) -> p b k", b=NB)[:, :, FPAD:FSB], smp, ACT.Copy).then_inc(dense_free[par], 1)
                    act.wait_ge(f_conv, j * 2 + 1)
                    act.wait_ge(f_a, j * 1)
                    act.activation(fth[:, 0:FO], fout[:, 0, 0:FO], ACT.Tanh).then_inc(f_th, 1)
                    act.wait_ge(f_a, j + 1)
                    act.activation(y_hi[:].rearrange("p k t -> p (k t)")[:, bass.ds(i * T, T)], fa[:], ACT.Copy).then_inc(f_hi, 1)

            def dve_f(dve):
                link = chains["dve"]
                with dve.Fori(0, count) as i:
                    link.enter(i, 2 * FCONV + 2)
                    j = i + j0
                    for u in range(2):
                        par, k0 = slot(n0, u, i, 2)
                        dve.wait_ge(dense_free[par], k0 + 1)
                        fb, fo = fin[:, u, :], fout[:, u, 0:FO]
                        fv = lambda name, n, o=0: fea[:, bass.ds(j * n + (FEA[name][0] + u * FT * n + o), 1)]
                        hist = fea[:, bass.ds(j * (NB * FPAD) + (FEA["fhist"][0] + u * FT * NB * FPAD), NB * FPAD)]
                        link(dve.tensor_copy(fb[:, FPB:FW].rearrange("p (b k) -> p b k", b=NB)[:, :, 0:FPAD],
                                             hist.rearrange("p (b k) -> p b k", b=NB)))
                        link(dve.tensor_scalar(fo, fb[:, 0:FO], fv("fconvw", FCONV, 0), fv("fconvb", 1), ALU.mult, ALU.add))
                        for k in range(1, FCONV):
                            ins = dve.scalar_tensor_tensor(fo, fb[:, k:k + FO], fv("fconvw", FCONV, k), fo, ALU.mult, ALU.add)
                            if k < FCONV - 1:
                                link(ins)
                        ins.then_inc(f_conv, 1)
                    dve.wait_ge(f_conv, j * 2 + 2)
                    dve.wait_ge(f_th, j + 1)
                    link(dve.scalar_tensor_tensor(fg[:, 0:FO], fth[:, 0:FO], 1.0, fout[:, 0, 0:FO], ALU.add, ALU.mult))
                    smp = lambda a: a[:, FPB:FW].rearrange("p (b k) -> p b k", b=NB)[:, :, 0:DT]
                    dve.wait_ge(f_hi, j)
                    dve.tensor_tensor(fa[:, 0:SEQ], fg[:, 0:SEQ], fout[:, 1, 0:SEQ], ALU.mult)
                    dve.tensor_tensor(fa[:, SEQ:T].rearrange("p (b t) -> p b t", b=NB), smp(fg), smp(fout[:, 1, :]), ALU.mult).then_inc(f_a, 1)
                    dve.wait_ge(f_hi, j + 1)
                    yl, yh = (a[:].rearrange("p k t -> p (k t)")[:, bass.ds(i * T, T)] for a in (y_lo, y_hi))
                    link(dve.tensor_tensor(yl, fa[:], yh.bitcast(F32), ALU.subtract))
                link.leave(count)
            pe_prog.append(pe_f); act_prog.append(act_f); dve_prog.append(dve_f)

        j0 = 0
        for piece, count in enumerate(FFN_PIECES):
            ffn_piece(j0, count)
            edge(f"edge_up{piece}")
            residual_stage(take(KT), y_hi, y_lo, count, None, None)
            edge(f"edge_down{piece}")
            j0 += count

        fo_ = ExitStack()
        yt = stage_sb(fo_, "yt", [P, KT, T])
        y_count = norm_stage("normf", h_res, "final", None, None, plain=yt)
        fo_.close()
        hs.close()

        def act_out(act):
            act.dma_start(io["tails"], tails[:].rearrange("p n k -> p (n k)")).then_inc(out_done, 16)
            act.dma_start(io["ftails"], ftails[:].rearrange("p n k -> p (n k)")).then_inc(out_done, 16)
            act.wait_ge(norm_sems[4], y_count)
            act.dma_start(io["y_t"], yt[:]).then_inc(out_done, 16)
        act_prog.append(act_out)
        final_waits += [(ssm_out, GROUPS * 32), (kv_out, 32), (memkv_out, 32), (out_done, 48)]
        block = ctx.enter_context(nc.Block())
        n_tiles = nstream[0]

        @block.sync
        def _(sp):
            def load(par, k, n):
                sp.wait_ge(w_split[par], k)
                sp.dma_start(w_raw[:, par, :], io["wstream"][n, :, :] if isinstance(n, int) else
                             io["wstream"][bass.ds(n, 1), :, :].rearrange("o p c -> (o p) c")).then_inc(w_landed[par], 16)
            first = (n_pages_at + 2) // 2
            first = min(first, n_tiles // 2)
            with sp.Fori(0, first) as i:
                for par in range(2):
                    load(par, i, i * 2 + par)
            tail = n_tiles % 2 and first == n_tiles // 2
            if tail:
                load(0, n_tiles // 2, n_tiles - 1)
            if sp_pages[0]:
                sp_pages[0](sp)
            if first < n_tiles // 2:
                with sp.Fori(first, n_tiles // 2) as i:
                    for par in range(2):
                        load(par, i, i * 2 + par)
            if n_tiles % 2 and not tail:
                load(0, n_tiles // 2, n_tiles - 1)
            for s_, v_ in final_waits:
                sp.wait_ge(s_, v_)

        @block.gpsimd
        def _(pool):
            turns = pool.alloc_register("turns")
            pool.reg_mov(turns, 0)

            def split(par, k, n):
                pool.wait_ge(dense_full[par], k)
                pool.wait_ge(w_landed[par], k * 16 + 16)
                pool.sem_inc(w_taken, 1)
                pool.tensor_scalar(w_hi[:, par, :], w_raw[:, par, :], 1.0, 1.0, ALU.mult, ALU.mult).then_inc(w_hi_done, 1)
                pool.wait_ge(w_hi_done, n + 1)
                pool.tensor_tensor(w_lo[:, par, :], w_raw[:, par, :], w_hi[:, par, :].bitcast(F32), ALU.subtract).then_inc(w_split[par], 1)
            with pool.Fori(0, n_tiles // 2) as i:
                for par in range(2):
                    split(par, i, i * 2 + par)
            if n_tiles % 2:
                split(0, n_tiles // 2, n_tiles - 1)

        @block.tensor
        def _(pe):
            for f in pe_prog:
                f(pe)

        @block.scalar
        def _(act):
            chains["act"] = Chain(act, act_step)
            for f in act_prog:
                f(act)

        @block.vector
        def _(dve):
            chains["dve"] = Chain(dve, dve_step)
            for f in dve_prog:
                f(dve)


def weight_stream(w_in, w_ssd_out, w_attn_out, w_mem_kv, w_mem_out, w_o, w_up, w_down):
    tiles = []

    def add(w, column, row=0):
        tile = np.zeros((D, P), w.dtype)
        block = w[row:row + D, column:column + P]
        tile[:block.shape[0], :block.shape[1]] = block
        tiles.append(tile.reshape(KT, P, P).transpose(1, 0, 2).reshape(P, D))

    inner = 2 * D
    x_at, b_at, c_at, dt_at = inner, 2 * inner, 2 * inner + D, 2 * inner + 2 * D
    q_at = dt_at + HEADS
    k_at, v_at = q_at + D, q_at + D + 256
    qm_at = v_at + 256
    gate_at = qm_at + D

    def groups(which):
        for g in which:
            for column in (x_at + g * 256, x_at + g * 256 + P, b_at + g * P, c_at + g * P, g * 256, g * 256 + P):
                add(w_in, column)

    def branch(number, w, row=0):
        for m in range(KT):
            add(w_in, gate_at + number * D + m * P)
            add(w, m * P, row)

    add(w_in, dt_at)
    groups(range(4))
    for m in range(KT):
        add(w_ssd_out, m * P)
    groups(range(4, 8))
    branch(0, w_ssd_out, D)
    for column in (k_at, k_at + P, v_at, v_at + P):
        add(w_in, column)
    for m in range(KT):
        add(w_in, q_at + m * P)
    branch(1, w_attn_out)
    for m in range(2 * KT):
        add(w_mem_kv, m * P)
    for m in range(KT):
        add(w_in, qm_at + m * P)
    branch(2, w_mem_out)
    for m in range(KT):
        add(w_o, m * P)
    j = 0
    for piece, count in enumerate(FFN_PIECES):
        for _ in range(count):
            add(w_up, j * P)
            add(w_up, (FT + j) * P)
            j += 1
        for m in range(KT):
            add(w_down, m * P, piece * D)
    return np.stack(tiles)


def constants():
    out = np.zeros((P, CST_W), np.float32)

    def put(name, a):
        at, _ = CST[name]
        out[:a.shape[0], at:at + a.shape[1]] = a

    i, s, e, b = np.arange(P), np.arange(TS), np.arange(DT), np.arange(NB)
    same = s[:, None] // DT == s[None] // DT
    put("ident", np.eye(P))
    put("ones", np.ones((P, P)))
    put("upto_p", i[:, None] <= i[None])
    put("after_p", i[:, None] > i[None])
    put("upto_s", same & (s[:, None] <= s[None]))
    put("after_s", same & (s[:, None] > s[None]))
    put("same_b", s[:, None] // DT == b[None])
    rot, swap = np.zeros((P, P)), np.zeros((P, P))
    for head in (0, 64):
        rot[head + 8 + e, head + e] = -1
        rot[head + e, head + 8 + e] = 1
    swap[i, (i + 64) % P] = 1
    put("rot", rot)
    put("swap", swap)
    put("causal", np.where(i[:, None] >= i[None], 0, NEG))
    put("own", np.where(i[:, None] % DT >= e[None], 0, NEG))
    put("blk_lt", np.tile((b[None] < b[:, None]).reshape(1, NB * NB), (P, 1)))
    position = np.concatenate([np.arange(SEQ), np.tile(PAST + e, NB)]).astype(np.float32)
    inverse = np.float32(500000.0) ** (-e.astype(np.float32) * np.float32(2) / np.float32(16))
    angle = (inverse.astype(np.float32)[:, None] * position[None]).astype(np.float32)
    cos, sin = np.ones((P, T)), np.zeros((P, T))
    for row in (0, 8, 64, 72):
        cos[row:row + 8], sin[row:row + 8] = np.cos(angle), np.sin(angle)
    put("cos", cos)
    put("sin", sin)
    return out


def features_down(a):
    return np.ascontiguousarray(a.T.reshape(-1, P, a.shape[0]).transpose(1, 0, 2))


def tokens_down(a):
    return a.transpose(2, 1, 0).reshape(a.shape[2], -1)


def per_feature(inp):
    out = np.zeros((P, FEA_W), np.float32)

    def put(name, a):
        at, _ = FEA[name]
        a = a.reshape(a.shape[0], -1)
        out[:a.shape[0], at:at + a.shape[1]] = a

    def column(a):
        return a.reshape(-1, P).T

    def rows(a, tiles):
        return a.reshape(-1, tiles, P).transpose(2, 1, 0)

    put("norm1", column(inp["norm1_w"][0]))
    put("norm2", column(inp["norm2_w"][0]))
    put("memn", column(inp["mem_norm_w"][0]))
    put("final", column(inp["final_norm_w"]))
    put("ssdn", column(inp["ssd_norm_w"][0]))
    put("dskip", column(np.repeat(inp["d_skip"][0], 64)))
    put("dtb", inp["dt_bias"][0][:, None])
    put("alog", inp["a_log"][0][:, None])
    put("convw", rows(inp["ssd_conv_w"][0], NCV))
    put("convb", column(inp["ssd_conv_b"][0]))
    put("hist", rows(inp["state_conv"][0].reshape(NB * PAD, -1), NCV))
    put("fconvw", rows(inp["ffn_conv_w"][0], 2 * FT))
    put("fconvb", column(inp["ffn_conv_b"][0]))
    put("fhist", rows(inp["state_ffn_conv"][0].reshape(NB * FPAD, -1), 2 * FT))
    return out


def kernel(**inputs):
    import concourse.bacc as _bacc
    from concourse.bass_utils import run_bass_kernel_spmd as _run

    inp = {name: np.asarray(a) for name, a in inputs.items()}
    data = {
        "wstream": weight_stream(*(inp[name][0] for name in ("w_in", "w_ssd_out", "w_attn_out", "w_mem_kv", "w_mem_out",
                                                             "w_o", "w_up", "w_down"))),
        "x_t": features_down(np.concatenate([inp["x_prompt"][0], inp["x_sample"].reshape(TS, D)], 0)),
        "cst": constants(),
        "fea": per_feature(inp),
        "state_t": inp["state_ssm"][0].reshape(NB, GROUPS, GH, 64, P).transpose(1, 4, 0, 2, 3).reshape(GROUPS * P, -1),
        "mem_t": features_down(inp["mem_prompt"][0]),
        "k_pages": inp["cache_k"][0].reshape(-1, PAGE, 2, P).transpose(0, 3, 2, 1).reshape(-1, P, 2 * PAGE),
        "v_pages": inp["cache_v"][0].reshape(-1, PAGE, 2 * P),
        "mem_kt": inp["cache_mem_k"][0].reshape(NB, MEM, 4, 2, P).transpose(2, 4, 0, 3, 1).reshape(4 * P, -1),
        "mem_v": inp["cache_mem_v"][0].reshape(NB, 2, P, 4, MEM).transpose(3, 2, 0, 1, 4).reshape(4 * P, -1),
        "page_table": inp["page_table"].reshape(1, -1),
    }
    outs = {"y_t": (P, KT, T), "kv_t": (P, 4, T), "memkv_t": (P, 2 * KT, MEM), "ssm_p": (GROUPS * P, 256),
            "ssm_s": (GROUPS * P, NB * 256), "tails": (P, NCV * (PAD + NB * PAD)),
            "ftails": (P, 2 * FT * (FPAD + NB * FPAD))}

    nc = _bacc.Bacc("TRN2", target_bir_lowering=False, num_devices=1)
    arrays, io = {}, {}
    for name, a in data.items():
        a = np.ascontiguousarray(a)
        arrays[f"{name}_dram"] = a
        io[name] = nc.dram_tensor(f"{name}_dram", a.shape, mybir.dt.from_np(a.dtype), kind="ExternalInput").ap()
    for name, shape in outs.items():
        io[name] = nc.dram_tensor(f"{name}_dram", shape, F32, kind="ExternalOutput").ap()
    build_program(nc, io)
    result = _run(nc, [arrays], core_ids=[0]).results[0]
    got = {name: np.asarray(result[f"{name}_dram"]) for name in outs}

    def parts(a, rows):
        return a[:rows], a[rows:]

    y_p, y_s = parts(tokens_down(got["y_t"]), SEQ)
    k_p, k_s = parts(tokens_down(got["kv_t"][:, 0:2]), SEQ)
    v_p, v_s = parts(tokens_down(got["kv_t"][:, 2:4]), SEQ)
    mem_k, mem_v = (tokens_down(got["memkv_t"][:, j * KT:(j + 1) * KT]).reshape(1, 1, MEM, 4, 256) for j in range(2))
    ssm_p = got["ssm_p"].reshape(GROUPS, P, GH, 64).transpose(0, 2, 3, 1).reshape(1, 1, HEADS, 64, P)
    ssm_s = got["ssm_s"].reshape(GROUPS, P, NB, GH, 64).transpose(2, 0, 3, 4, 1).reshape(1, NB, HEADS, 64, P)
    conv_p, conv_s = parts(tokens_down(got["tails"].reshape(P, NCV, -1)), PAD)
    ffn_p, ffn_s = parts(tokens_down(got["ftails"].reshape(P, 2 * FT, -1)), FPAD)
    return tuple(np.ascontiguousarray(a) for a in (
        y_p.reshape(1, SEQ, D), y_s.reshape(NB, DT, D),
        k_p.reshape(1, 1, SEQ, 4, 64), v_p.reshape(1, 1, SEQ, 4, 64), mem_k, mem_v, ssm_p,
        conv_p.reshape(1, 1, PAD, -1), ffn_p.reshape(1, 1, FPAD, -1),
        k_s.reshape(1, NB, DT, 4, 64), v_s.reshape(1, NB, DT, 4, 64), ssm_s,
        conv_s.reshape(1, NB, PAD, -1), ffn_s.reshape(1, NB, FPAD, -1)))
```

```python
from contextlib import ExitStack

import numpy as np

import concourse.bass as bass
from concourse import mybir

F32 = mybir.dt.float32
F32R = mybir.dt.float32r
ALU = mybir.AluOpType
ACT = mybir.ActivationFunctionType
AX = mybir.AxisListType.X

P = 128
D = 1024
KT = D // P
SEQ = 512
NB, DT = 8, 8
TS = NB * DT
T = SEQ + TS
HALF = T // 2
CH = SEQ // P
HEADS = 32
GROUPS = 8
GH = HEADS // GROUPS
SCONV, FCONV = 4, 3
NCV = 32
FT = 22
PAD = SCONV - 1
PBUF = SEQ + PAD
SB1 = DT + PAD
CW = PBUF + NB * SB1
FPAD = FCONV - 1
FPB = SEQ + FPAD
FSB = DT + FPAD
FW = FPB + NB * FSB
PAST, PAGE = 2048, 128
NPG = PAST // PAGE
MEM = 256
EPS = 1e-6
NEG = -1e30


def offsets(parts):
    at, out = 0, {}
    for name, width in parts:
        out[name] = (at, width)
        at += width
    return out, at


CST, CST_W = offsets([
    ("ident", P), ("ones", P), ("upto_p", P), ("after_p", P), ("upto_s", TS), ("after_s", TS),
    ("same_b", NB), ("rot", P), ("swap", P), ("causal", P), ("own", 2 * TS - DT), ("blk_lt", 64),
    ("cos", T), ("sin", T)])
FEA, FEA_W = offsets([
    ("norm1", KT), ("norm2", KT), ("memn", KT), ("final", KT), ("ssdn", 16), ("dskip", 16),
    ("dtb", 1), ("alog", 1), ("convw", NCV * SCONV), ("convb", NCV), ("hist", NCV * NB * PAD),
    ("fconvw", 2 * FT * FCONV), ("fconvb", 2 * FT), ("fhist", 2 * FT * NB * FPAD)])

N_DT = 1
N_GRP = 6
FFN_PIECES = (8, 8, 6)


class Chain:

    def __init__(self, eng, sem):
        self.e, self.sem, self.base, self.i, self.per, self.local = eng, sem, 0, None, 0, 0

    def value(self):
        v = self.base + self.local
        return v if self.i is None else self.i * self.per + v

    def __call__(self, ins):
        ins.then_inc(self.sem, 1)
        self.local += 1
        self.e.wait_ge(self.sem, self.value())

    def enter(self, i, per):
        self.base, self.local, self.i, self.per = self.base + self.local, 0, i, per

    def leave(self, trips):
        assert self.local == self.per, f"links of a turn: {self.local}, not {self.per}"
        self.base, self.local, self.i = self.base + trips * self.per, 0, None


def build_program(nc, io):
    ctx = ExitStack()
    with ctx:
        def sb(name, shape, dt=F32):
            return ctx.enter_context(nc.sbuf_tensor(name, shape, dt))

        def stage_sb(stack, name, shape, dt=F32):
            return stack.enter_context(nc.sbuf_tensor(name, shape, dt))

        def sem(name):
            return ctx.enter_context(nc.semaphore(name))

        cst = sb("cst", [P, CST_W])
        fea = sb("fea", [P, FEA_W])
        xn_hi, xn_lo = sb("xn_hi", [P, KT, T], F32R), sb("xn_lo", [P, KT, T], F32R)
        y_hi, y_lo = sb("y_hi", [P, KT, T], F32R), sb("y_lo", [P, KT, T], F32R)
        merged = sb("merged", [P, KT, T])
        w_raw = sb("w_raw", [P, 2, D])
        w_hi, w_lo = sb("w_hi", [P, 2, D], F32R), sb("w_lo", [P, 2, D], F32R)
        w_taken = sem("w_taken")
        pad1 = sb("pad1", [P, 1])
        era = ExitStack()
        dt_tok = stage_sb(era, "dt_tok", [P, 2, CH + 1, HEADS])
        dec = stage_sb(era, "dec", [P, CH + 1, HEADS])
        tot = stage_sb(era, "tot", [P, CH * HEADS + NB * HEADS])

        tails = stage_sb(era, "tails", [P, NCV, PAD + NB * PAD])

        def c_(name, p=P):
            at, w = CST[name]
            return cst[0:p, at:at + w]

        def f_(name, i=0, n=1, p=P):
            at, _ = FEA[name]
            return fea[0:p, at + i * n:at + i * n + n]

        ident, ones = c_("ident"), c_("ones")

        dps = ctx.enter_context(nc.psum_tensor("dps", [P, 2, 2, 512], F32))
        psA = ctx.enter_context(nc.psum_tensor("psA", [P, 512], F32))
        psLE = ctx.enter_context(nc.psum_tensor("psLE", [P, 2, 512], F32))
        psL, psE = psLE[:, 0, :], psLE[:, 1, :]
        psY = ctx.enter_context(nc.psum_tensor("psY", [P, 512], F32))

        w_landed = [sem("w_landed0"), sem("w_landed1")]
        w_hi_done = sem("w_hi_done")
        w_split = [sem("w_split0"), sem("w_split1")]
        dense_full = [sem("dense_full0"), sem("dense_full1")]
        dense_free = [sem("dense_free0"), sem("dense_free1")]
        const_in, x_in = sem("const_in"), sem("x_in")
        out_done = sem("out_done")
        dve_step, act_step = sem("dve_step"), sem("act_step")
        stage_done, passed = [sem("pe_stage"), sem("act_stage"), sem("dve_stage")], [0]

        pe_prog, act_prog, dve_prog = [], [], []
        chains = {}

        def edge(name):
            passed[0] += 1
            count = passed[0]

            def side(own):
                def f(e):
                    e.drain().then_inc(stage_done[own], 1)
                    for k in range(3):
                        e.wait_ge(stage_done[k], count)
                return f
            pe_prog.append(side(0)); act_prog.append(side(1)); dve_prog.append(side(2))

        def halves(ps, par, width=T):
            return ps[:, par, :, 0:HALF]

        def two(ap):
            return ap.rearrange("p (h c) -> p h c", h=2)

        def slot(n0, u, i=0, nb=0):
            return (n0 + u) % 2, (n0 + u) // 2 + i * (nb // 2)

        def pe_dense(pe, tile, hi, lo, nk=KT, width=T):
            par, k0 = tile
            pe.wait_ge(w_split[par], k0 + 1)
            pe.wait_ge(dense_free[par], k0)
            spans = [(0, 0, width)] if width <= 512 and width != T else [(0, 0, HALF), (1, HALF, HALF)]
            for k in range(nk):
                wh, wl = w_hi[:, par, k * P:(k + 1) * P], w_lo[:, par, k * P:(k + 1) * P]
                for j, (w, a) in enumerate(((wh, hi), (wh, lo), (wl, hi))):
                    for b, c0, cw in spans:
                        mm = pe.matmul(dps[:, par, b, 0:cw], w, a[:, k, c0:c0 + cw],
                                       start=(k == 0 and j == 0), stop=(k == nk - 1 and j == 2))
            mm.then_inc(dense_full[par], 1)

        final_waits = []
        nstream = [0]

        def take(count):
            n = nstream[0]
            nstream[0] += count
            return n

        norm_sems = [sem(f"norm_{k}") for k in ("sq_ready", "sq_used", "mean", "root", "t_ready", "hi_ready")]
        norm_count = [0]

        def norm_stage(name, src, wname, hi, lo, width=T, kts=KT, ready=(), half_in=1.0, plain=None):
            st = ExitStack()
            sq = stage_sb(st, f"{name}_sq", [P, 2, width])
            rs = stage_sb(st, f"{name}_rs", [P, width])
            t = stage_sb(st, f"{name}_t", [P, 2, width])
            st.close()
            sq_ready, sq_used, mean_ready, root_ready, t_ready, hi_ready = norm_sems
            norms = norm_count[0]
            norm_count[0] += 1
            done = norms * kts
            if width == T:
                sp = lambda ap: two(ap)
                ps = dps[:, 0, :, 0:HALF]
                spans = [(0, 0, HALF), (1, HALF, HALF)]
            else:
                sp = lambda ap: ap
                ps = dps[:, 0, 0, 0:width]
                spans = [(0, 0, width)]

            def pe_f(pe):
                for k in range(kts):
                    pe.wait_ge(sq_ready, done + k + 1)
                    for b, c0, cw in spans:
                        mm = pe.matmul(dps[:, 0, b, 0:cw], ones, sq[:, k % 2, c0:c0 + cw],
                                       start=(k == 0), stop=(k == kts - 1))
                    mm.then_inc(sq_used, 1)

            def act_f(act):
                for s, v in ready:
                    act.wait_ge(s, v)
                for k in range(kts):
                    if k >= 2:
                        act.wait_ge(sq_used, done + k - 1)
                    act.activation(sq[:, k % 2, :], src[:, k, :], ACT.Square).then_inc(sq_ready, 1)
                act.wait_ge(mean_ready, norms + 1)
                act.activation(rs[:], rs[:], ACT.Sqrt).then_inc(root_ready, 1)
                if hi is not None:
                    for k in range(kts):
                        act.wait_ge(t_ready, done + k + 1)
                        act.activation(hi[:, k, 0:width], t[:, k % 2, :], ACT.Copy).then_inc(hi_ready, 1)

            def dve_f(dve):
                link = chains["dve"]
                for s, v in ready:
                    dve.wait_ge(s, v)
                dve.wait_ge(sq_used, done + kts)
                dve.tensor_scalar(sp(rs[:]), ps, 1.0 / D, EPS, ALU.mult, ALU.add).then_inc(mean_ready, 1)
                dve.wait_ge(root_ready, norms + 1)
                link(dve.reciprocal(rs[:], rs[:]))
                for k in range(kts):
                    if hi is None:
                        dve.scalar_tensor_tensor(plain[:, k, :], src[:, k, :], f_(wname, k), rs[:],
                                                 ALU.mult, ALU.mult).then_inc(t_ready, 1)
                        continue
                    if k >= 2:
                        dve.wait_ge(hi_ready, done + k - 1)
                    dve.scalar_tensor_tensor(t[:, k % 2, :], src[:, k, :], f_(wname, k), rs[:],
                                             ALU.mult, ALU.mult).then_inc(t_ready, 1)
                    dve.wait_ge(hi_ready, done + k + 1)
                    link(dve.tensor_tensor(lo[:, k, 0:width], t[:, k % 2, :], hi[:, k, 0:width].bitcast(F32),
                                           ALU.subtract))
            pe_prog.append(pe_f); act_prog.append(act_f); dve_prog.append(dve_f)
            return done + kts

        s0 = ExitStack()
        x_t = stage_sb(s0, "x_t", [P, KT, T])

        def act_load(act):
            act.dma_start(cst[:], io["cst"]).then_inc(const_in, 16)
            act.dma_start(fea[:], io["fea"]).then_inc(const_in, 16)
            act.dma_start(x_t[:], io["x_t"]).then_inc(x_in, 16)

        act_prog.append(act_load)
        pe_prog.append(lambda pe: pe.wait_ge(const_in, 32))

        def dve_scale(dve):
            link = chains["dve"]
            dve.wait_ge(const_in, 32)
            for name, w in (("convw", NCV * SCONV), ("convb", NCV), ("ssdn", 16),
                            ("fconvw", FT * FCONV), ("fconvb", FT)):
                a, _ = FEA[name]
                link(dve.tensor_scalar(fea[:, a:a + w], fea[:, a:a + w], 0.5, None, ALU.mult))
        dve_prog.append(dve_scale)
        norm_stage("norm1", x_t, "norm1", xn_hi, xn_lo, ready=((const_in, 32), (x_in, 16)))
        s0.close()
        edge("edge_norm1")

        s1 = ExitStack()
        n0 = take(N_DT)
        dtv = [stage_sb(s1, f"dtv{i}", [HEADS, T]) for i in range(6)]
        acol = stage_sb(s1, "acol", [HEADS, 1])
        da_b = stage_sb(s1, "da_b", [TS, NB, HEADS])
        dt_x, dt_e, dt_l, dt_t, dt_f = (sem(f"dt_{k}") for k in ("x", "exp", "ln", "tr", "full"))
        dt_n, dt_u, a_neg, dt_tokd = sem("dt_n"), sem("dt_u"), sem("dt_a"), sem("dt_tokd")
        dtx, dtr, dtn, dte, dtu, dtl = dtv

        def pe_dt(pe):
            pe_dense(pe, slot(n0, 0), xn_hi, xn_lo)
            pe.wait_ge(dt_f, 1)
            for j, v in enumerate((dtx, dtr)):
                for c in range(CH + 1):
                    m = P if c < CH else TS
                    o = (j * (CH + 1) + c) * HEADS
                    tr = pe.transpose(psA[0:m, o:o + HEADS], v[:, c * P:c * P + m], cst[0:HEADS, CST["ident"][0]:CST["ident"][0] + HEADS])
            tr.then_inc(dt_t, 1)
            pe.wait_ge(dt_tokd, 1)
            da = dt_tok[:, 1, 0:CH, :].rearrange("p c h -> p (c h)")
            pe.matmul(psL[:, 0:CH * HEADS], c_("after_p"), da, start=True, stop=True)
            pe.matmul(psL[0:TS, 128:160], c_("after_s", TS), dt_tok[0:TS, 1, CH, :], start=True, stop=True)
            pe.matmul(psE[:, 0:CH * HEADS], ones, da, start=True, stop=True)
            pe.matmul(psE[:, 128:384], cst[0:TS, CST["ones"][0]:CST["ones"][0] + P],
                      da_b[:].rearrange("p b h -> p (b h)"), start=True, stop=True).then_inc(dt_t, 1)

        def act_dt(act):
            link = chains["act"]
            act.wait_ge(dense_full[0], 1)
            act.activation(two(dtx[:]), dps[0:HEADS, 0, :, 0:HALF], ACT.Identity, bias=f_("dtb", p=HEADS)).then_inc(dense_free[0], 1)
            act.activation(acol[:], f_("alog", p=HEADS), ACT.Exp).then_inc(a_neg, 1)
            act.wait_ge(dt_n, 1)
            act.activation(dte[:], dtn[:], ACT.Exp).then_inc(dt_e, 1)
            act.wait_ge(dt_u, 1)
            act.activation(dtl[:], dtu[:], ACT.Ln).then_inc(dt_l, 1)
            act.wait_ge(dt_t, 2)
            link(act.activation(dec[:, 0:CH, :].rearrange("p c h -> p (c h)"), psL[:, 0:128], ACT.Exp))
            link(act.activation(dec[0:TS, CH, :], psL[0:TS, 128:160], ACT.Exp))
            link(act.activation(tot[:], psE[:, 0:384], ACT.Exp))

        def dve_dt(dve):
            link = chains["dve"]
            tt = lambda o, a, b, op: link(dve.tensor_tensor(o, a, b, op))
            ts = lambda o, a, s, op: link(dve.tensor_scalar(o, a, s, None, op))
            dve.wait_ge(dense_free[0], 1)
            ts(dtr[:], dtx[:], 0.0, ALU.max)
            ts(dtn[:], dtx[:], -1.0, ALU.mult)
            dve.tensor_tensor(dtn[:], dtn[:], dtx[:], ALU.min).then_inc(dt_n, 1)
            dve.wait_ge(dt_e, 1)
            dve.tensor_scalar(dtu[:], dte[:], 1.0, None, ALU.add).then_inc(dt_u, 1)
            dve.wait_ge(dt_l, 1)
            ts(dtu[:], dtu[:], 1.0, ALU.subtract)
            ts(dtn[:], dtu[:], 0.0, ALU.is_equal)
            tt(dtl[:], dtl[:], dtn[:], ALU.add)
            tt(dtu[:], dtu[:], dtn[:], ALU.add)
            link(dve.reciprocal(dtu[:], dtu[:]))
            tt(dtl[:], dtl[:], dtu[:], ALU.mult)
            tt(dtl[:], dtl[:], dte[:], ALU.mult)
            tt(dtx[:], dtl[:], dtr[:], ALU.add)
            dve.wait_ge(a_neg, 1)
            link(dve.tensor_scalar(acol[:], acol[:], -1.0, None, ALU.mult))
            dve.tensor_scalar(dtr[:], dtx[:], acol[:], None, ALU.mult).then_inc(dt_f, 1)
            dve.wait_ge(dt_t, 1)
            link(dve.tensor_copy(dt_tok[:, :, 0:CH, :], psA[:, 0:320].rearrange("p (j c h) -> p j c h", j=2, c=CH + 1)[:, :, 0:CH, :]))
            link(dve.tensor_copy(dt_tok[0:TS, :, CH, :], psA[0:TS, 0:320].rearrange("p (j c h) -> p j c h", j=2, c=CH + 1)[:, :, CH, :]))
            dve.tensor_tensor(da_b[:], dt_tok[0:TS, 1:2, CH, :].to_broadcast([TS, NB, HEADS]),
                              c_("same_b", TS).rearrange("p (b o) -> p b o", o=1).to_broadcast([TS, NB, HEADS]),
                              ALU.mult).then_inc(dt_tokd, 1)

        pe_prog.append(pe_dt); act_prog.append(act_dt); dve_prog.append(dve_dt)
        s1.close()
        edge("edge_dt")

        ssd_stack = ExitStack()
        ss = lambda n, s, d=F32: stage_sb(ssd_stack, n, s, d)
        cbuf = ss("cbuf", [P, 2, CW])
        cout = ss("cout", [P, 2, CW])
        cth = ss("cth", [P, CW])
        xg2, zg2 = ss("xg", [P, 2, 2, T]), ss("zg", [P, 2, 2, T])
        bg2, cg2 = ss("bg", [P, 2, T]), ss("cg", [P, 2, T])
        yg = ss("yg", [P, 2, T])
        rhs_a = ss("rhs_a", [P, GH, P])
        cbm = ss("cbm", [P, P])
        btok = ss("btok", [P, P])
        xdt, xdtd = ss("xdt", [P, 256]), ss("xdtd", [P, 256])
        l_exp, e_exp = ss("l_exp", [P, 512]), ss("e_exp", [P, 512])
        state = ss("state", [P, 256])
        st_in = ss("st_in", [P, NB, 256])
        bm = ss("bm", [TS, NB, P])
        rstd = ss("rstd", [P, T])
        ssd_stack.close()
        era.close()

        conv_ready = sem("conv_ready")
        th_ready, feat_ready = sem("th_ready"), sem("feat_ready")
        zth_ready = sem("zth_ready")
        a_full, a_free, le_full, exp_ready = sem("a_full"), sem("a_free"), sem("le_full"), sem("exp_ready")
        rhs_ready, m_ready, y_full, y_free = sem("rhs_ready"), sem("m_ready"), sem("y_full"), sem("y_free")
        n_full, n_free = sem("n_full"), sem("n_free")
        st_landed = sem("st_landed")
        gsq_ready, gsum_full, gmean_ready, groot_ready = sem("gsq_ready"), sem("gsum_full"), sem("gmean_ready"), sem("groot_ready")
        gate_ready, gt_ready, ghi_ready = sem("gate_ready"), sem("gt_ready"), sem("ghi_ready")
        ssm_ready, ssm_out = sem("ssm_ready"), sem("ssm_out")

        def cols(ap2, off, w=1):
            return ap2[:, bass.ds(off, w)]

        def flat(t3):
            return t3[:].rearrange("p k t -> p (k t)")

        def by_seq(ap):
            return ap.rearrange("p (b t) -> p b t", b=NB)

        def per_head(ap):
            return ap.rearrange("p (h d) -> p h d", h=GH)

        def spread(ap, m, w):
            return ap.rearrange("p (h o) -> p h o", o=1).to_broadcast([m, GH, w])

        def over_heads(ap, m, w):
            return ap.rearrange("p (o i) -> p o i", o=1).to_broadcast([m, GH, w])

        def tile_of(N, u):
            late = (KT if N > 4 else 0) if isinstance(N, int) else 0
            return (N_DT + late + u) % 2, (N_DT + late + u) // 2 + N * (N_GRP // 2)

        def tail_at(N, u):
            return N * 2 + u if u < 2 else N + (16 if u == 2 else 24)

        def act_copy(act, N, u):
            par, k0 = tile_of(N, u)
            act.wait_ge(dense_full[par], k0 + 1)
            if u >= 2:
                act.wait_ge(conv_ready, N * 4 + u - 1)
            cb = cbuf[:, u % 2, :]
            n_tail = PAD + NB * PAD
            tl = cols(flat(tails), tail_at(N, u) * n_tail, n_tail)
            sample = by_seq(dps[:, par, 1, SEQ - HALF:HALF])
            act.activation(cb[:, PAD:PAD + HALF], dps[:, par, 0, 0:HALF], ACT.Copy)
            act.activation(cb[:, PAD + HALF:PBUF], dps[:, par, 1, 0:SEQ - HALF], ACT.Copy)
            act.activation(by_seq(tl[:, PAD:n_tail]), sample[:, :, DT - PAD:DT], ACT.Copy)
            act.activation(tl[:, 0:PAD], dps[:, par, 1, SEQ - HALF - PAD:SEQ - HALF], ACT.Copy)
            act.activation(by_seq(cb[:, PBUF:CW])[:, :, PAD:SB1], sample, ACT.Copy).then_inc(dense_free[par], 1)

        def act_tanh(act, N, u):
            act.wait_ge(conv_ready, N * 4 + u + 1)
            act.wait_ge(feat_ready, N * 4 + u)
            act.activation(cth[:, 0:CW - PAD], cout[:, u % 2, 0:CW - PAD], ACT.Tanh).then_inc(th_ready, 1)

        def act_z(act, N, q, j):
            par, k0 = tile_of(N, 4 + j)
            act.wait_ge(dense_full[par], k0 + 1)
            act.activation(two(zg2[:, q, j, :]), dps[:, par, :, 0:HALF], ACT.Tanh, scale=0.5).then_inc(zth_ready, 1)

        GROUP_LINKS = 58

        def dve_conv(dve, link, N, u):
            tix = tail_at(N, u)
            cb, co = cbuf[:, u % 2, :], cout[:, u % 2, 0:CW - PAD]
            par, k0 = tile_of(N, u)
            dve.wait_ge(dense_free[par], k0 + 1)
            link(dve.tensor_copy(by_seq(cb[:, PBUF:CW])[:, :, 0:PAD], by_seq(cols(fea, tix * (NB * PAD) + FEA["hist"][0], NB * PAD))))
            w = lambda j: cols(fea, tix * SCONV + (FEA["convw"][0] + j))
            if u >= 2:
                dve.wait_ge(th_ready, N * 4 + u - 1)
            link(dve.tensor_scalar(co, cb[:, 0:CW - PAD], w(0), cols(fea, tix + FEA["convb"][0]), ALU.mult, ALU.add))
            for j in range(1, SCONV):
                ins = dve.scalar_tensor_tensor(co, cb[:, j:j + CW - PAD], w(j), co, ALU.mult, ALU.add)
                if j < SCONV - 1:
                    link(ins)
            ins.then_inc(conv_ready, 1)
            dve.wait_ge(conv_ready, N * 4 + u + 1)

        def dve_silu(dve, N, q, u):
            dst = (xg2[:, q, 0, :], xg2[:, q, 1, :], bg2[:, q, :], cg2[:, q, :])[u]
            co, th = cout[:, u % 2, :], cth
            seqs = lambda a: by_seq(a[:, PBUF:CW])[:, :, 0:DT]
            dve.wait_ge(th_ready, N * 4 + u + 1)
            dve.scalar_tensor_tensor(dst[:, 0:SEQ], th[:, 0:SEQ], 1.0, co[:, 0:SEQ], ALU.add, ALU.mult)
            dve.scalar_tensor_tensor(by_seq(dst[:, SEQ:T]), seqs(th), 1.0, seqs(co), ALU.add, ALU.mult).then_inc(feat_ready, 1)
            dve.wait_ge(feat_ready, N * 4 + u + 1)

        def dve_z(dve, N, q, j):
            dve.wait_ge(zth_ready, N * 2 + j + 1)
            par, k0 = tile_of(N, 4 + j)
            dve.scalar_tensor_tensor(two(zg2[:, q, j, :]), two(zg2[:, q, j, :]), 1.0, dps[:, par, :, 0:HALF],
                                     ALU.add, ALU.mult).then_inc(dense_free[par], 1)
            dve.wait_ge(dense_free[par], k0 + 1)

        def dve_rhs(dve, G, c):
            m = P if c < CH else TS
            up = c_("upto_p") if c < CH else c_("upto_s", TS)
            dve.tensor_tensor(rhs_a[0:m, :, 0:m], over_heads(up, m, m), spread(cols(dt_tok[0:m, 1, c, :], G * GH, GH), m, m),
                              ALU.mult).then_inc(rhs_ready, 1)

        def pe_group(pe, G, q, ahead):
            xg, bg, cg, zg = xg2[:, q], bg2[:, q], cg2[:, q], zg2[:, q]
            pe.wait_ge(feat_ready, G * 4 + 4)
            for c in range(CH + 1):
                last = c == CH
                m = P if not last else TS
                lo_, hi_ = c * P, c * P + m
                pe.wait_ge(a_free, G * 5 + c)
                pe.matmul(psA[0:m, 384:384 + m], bg[:, lo_:hi_], cg[:, lo_:hi_], start=True, stop=True)
                for j in range(2):
                    pe.transpose(psA[0:m, j * P:(j + 1) * P], xg[:, j, lo_:hi_], ident)
                pe.transpose(psA[0:m, 256:384], bg[:, lo_:hi_], ident).then_inc(a_full, 1)
                pe.wait_ge(rhs_ready, G * 5 + c + 1)
                if c == 0:
                    pe.wait_ge(gmean_ready, G)
                rv = rhs_a[0:m, :, 0:m]
                if c > 0:
                    pe.matmul(per_head(psE[:, 0:GH * m]), cst[0:m, CST["ones"][0]:CST["ones"][0] + P], rv, start=True, stop=True)
                pe.matmul(per_head(psL[0:m, 0:GH * m]), c_("after_p") if not last else c_("after_s", TS), rv,
                          start=True, stop=True).then_inc(le_full, 1)
                if ahead:
                    pe_dense(pe, tile_of(ahead(G), c), xn_hi, xn_lo)
                pe.wait_ge(m_ready, G * 5 + c + 1)
                pe.wait_ge(y_free, G * 5 + c)
                lv, ev = per_head(l_exp[0:m, 0:GH * m]), per_head(e_exp[:, 0:GH * m])
                if last:
                    pe.wait_ge(st_landed, G * 16 + 16)
                    for b in range(NB):
                        for j in range(2):
                            o = 2 * m + (b * 2 + j) * 16
                            pe.matmul(psY[:, o:o + 16].rearrange("p (h t) -> p h t", h=2),
                                      st_in[:, b, j * P:(j + 1) * P], ev[:, 2 * j:2 * j + 2, b * DT:(b + 1) * DT],
                                      start=True, stop=True)
                for h in range(GH):
                    o = psY[(h % 2) * 64:(h % 2) * 64 + 64, (h // 2) * m:(h // 2 + 1) * m]
                    carried = 0 < c < CH
                    mm = pe.matmul(o, xdt[0:m, h * 64:h * 64 + 64], lv[:, h, :], start=True, stop=not carried)
                    if carried:
                        pe.matmul(o, state[:, h * 64:h * 64 + 64], ev[:, h, :], start=False, stop=True)
                if not last:
                    pe.matmul(psY[:, 256:512], btok[:], xdtd[:], start=True, stop=True).then_inc(y_full, 1)
                else:
                    mm.then_inc(y_full, 1)
            for r in range(4):
                if r > 1:
                    pe.wait_ge(n_free, G * 4 + r - 1)
                bank = psL if r % 2 == 0 else psE
                for b in (2 * r, 2 * r + 1):
                    mm = pe.matmul(bank[:, (b % 2) * 256:(b % 2) * 256 + 256], bm[:, b, :], xdtd[0:TS, :],
                                   start=True, stop=True)
                mm.then_inc(n_full, 1)
            if ahead:
                pe_dense(pe, tile_of(ahead(G), 5), xn_hi, xn_lo)
            pe.wait_ge(n_free, G * 4 + 4)
            pe.wait_ge(gsq_ready, G + 1)
            for hf, bank in ((0, psL), (1, psE)):
                for j in range(2):
                    mm = pe.matmul(bank[:, 0:HALF], ones, zg[:, j, hf * HALF:(hf + 1) * HALF], start=(j == 0), stop=(j == 1))
            mm.then_inc(gsum_full, 1)

        def act_group(act, G, q, first_y, ahead):
            zg = zg2[:, q]
            for c in range(CH + 1):
                act.wait_ge(le_full, G * 5 + c + 1)
                m = P if c < CH else TS
                ins = act.activation(l_exp[0:m, 0:GH * m], psL[0:m, 0:GH * m], ACT.Exp)
                if c > 0:
                    ins = act.activation(e_exp[:, 0:GH * m], psE[:, 0:GH * m], ACT.Exp)
                ins.then_inc(exp_ready, 1)
                if c == 1:
                    act.wait_ge(ssm_out, G * 32)
                    act.dma_start(st_in[:], io["state_t"][bass.ds(G * P, P), :].rearrange("n (b q) -> n b q", b=NB)).then_inc(st_landed, 16)
                if ahead:
                    N = ahead(G)
                    if c < 4:
                        act_copy(act, N, c)
                    else:
                        act_z(act, N, 1 - q, 0)
                    if c >= 1:
                        act_tanh(act, N, c - 1)
            act.wait_ge(gate_ready, G + 1)
            for j in range(2):
                ins = act.activation(zg[:, j, :], yg[:, j, :], ACT.Square)
            ins.then_inc(gsq_ready, 1)
            if ahead:
                act_z(act, N, 1 - q, 1)
            act.wait_ge(gmean_ready, G + 1)
            act.activation(rstd[:], rstd[:], ACT.Sqrt).then_inc(groot_ready, 1)
            act.wait_ge(ssm_ready, G + 1)
            act.dma_start(io["ssm_s"][bass.ds(G * P, P), :].rearrange("n (b q) -> n b q", b=NB), st_in[:]).then_inc(ssm_out, 16)
            act.dma_start(io["ssm_p"][bass.ds(G * P, P), :], state[:]).then_inc(ssm_out, 16)
            for j in range(2):
                act.wait_ge(gt_ready, G * 2 + (j + 1))
                yh = cols(flat(y_hi), (G * 2 - first_y + j) * T, T)
                act.activation(yh, zg[:, j, :], ACT.Copy).then_inc(ghi_ready, 1)

        def dve_group(dve, link, G, q, first_y, ahead):
            xg, bg, cg, zg = xg2[:, q], bg2[:, q], cg2[:, q], zg2[:, q]
            N = ahead(G) if ahead else None
            for c in range(CH + 1):
                last = c == CH
                m = P if not last else TS
                lo_, hi_ = c * P, c * P + m
                up = c_("upto_p") if not last else c_("upto_s", TS)
                dve.wait_ge(a_full, G * 5 + c + 1)
                link(dve.tensor_tensor(per_head(xdt[0:m, :]), per_head(psA[0:m, 0:256]), spread(cols(dt_tok[0:m, 0, c, :], G * GH, GH), m, 64), ALU.mult))
                link(dve.tensor_copy(btok[0:m, :], psA[0:m, 256:384]))
                dve.tensor_tensor(cbm[0:m, 0:m], psA[0:m, 384:384 + m], up, ALU.mult).then_inc(a_free, 1)
                dve.wait_ge(a_free, G * 5 + c + 1)
                link(dve.tensor_tensor(per_head(xdtd[0:m, :]), per_head(xdt[0:m, :]), spread(cols(dec[0:m, c, :], G * GH, GH), m, 64), ALU.mult))
                if last:
                    link(dve.tensor_tensor(bm[:], btok[0:TS, :].rearrange("p (o n) -> p o n", o=1).to_broadcast([TS, NB, P]),
                                           c_("same_b", TS).rearrange("p (b o) -> p b o", o=1).to_broadcast([TS, NB, P]), ALU.mult))
                dve.wait_ge(exp_ready, G * 5 + c + 1)
                lv, ev = per_head(l_exp[0:m, 0:GH * m]), per_head(e_exp[:, 0:GH * m])
                ins = dve.tensor_tensor(lv, lv, over_heads(cbm[0:m, 0:m], m, m), ALU.mult)
                if c > 0:
                    ins = dve.tensor_tensor(ev, ev, over_heads(cg[:, lo_:hi_], P, m), ALU.mult)
                ins.then_inc(m_ready, 1)
                dve.wait_ge(m_ready, G * 5 + c + 1)
                if not last:
                    dve_rhs(dve, G, c + 1)
                if ahead and c >= 1:
                    dve_conv(dve, link, N, c - 1)
                if ahead and c >= 2:
                    dve_silu(dve, N, 1 - q, c - 2)
                dve.wait_ge(y_full, G * 5 + c + 1)
                for j in range(2):
                    dsk = cols(fea, G * 2 + (FEA["dskip"][0] + j))
                    link(dve.scalar_tensor_tensor(yg[:, j, lo_:hi_], xg[:, j, lo_:hi_], dsk, psY[:, j * m:(j + 1) * m], ALU.mult, ALU.add))
                if not last:
                    if c > 0:
                        link(dve.tensor_tensor(per_head(state[:]), per_head(state[:]), spread(cols(tot, G * GH + c * HEADS, GH), P, 64), ALU.mult))
                        ins = dve.tensor_tensor(state[:], state[:], psY[:, 256:512], ALU.add)
                    else:
                        dve.wait_ge(ssm_out, G * 32)
                        ins = dve.tensor_copy(state[:], psY[:, 256:512])
                    ins.then_inc(y_free, 1)
                    dve.wait_ge(y_free, G * 5 + c + 1)
            for hh in range(2):
                r0, r1 = hh * 64, hh * 64 + 64
                yv = yg[r0:r1, :, SEQ:T].rearrange("p q (b t) -> p b q t", b=NB)
                ov = psY[r0:r1, 128:384].rearrange("p (b q h t) -> p b q h t", b=NB, q=2, h=2)[:, :, :, hh, :]
                ins = dve.tensor_tensor(yv, yv, ov, ALU.add)
                if hh == 0:
                    link(ins)
            ins.then_inc(y_free, 1)
            dve.wait_ge(y_free, G * 5 + 5)
            dve.tensor_tensor(yg[:], yg[:], zg, ALU.mult).then_inc(gate_ready, 1)
            for b in range(NB):
                link(dve.tensor_tensor(per_head(st_in[:, b, :]), per_head(st_in[:, b, :]), spread(cols(tot, G * GH + (CH + b) * HEADS, GH), P, 64), ALU.mult))
            for r in range(4):
                bank = psL if r % 2 == 0 else psE
                dve.wait_ge(n_full, G * 4 + r + 1)
                sv = st_in[:, 2 * r:2 * r + 2, :].rearrange("p b q -> p (b q)")
                dve.tensor_tensor(sv, sv, bank, ALU.add).then_inc(n_free, 1)
            dve.wait_ge(n_free, G * 4 + 4)
            dve.sem_inc(ssm_ready, 1)
            if ahead:
                dve_silu(dve, N, 1 - q, 3)
                dve_z(dve, N, 1 - q, 0)
                dve_rhs(dve, N, 0)
            dve.wait_ge(gsum_full, G + 1)
            link(dve.tensor_scalar(rstd[:, 0:HALF], psL[:, 0:HALF], 1.0 / 1024, EPS, ALU.mult, ALU.add))
            dve.tensor_scalar(rstd[:, HALF:T], psE[:, 0:HALF], 1.0 / 1024, EPS, ALU.mult, ALU.add).then_inc(gmean_ready, 1)
            if ahead:
                dve_z(dve, N, 1 - q, 1)
            dve.wait_ge(groot_ready, G + 1)
            link(dve.reciprocal(rstd[:], rstd[:]))
            for j in range(2):
                dve.scalar_tensor_tensor(zg[:, j, :], yg[:, j, :], cols(fea, G * 2 + (FEA["ssdn"][0] + j)), rstd[:], ALU.mult, ALU.mult).then_inc(gt_ready, 1)
            for j in range(2):
                dve.wait_ge(ghi_ready, G * 2 + j + 1)
                off = (G * 2 - first_y + j) * T
                link(dve.tensor_tensor(cols(flat(y_lo), off, T), zg[:, j, :], cols(flat(y_hi), off, T).bitcast(F32), ALU.subtract))

        def pe_first(pe):
            for u in range(N_GRP):
                pe_dense(pe, tile_of(0, u), xn_hi, xn_lo)

        def act_first(act):
            for u in range(4):
                act_copy(act, 0, u)
                if u >= 1:
                    act_tanh(act, 0, u - 1)
            act_tanh(act, 0, 3)
            for j in range(2):
                act_z(act, 0, 0, j)

        def dve_first(dve):
            link = chains["dve"]
            for u in range(4):
                dve_conv(dve, link, 0, u)
                if u >= 1:
                    dve_silu(dve, 0, 0, u - 1)
            dve_silu(dve, 0, 0, 3)
            for j in range(2):
                dve_z(dve, 0, 0, j)
            dve_rhs(dve, 0, 0)

        nxt = lambda G: G + 1

        def pe_half0(pe):
            with pe.Fori(0, 2) as i:
                for q in range(2):
                    pe_group(pe, i * 2 + q, q, nxt)

        def act_half0(act):
            with act.Fori(0, 2) as i:
                for q in range(2):
                    act_group(act, i * 2 + q, q, 0, nxt)

        def dve_half0(dve):
            link = chains["dve"]
            with dve.Fori(0, 2) as i:
                link.enter(i, 2 * GROUP_LINKS)
                for q in range(2):
                    dve_group(dve, link, i * 2 + q, q, 0, nxt)
                link.leave(2)

        dve_prog.append(lambda dve: chains["dve"](dve.memset(cbuf[:, :, 0:PAD], 0.0)))
        pe_prog.append(pe_first); act_prog.append(act_first); dve_prog.append(dve_first)
        pe_prog.append(pe_half0); act_prog.append(act_half0); dve_prog.append(dve_half0)
        take(5 * N_GRP)
        edge("edge_ssd0")

        n0c = take(KT)

        def pe_c(pe):
            with pe.Fori(0, KT // 2) as i:
                for u in range(2):
                    pe_dense(pe, slot(n0c, u, i, 2), y_hi, y_lo)

        def act_c(act):
            with act.Fori(0, KT // 2) as i:
                for u in range(2):
                    par, k0 = slot(n0c, u, i, 2)
                    act.wait_ge(dense_full[par], k0 + 1)
                    act.activation(two(flat(merged)[:, bass.ds((i * 2 + u) * T, T)]),
                                   dps[:, par, :, 0:HALF], ACT.Copy).then_inc(dense_free[par], 1)
        pe_prog.append(pe_c); act_prog.append(act_c)
        edge("edge_out0")
        def half1(group):
            for G in range(4, GROUPS):
                group(G, G % 2, nxt if G < GROUPS - 1 else None)
        pe_prog.append(lambda pe: half1(lambda G, q, ahead: pe_group(pe, G, q, ahead)))
        act_prog.append(lambda act: half1(lambda G, q, ahead: act_group(act, G, q, KT, ahead)))
        dve_prog.append(lambda dve: half1(lambda G, q, ahead: dve_group(dve, chains["dve"], G, q, KT, ahead)))
        take(3 * N_GRP)


        def act_states_out(act):
            act.dma_start(io["tails"], flat(tails)).then_inc(out_done, 16)
            act.wait_ge(ssm_out, GROUPS * 32)
            act.wait_ge(out_done, 16)
        act_prog.append(act_states_out)
        edge("edge_ssd1")

        merged_done, merges = sem("merged_done"), [0]

        def merge_stage(name, first):
            st = ExitStack()
            gth = stage_sb(st, f"{name}_gth", [P, 2, T])
            tmp = stage_sb(st, f"{name}_tmp", [P, 2, T])
            st.close()
            n0 = take(2 * KT)
            before = merges[0] * KT
            merges[0] += 1

            def pe_f(pe):
                with pe.Fori(0, KT // 2) as i:
                    for u in range(4):
                        gate = u % 2 == 0
                        pe_dense(pe, slot(n0, u, i, 4), xn_hi if gate else y_hi, xn_lo if gate else y_lo)

            def act_f(act):
                with act.Fori(0, KT // 2) as i:
                    for u in (0, 2):
                        par, k0 = slot(n0, u, i, 4)
                        act.wait_ge(merged_done, i * 2 + before)
                        act.wait_ge(dense_full[par], k0 + 1)
                        act.activation(two(gth[:, u // 2, :]), dps[:, par, :, 0:HALF], ACT.Tanh, scale=0.5).then_inc(dense_free[par], 1)

            def dve_f(dve):
                link = chains["dve"]
                with dve.Fori(0, KT // 2) as i:
                    link.enter(i, 2)
                    for j in range(2):
                        gp, gk = slot(n0, 2 * j, i, 4)
                        par, k0 = slot(n0, 2 * j + 1, i, 4)
                        mv = merged[:].rearrange("p k t -> p (k t)")[:, bass.ds((i * 2 + j) * T, T)]
                        dve.wait_ge(dense_free[gp], gk + 1)
                        dve.wait_ge(dense_full[par], k0 + 1)
                        ps = dps[:, par, :, 0:HALF]
                        if first:
                            dve.tensor_tensor(two(tmp[:, j, :]), two(mv), ps, ALU.add).then_inc(dense_free[par], 1)
                            dve.wait_ge(dense_free[par], k0 + 1)
                            dve.scalar_tensor_tensor(mv, gth[:, j, :], 1.0, tmp[:, j, :], ALU.add, ALU.mult).then_inc(merged_done, 1)
                            link(dve.memset(pad1[:], 0.0))
                        else:
                            dve.scalar_tensor_tensor(two(tmp[:, j, :]), two(gth[:, j, :]), 1.0, ps, ALU.add, ALU.mult).then_inc(dense_free[par], 1)
                            dve.wait_ge(dense_free[par], k0 + 1)
                            link(dve.tensor_tensor(mv, mv, tmp[:, j, :], ALU.add))
                            dve.sem_inc(merged_done, 1)
                link.leave(KT // 2)
            pe_prog.append(pe_f); act_prog.append(act_f); dve_prog.append(dve_f)

        merge_stage("m0", True)
        edge("edge_m0")

        att = ExitStack()
        as_ = lambda n, s, d=F32: stage_sb(att, n, s, d)
        ks = as_("ks", [P, 2, T])
        v_new = as_("v_new", [TS, 256])
        qbd = as_("qbd", [P, 2, NB, P])
        ys = as_("ys", [64, 16, TS])
        pro = ExitStack()
        ps_ = lambda n, s, d=F32: stage_sb(pro, n, s, d)
        ksw = ps_("ksw", [P, 2, T])
        v_tok = ps_("v_tok", [P, CH, 256])
        raw, ropet = ps_("raw", [P, T]), ps_("ropet", [P, T])
        keys_only = ExitStack()
        vs = stage_sb(keys_only, "vs", [P, 2, T])
        keys_only.close()
        qk2 = ps_("qk", [P, 2, T])
        kcur2 = ps_("kcur", [P, 2, SEQ])
        vcur2 = ps_("vcur", [P, 2, CH, 64])
        prob = ps_("prob", [P, 4, SEQ])
        prob_t = ps_("prob_t", [P, CH, SEQ])
        nmax, psum_, prec = ps_("nmax", [P, 4]), ps_("psum_", [P, 4]), ps_("prec", [P, 4])
        pro.close()

        raw_ready, rot_full, rope_done = sem("raw_ready"), sem("rot_full"), sem("rope_done")
        sw_full, sw_copied = sem("sw_full"), sem("sw_copied")
        vt_full, vt_copied = sem("vt_full"), sem("vt_copied")
        kv_out = sem("kv_out")
        n_kv = take(4)

        def rope(dve, link, dst, n_done, n_rot, banks=psLE):
            dve.wait_ge(rot_full, n_rot)
            dve.tensor_tensor(two(ropet[:]), two(c_("sin")), banks[:, :, 0:HALF], ALU.mult)
            link(dve.tensor_tensor(dst, raw[:], c_("cos"), ALU.mult))
            dve.tensor_tensor(dst, dst, ropet[:], ALU.add).then_inc(rope_done, 1)
            dve.wait_ge(rope_done, n_done)

        def pe_rot(pe, src, mat, done, banks=psLE):
            for b in range(2):
                mm = pe.matmul(banks[:, b, 0:HALF], mat, src[:, b * HALF:(b + 1) * HALF], start=True, stop=True)
            mm.then_inc(done, 1)

        def pe_kv(pe):
            for u in range(2):
                pe_dense(pe, slot(n_kv, u), xn_hi, xn_lo)
            for j in range(2):
                pe.wait_ge(raw_ready, j + 1)
                pe_rot(pe, raw, c_("rot"), rot_full)
                pe.wait_ge(rope_done, j + 1)
            for u in range(2, 4):
                pe_dense(pe, slot(n_kv, u), xn_hi, xn_lo)
            for j in range(2):
                if j:
                    pe.wait_ge(sw_copied, 1)
                pe_rot(pe, ks[:, j, :], c_("swap"), sw_full)
            par, k0 = slot(n_kv, 3)
            pe.wait_ge(dense_free[par], k0 + 1)
            for c in range(CH):
                bank = psA if c < 2 else psY
                for j in range(2):
                    mm = pe.transpose(bank[:, (c % 2) * 256 + j * P:(c % 2) * 256 + (j + 1) * P], vs[:, j, c * P:(c + 1) * P], ident)
            mm.then_inc(vt_full, 1)
            pe.wait_ge(vt_copied, 1)
            for j in range(2):
                mm = pe.transpose(psA[0:TS, j * P:(j + 1) * P], vs[:, j, SEQ:T], ident)
            mm.then_inc(vt_full, 1)

        def act_kv(act):
            for u in range(4):
                par, k0 = slot(n_kv, u)
                act.wait_ge(dense_full[par], k0 + 1)
                if u == 0:
                    act.activation(two(raw[:]), dps[:, par, :, 0:HALF], ACT.Copy).then_inc(dense_free[par], 1)
                    act.wait_ge(dense_free[par], k0 + 1)
                    act.sem_inc(raw_ready, 1)
                elif u == 1:
                    act.wait_ge(rope_done, 1)
                    act.activation(two(raw[:]), dps[:, par, :, 0:HALF], ACT.Copy).then_inc(dense_free[par], 1)
                    act.wait_ge(dense_free[par], k0 + 1)
                    act.sem_inc(raw_ready, 1)
                else:
                    act.activation(two(vs[:, u - 2, :]), dps[:, par, :, 0:HALF], ACT.Copy).then_inc(dense_free[par], 1)
            act.wait_ge(dense_free[par], k0 + 1)
            act.dma_start(io["kv_t"][:, 2:4, :], vs[:]).then_inc(kv_out, 16)
            for j in range(2):
                act.wait_ge(sw_full, j + 1)
                act.activation(two(ksw[:, j, :]), psLE[:, :, 0:HALF], ACT.Copy).then_inc(sw_copied, 1)
            act.wait_ge(rope_done, 2)
            act.dma_start(io["kv_t"][:, 0:2, :], ks[:]).then_inc(kv_out, 16)
            act.wait_ge(kv_out, 32)

        def dve_kv(dve):
            link = chains["dve"]
            dve.memset(qbd[:], 0.0)
            for j in range(2):
                dve.wait_ge(raw_ready, j + 1)
                rope(dve, link, ks[:, j, :], j + 1, j + 1)
            dve.wait_ge(vt_full, 1)
            dve.tensor_copy(v_tok[:, 0:2, :], psA[:].rearrange("p (c f) -> p c f", c=2))
            dve.tensor_copy(v_tok[:, 2:4, :], psY[:].rearrange("p (c f) -> p c f", c=2)).then_inc(vt_copied, 1)
            dve.wait_ge(vt_full, 2)
            dve.tensor_copy(v_new[:], psA[0:TS, 0:256]).then_inc(vt_copied, 1)
        pe_prog.append(pe_kv); act_prog.append(act_kv); dve_prog.append(dve_kv)
        edge("edge_kv")

        n_q = take(KT)
        s_full, s_max, s_exp, p_norm = sem("s_full"), sem("s_max"), sem("s_exp"), sem("p_norm")
        t_full, t_copied, pv_full = sem("t_full"), sem("t_copied"), sem("pv_full")
        yhi_ready, ylo_ready, qsw_full, qbd_done, kv_cur = sem("yhi_ready"), sem("ylo_ready"), sem("qsw_full"), sem("qbd_done"), sem("kv_cur")

        ROUNDS, LOOK = 2 * CH, 3

        def q_bank(tt, r):
            par, _ = slot(n_q, tt)
            return (psL, psE, dps[:, par, 0, :], dps[:, par, 1, :])[r % 4]

        def pe_prep(pe, j, tt, step):
            par, _ = slot(n_q, tt)
            t = j * 4 + tt
            if step == "project":
                pe_dense(pe, slot(n_q, tt, j, 4), xn_hi, xn_lo)
            if step == "rotate":
                pe.wait_ge(raw_ready, t + 3)
                pe_rot(pe, raw, c_("rot"), rot_full, dps[:, par])
            if step == "swap":
                pe.wait_ge(rope_done, t + 3)
                pe.matmul(dps[:, par, 0, 0:TS], c_("swap"), qk2[:, tt % 2, SEQ:T], start=True, stop=True).then_inc(qsw_full, 1)

        def pe_scores_q(pe, t, tt, r):
            hh, i = r // CH, r % CH
            qk, kcur = qk2[:, tt % 2, :], kcur2[:, tt // 2, :]
            pe.wait_ge(s_exp, t * 8 + (r + 1))
            rows = slice(hh * 64, hh * 64 + 64)
            bank = q_bank(tt, r)
            pe.matmul(bank[:, 0:(i + 1) * P], qk[rows, i * P:(i + 1) * P], kcur[rows, 0:(i + 1) * P], start=True, stop=False)
            pe.matmul(bank[:, i * P:(i + 1) * P], ident, c_("causal"), start=False, stop=True).then_inc(s_full, 1)

        def pe_products_q(pe, t, tt, hh):
            pe.wait_ge(t_copied, t * 8 + (hh * CH + CH))
            if hh == 0:
                pe.wait_ge(ylo_ready, t)
            for kt in range(CH):
                mm = pe.matmul(psY[hh * 64:hh * 64 + 64, kt * P:SEQ], vcur2[:, tt // 2, kt, :], prob_t[:, kt, kt * P:SEQ],
                               start=(kt == 0), stop=(kt == CH - 1))
            mm.then_inc(pv_full, 1)

        def pe_q(pe):
            with pe.Fori(0, 2) as j:
                for step in ("project", "rotate", "swap"):
                    pe_prep(pe, j, 0, step)
                for tt in range(4):
                    t = j * 4 + tt
                    pe.wait_ge(qbd_done, t + 1)
                    if tt % 2 == 0:
                        pe.wait_ge(kv_cur, j * 2 + (tt // 2 + 1))
                    for r in range(LOOK):
                        pe_scores_q(pe, t, tt, r)
                    if tt:
                        pe_products_q(pe, j * 4 + (tt - 1), tt - 1, 1)
                    for r in range(ROUNDS):
                        if r + LOOK < ROUNDS:
                            pe_scores_q(pe, t, tt, r + LOOK)
                        pe.wait_ge(p_norm, t * 8 + (r + 1))
                        pe.wait_ge(t_copied, t * 8 + r)
                        for kt in range(r % CH + 1):
                            mm = pe.transpose(psA[:, kt * P:(kt + 1) * P], prob[:, r % 4, kt * P:(kt + 1) * P], ident)
                        mm.then_inc(t_full, 1)
                        if r == CH:
                            pe_products_q(pe, t, tt, 0)
                        if tt < 3 and r in (1, 3, 6):
                            pe_prep(pe, j, tt + 1, {1: "project", 3: "rotate", 6: "swap"}[r])
                pe_products_q(pe, j * 4 + 3, 3, 1)

        def act_prep(act, j, tt):
            t = j * 4 + tt
            par, k0 = slot(n_q, tt, j, 4)
            act.wait_ge(dense_full[par], k0 + 1)
            act.wait_ge(rope_done, t + 2)
            act.activation(two(raw[:]), dps[:, par, :, 0:HALF], ACT.Copy, scale=0.125).then_inc(dense_free[par], 1)
            act.wait_ge(dense_free[par], k0 + 1)
            act.sem_inc(raw_ready, 1)
            if tt % 2 == 0:
                g = tt // 2
                act.wait_ge(pv_full, j * 8)
                for hf in range(2):
                    rows = slice(hf * 64, hf * 64 + 64)
                    act.activation(kcur2[rows, g, :], flat(ks if hf == g else ksw)[rows, bass.ds(j * T, SEQ)], ACT.Copy)
                act.activation(vcur2[:, g], v_tok[:, :, bass.ds(j * P + g * 64, 64)], ACT.Copy).then_inc(kv_cur, 1)

        def act_exp_q(act, t, tt, r):
            w = (r % CH + 1) * P
            act.wait_ge(s_max, t * 8 + (r + 1))
            act.activation(prob[:, r % 4, 0:w], q_bank(tt, r)[:, 0:w], ACT.Exp, bias=nmax[:, r % 4:r % 4 + 1],
                           accum_out=psum_[:, r % 4:r % 4 + 1]).then_inc(s_exp, 1)

        def act_y_q(act, t):
            act.wait_ge(pv_full, t * 2 + 2)
            act.activation(cols(flat(y_hi), t * T, SEQ), psY[:], ACT.Copy).then_inc(yhi_ready, 1)

        def act_q(act):
            act.sem_inc(s_exp, 4)
            with act.Fori(0, 2) as j:
                act_prep(act, j, 0)
                for tt in range(4):
                    t = j * 4 + tt
                    for r in range(LOOK):
                        act_exp_q(act, t, tt, r)
                    if tt:
                        act_y_q(act, j * 4 + (tt - 1))
                    for r in range(ROUNDS):
                        i = r % CH
                        if r + LOOK < ROUNDS:
                            act_exp_q(act, t, tt, r + LOOK)
                        act.wait_ge(t_full, t * 8 + (r + 1))
                        if i == 0:
                            act.wait_ge(pv_full, t * 2 + r // CH)
                        act.activation(prob_t[:, 0:i + 1, i * P:(i + 1) * P], psA[:, 0:(i + 1) * P].rearrange("p (k q) -> p k q", q=P),
                                       ACT.Copy).then_inc(t_copied, 1)
                        if tt < 3 and r == 2:
                            act_prep(act, j, tt + 1)
                act_y_q(act, j * 4 + 3)

        def dve_queries_q(dve, link, j, tt):
            t = j * 4 + tt
            rope(dve, link, qk2[:, tt % 2, :], t + 3, t + 3, dps[:, slot(n_q, tt)[0]])

        def dve_sample_q(dve, j, tt):
            t = j * 4 + tt
            g, r0 = tt // 2, (tt % 2) * 2
            par, _ = slot(n_q, tt)
            dve.wait_ge(qsw_full, t + 1)
            rows = slice(g * 64, g * 64 + 64)
            for hf in range(2):
                src = qk2[rows, tt % 2, SEQ:T] if hf == g else dps[rows, par, 0, 0:TS]
                col = g * 32 + (r0 + hf) * DT
                ap = qbd[rows, bass.ds(j, 1), :, bass.ds(j * 64 + col, DT)].rearrange("p o b c -> p (o b) c")
                ins = dve.tensor_copy(ap, by_seq(src))
            ins.then_inc(qbd_done, 1)

        def dve_max_q(dve, t, tt, r):
            dve.wait_ge(s_full, t * 8 + (r + 1))
            dve.wait_ge(s_exp, t * 8 + (r + 1))
            dve.tensor_reduce(nmax[:, r % 4:r % 4 + 1], q_bank(tt, r)[:, 0:(r % CH + 1) * P], AX, ALU.max, negate=True).then_inc(s_max, 1)

        def dve_y_q(dve, t):
            dve.wait_ge(yhi_ready, t + 1)
            dve.tensor_tensor(cols(flat(y_lo), t * T, SEQ), psY[:], cols(flat(y_hi), t * T, SEQ).bitcast(F32), ALU.subtract).then_inc(ylo_ready, 1)
            dve.wait_ge(ylo_ready, t + 1)

        def dve_q(dve):
            link = chains["dve"]
            with dve.Fori(0, 2) as j:
                link.enter(j, PER_Q)
                dve_queries_q(dve, link, j, 0)
                dve_sample_q(dve, j, 0)
                for tt in range(4):
                    t = j * 4 + tt
                    for r in range(LOOK):
                        dve_max_q(dve, t, tt, r)
                    for r in range(ROUNDS):
                        if r + LOOK < ROUNDS:
                            dve_max_q(dve, t, tt, r + LOOK)
                        w = (r % CH + 1) * P
                        dve.wait_ge(s_exp, t * 8 + (r + 5))
                        link(dve.reciprocal(prec[:, r % 4:r % 4 + 1], psum_[:, r % 4:r % 4 + 1]))
                        dve.tensor_scalar(prob[:, r % 4, 0:w], prob[:, r % 4, 0:w], prec[:, r % 4:r % 4 + 1], None, ALU.mult).then_inc(p_norm, 1)
                        if tt and r == 0:
                            dve_y_q(dve, j * 4 + (tt - 1))
                        if tt < 3 and r == 4:
                            dve_queries_q(dve, link, j, tt + 1)
                        if tt < 3 and r == 6:
                            dve_sample_q(dve, j, tt + 1)
                dve_y_q(dve, j * 4 + 3)
            link.leave(2)

        PER_Q = 36
        pe_prog.append(pe_q); act_prog.append(act_q); dve_prog.append(dve_q)
        edge("edge_q")

        n_pages_at = nstream[0]
        sam = ExitStack()
        sa = lambda n, s, d=F32: stage_sb(sam, n, s, d)
        ptab = sa("ptab", [1, NB * NPG], mybir.dt.int32)
        kpg = sa("kpg", [P, 2, 4, 256])
        vpg = sa("vpg", [P, 4, 4, 256])
        sc = sa("sc", [P, 2, PAST + TS])
        pt_s = sa("pt_s", [P, NPG, P])
        pt_own = sa("pt_own", [TS, P])
        qb = sa("qb", [P, 2, P])
        gs, bmx, cmp1, cmp2 = sa("gs", [P, 8]), sa("bmx", [P, 9]), sa("cmp1", [P, 8, 8]), sa("cmp2", [P, 8, 8])
        rank, bias, nm, ssum = sa("rank", [P, 8]), sa("bias", [P, 9]), sa("nm", [P, 1]), sa("ssum", [P, 9])
        yf = pt_s[:, 0:CH, :].rearrange("p c (k t) -> p (c k) t", k=2)
        yo = sa("yo", [P, 64])
        sam.close(); att.close()
        k_landed, v_landed = ([sem(f"{k}_landed{slot_}") for slot_ in range(n)] for k, n in (("k", 2), ("v", 4)))
        pt_in, b_qb, b_s, b_sc, b_own, b_bias, b_exp, b_norm = (sem(f"b_{k}") for k in ("pt", "qb", "s", "sc", "own", "bias", "exp", "norm"))
        b_t, b_tc, b_pv, b_yo, b_vused, b_yt, b_ys = (sem(f"b_{k}") for k in ("t", "tc", "pv", "yo", "vused", "yt", "ys"))
        sw_s, sw_y = sem("sw_s"), sem("sw_y")
        sam_start = sem("sam_start")

        def load_pages(dma, b, c, buf, src, landed, used, count):
            _, pages = nc.values_load_multi_w_load_instructions(ptab[0:1, bass.ds(b * NPG + c * 4, 4)], engines=(dma.engine,),
                                                                min_val=0, max_val=src.shape[0] - 1)
            dma.wait_ge(used, count)
            for k in range(4):
                dma.dma_start(buf[:, c % len(landed), k, :], src[bass.ds(pages[k], 1), :, :].rearrange("o p f -> (o p) f")).then_inc(landed[c % len(landed)], 16)

        def sp_keys(sp):
            sp.wait_ge(sam_start, 1)
            sp.dma_start(ptab[:], io["page_table"]).then_inc(pt_in, 16)
            sp.wait_ge(pt_in, 16)
            with sp.Fori(0, NB) as b:
                for c in range(4):
                    load_pages(sp, b, c, kpg, io["k_pages"], k_landed, b_s, b * 5 + (c - 1 if c >= 2 else 0))

        def pool_values(pool):
            pool.wait_ge(pt_in, 16)
            with pool.Fori(0, NB) as b:
                for c in range(4):
                    load_pages(pool, b, c, vpg, io["v_pages"], v_landed, b_vused, b * 4 + (c + 1))

        sp_pages = [sp_keys ]

        own_sc = dps[:, 1, 1, 0:TS]

        def pe_scores(pe, b, c):
            if c == CHUNKS:
                pe.wait_ge(b_own, b)
                for m in range(2):
                    mm = pe.matmul(own_sc, qb[:, m, :], ks[:, m, SEQ:T], start=(m == 0), stop=(m == 1))
                mm.then_inc(b_s, 1)
                return
            if c == 0:
                pe.wait_ge(b_qb, b + 1)
            pe.wait_ge(k_landed[c % 2], b * 128 + (c // 2 + 1) * 64)
            pe.wait_ge(b_sc, b * 4 + (c - 1 if c >= 2 else 0))
            for m in range(2):
                mm = pe.matmul(psLE[:, c % 2, :].rearrange("p (k t) -> p k t", k=4), qb[:, m, :],
                               kpg[:, c % 2, :, m * P:(m + 1) * P], start=(m == 0), stop=(m == 1))
            mm.then_inc(b_s, 1)

        def pe_turn(pe, b, q, c):
            if c == CHUNKS:
                pe.wait_ge(b_tc, b * 5 + 3)
                pe.matmul(psA[0:TS, 0:P], sc[:, q, PAST:], ident, start=True, stop=True).then_inc(b_t, 1)
                return
            if c == 0:
                pe.wait_ge(b_norm, b + 1)
            pe.wait_ge(b_tc, b * 5 + (c - 1 if c >= 2 else 0))
            bank = psA if c % 2 == 0 else psY
            for k in range(4):
                mm = pe.transpose(bank[:, k * P:(k + 1) * P], sc[:, q, (c * 4 + k) * P:(c * 4 + k + 1) * P], ident)
            mm.then_inc(b_t, 1)

        def pe_values(pe, b, c):
            out = dps[:, 0, 0, 0:256]
            pe.wait_ge(b_tc, b * 5 + (c + 1))
            if c == CHUNKS:
                pe.matmul(out, pt_own[:], v_new[:], start=False, stop=True).then_inc(b_pv, 1)
                return
            if c == 0:
                pe.wait_ge(b_yo, b)
            pe.wait_ge(v_landed[c], b * 64 + 64)
            for k in range(4):
                mm = pe.matmul(out, pt_s[:, c * 4 + k, :], vpg[:, c, k, :], start=(c == 0 and k == 0), stop=False)
            mm.then_inc(b_vused, 1)

        CHUNKS = NPG // 4
        out_t = dps[0:64, 1, 0, 0:P]

        def pe_out(pe, b):
            pe.wait_ge(b_yo, b + 1)
            pe.matmul(out_t, yo[:], ident, start=True, stop=True).then_inc(b_yt, 1)

        def pe_both(pe, b, q, ahead=True, first=False):
            for step in range(CHUNKS + 3):
                if step == 1 and not first:
                    pe_out(pe, b - 1)
                if ahead and step <= CHUNKS:
                    pe_scores(pe, b + 1, step)
                if 1 <= step <= CHUNKS + 1:
                    pe_turn(pe, b, q, step - 1)
                if step >= 2:
                    pe_values(pe, b, step - 2)

        def act_scores(act, b, q, c):
            act.wait_ge(b_s, b * 5 + (c + 1))
            act.activation(sc[:, q, c * 512:(c + 1) * 512], psLE[:, c % 2, :], ACT.Copy).then_inc(b_sc, 1)

        def act_exp(act, b, q):
            act.wait_ge(b_bias, b + 1)
            for n in range(8):
                act.activation(sc[:, q, n * 256:(n + 1) * 256], sc[:, q, n * 256:(n + 1) * 256], ACT.Exp, bias=bias[:, n:n + 1],
                               accum_out=ssum[:, n:n + 1])
            act.activation(sc[:, q, PAST:], sc[:, q, PAST:], ACT.Exp, bias=nm[:, 0:1], accum_out=ssum[:, 8:9]).then_inc(b_exp, 1)

        def act_values(act, b, c):
            if c == 0:
                act.wait_ge(b_pv, b)
            act.wait_ge(b_t, b * 5 + (c + 1))
            if c < CHUNKS:
                bank = psA if c % 2 == 0 else psY
                act.activation(pt_s[:, 4 * c:4 * c + 4, :], bank[:].rearrange("p (k r) -> p k r", k=4), ACT.Copy).then_inc(b_tc, 1)
                return
            act.activation(pt_own[:], psA[0:TS, 0:P], ACT.Copy).then_inc(b_tc, 1)

        def act_both(act, b, q, ahead=True):
            act_exp(act, b, q)
            for step in range(CHUNKS + 2):
                if ahead and step < CHUNKS:
                    act_scores(act, b + 1, 1 - q, step)
                if step >= 1:
                    act_values(act, b, step - 1)

        def dve_queries(dve, b):
            dve.tensor_copy(qb[:], qbd[:].rearrange("p m b c -> p m (b c)")[:, :, bass.ds(b * P, P)]).then_inc(b_qb, 1)

        def dve_scores(dve, link, b, q):
            for c in range(4):
                dve.wait_ge(b_sc, b * 4 + (c + 1))
                blk = sc[:, q, c * 512:(c + 1) * 512].rearrange("p (n k) -> p n k", n=2)
                link(dve.tensor_reduce(gs[:, 2 * c:2 * c + 2], blk, AX, ALU.add))
                link(dve.tensor_reduce(bmx[:, 2 * c:2 * c + 2], blk, AX, ALU.max))
            dve.wait_ge(b_s, b * 5 + 5)
            mask = cols(cst, CST["own"][0] + (TS - DT) - b * DT, TS)
            dve.tensor_tensor(sc[:, q, PAST:], own_sc, mask, ALU.add).then_inc(b_own, 1)
            dve.wait_ge(b_own, b + 1)
            link(dve.tensor_reduce(bmx[:, 8:9], sc[:, q, PAST:], AX, ALU.max))
            gm = gs[:].rearrange("p (o m) -> p o m", o=1).to_broadcast([P, 8, 8])
            gn = gs[:].rearrange("p (n o) -> p n o", o=1).to_broadcast([P, 8, 8])
            link(dve.tensor_tensor(cmp1[:], gm, gn, ALU.is_gt))
            link(dve.tensor_tensor(cmp2[:], gm, gn, ALU.is_equal))
            link(dve.tensor_tensor(cmp2[:], cmp2[:], c_("blk_lt").rearrange("p (n m) -> p n m", n=8), ALU.mult))
            link(dve.tensor_tensor(cmp1[:], cmp1[:], cmp2[:], ALU.add))
            link(dve.tensor_reduce(rank[:], cmp1[:], AX, ALU.add))
            link(dve.tensor_scalar(bias[:, 0:8], rank[:], 3.0, NEG, ALU.is_ge, ALU.mult))
            link(dve.tensor_tensor(bmx[:, 0:8], bmx[:, 0:8], bias[:, 0:8], ALU.add))
            link(dve.tensor_reduce(nm[:], bmx[:], AX, ALU.max, negate=True))
            dve.tensor_scalar(bias[:, 0:8], bias[:, 0:8], nm[:, 0:1], None, ALU.add).then_inc(b_bias, 1)

        def dve_norm(dve, link, b, q):
            dve.wait_ge(b_exp, b + 1)
            link(dve.tensor_reduce(rank[:, 0:1], ssum[:], AX, ALU.add))
            link(dve.reciprocal(rank[:, 1:2], rank[:, 0:1]))
            dve.tensor_scalar(sc[:, q, :], sc[:, q, :], rank[:, 1:2], None, ALU.mult).then_inc(b_norm, 1)

        def dve_values(dve, b):
            dve.wait_ge(b_pv, b + 1)
            for g in range(4):
                rows = slice(g * 32, g * 32 + 32)
                ins = dve.tensor_copy(yo[rows, :], dps[rows, 0, 0, g * 64:g * 64 + 64])
            ins.then_inc(b_yo, 1)

        def dve_out(dve, b):
            dve.wait_ge(b_yt, b + 1)
            dve.tensor_copy(ys[:, :, bass.ds(b * DT, DT)], out_t.rearrange("p (h t) -> p h t", h=16)).then_inc(b_ys, 1)

        SCORE_LINKS, NORM_LINKS = 17, 2

        def pe_s(pe):
            pe.sem_inc(b_vused, 4)
            for c in range(CHUNKS + 1):
                pe_scores(pe, 0, c)
            pe_both(pe, 0, 0, first=True)
            with pe.Fori(0, NB // 2 - 1) as i:
                for q in (1, 0):
                    pe_both(pe, i * 2 + (2 - q), q)
            pe_both(pe, NB - 1, 1, ahead=False)
            pe_out(pe, NB - 1)
            pe.wait_ge(b_ys, NB)
            pe.matmul(per_tile(psL), c_("swap", 64), ys[:].rearrange("p (k s) t -> p k s t", s=2)[:, :, 1, :],
                      start=True, stop=True).then_inc(sw_s, 1)

        def per_tile(bank):
            return bank.rearrange("p (k t) -> p k t", k=KT)

        def act_s(act):
            act.sem_inc(sam_start, 1)
            for c in range(CHUNKS):
                act_scores(act, 0, 0, c)
            act_both(act, 0, 0)
            with act.Fori(0, NB // 2 - 1) as i:
                for q in (1, 0):
                    act_both(act, i * 2 + (2 - q), q)
            act_both(act, NB - 1, 1, ahead=False)
            act.wait_ge(sw_y, 1)
            act.activation(y_hi[:, :, SEQ:T], yf, ACT.Copy).then_inc(yhi_ready, 1)

        def dve_s(dve):
            link = chains["dve"]
            dve_queries(dve, 0)
            dve_scores(dve, link, 0, 0)
            dve_queries(dve, 1)
            dve_norm(dve, link, 0, 0)
            dve_scores(dve, link, 1, 1)
            dve_values(dve, 0)
            with dve.Fori(0, NB // 2 - 1) as i:
                link.enter(i, 2 * (SCORE_LINKS + NORM_LINKS))
                for q in (1, 0):
                    b = i * 2 + (2 - q)
                    dve_queries(dve, b + 1)
                    dve_norm(dve, link, b, q)
                    dve_out(dve, b - 1)
                    dve_scores(dve, link, b + 1, 1 - q)
                    dve_values(dve, b)
                link.leave(NB // 2 - 1)
            dve_norm(dve, link, NB - 1, 1)
            dve_out(dve, NB - 2)
            dve_values(dve, NB - 1)
            dve_out(dve, NB - 1)
            dve.wait_ge(b_ys, NB)
            dve.wait_ge(sw_s, 1)
            dve.tensor_copy(yf[0:64], ys[:].rearrange("p (k s) t -> p k s t", s=2)[:, :, 0, :])
            dve.tensor_copy(yf[64:P], per_tile(psL)[64:P]).then_inc(sw_y, 1)
            dve.wait_ge(sw_y, 1)
            dve.wait_ge(yhi_ready, KT + 1)
            link(dve.tensor_tensor(y_lo[:, :, SEQ:T], yf, y_hi[:, :, SEQ:T].bitcast(F32), ALU.subtract))
        pe_prog.append(pe_s); act_prog.append(act_s); dve_prog.append(dve_s)
        edge("edge_s")
        merge_stage("m1", False)
        edge("edge_m1")

        mm_ = ExitStack()
        ms = lambda n, s, d=F32: stage_sb(mm_, n, s, d)
        km = ms("km", [P, KT, MEM])
        vm = ms("vm", [P, 2, D])
        mk = ExitStack()
        memx = stage_sb(mk, "memx", [P, KT, MEM])
        vmt = stage_sb(mk, "vmt", [P, KT, MEM])
        mem_in, memkv_out = sem("mem_in"), sem("memkv_out")
        act_prog.append(lambda act: act.dma_start(memx[:], io["mem_t"]).then_inc(mem_in, 16))
        norm_stage("normm", memx, "memn", y_hi, y_lo, width=MEM, ready=((mem_in, 16),))
        mk.close()
        edge("edge_normm")
        n_mem = take(2 * KT)
        vmt_full, vmt_copied = sem("vmt_full"), sem("vmt_copied")

        def pe_mem(pe):
            with pe.Fori(0, KT) as i:
                for u in range(2):
                    pe_dense(pe, slot(n_mem, u, i, 2), y_hi, y_lo, width=MEM)
            for par in range(2):
                pe.wait_ge(dense_free[par], (n_mem + 2 * KT) // 2 if (n_mem % 2 == 0) else (n_mem + 2 * KT + 1 - par) // 2)
            for kt in range(2):
                for j in range(KT):
                    r = kt * 2 + j // 4
                    if j % 4 == 0 and r >= 2:
                        pe.wait_ge(vmt_copied, r - 1)
                    bank = psA if r % 2 == 0 else psY
                    mm = pe.transpose(bank[:, (j % 4) * P:(j % 4 + 1) * P], vmt[:, j, kt * P:(kt + 1) * P], ident)
                    if j % 4 == 3:
                        mm.then_inc(vmt_full, 1)

        def act_mem(act):
            for dst in (km, vmt):
                base = n_mem if dst is km else n_mem + KT
                with act.Fori(0, KT // 2) as i:
                    for u in range(2):
                        par, k0 = slot(base, u, i, 2)
                        act.wait_ge(dense_full[par], k0 + 1)
                        act.activation(dst[:].rearrange("p k t -> p (k t)")[:, bass.ds((i * 2 + u) * MEM, MEM)],
                                       dps[:, par, 0, 0:MEM], ACT.Copy).then_inc(dense_free[par], 1)
            for par in range(2):
                act.wait_ge(dense_free[par], (n_mem + 2 * KT + 1 - par) // 2)
            act.dma_start(io["memkv_t"][:, 0:KT, :], km[:]).then_inc(memkv_out, 16)
            act.dma_start(io["memkv_t"][:, KT:2 * KT, :], vmt[:]).then_inc(memkv_out, 16)
            act.wait_ge(memkv_out, 32)

        def dve_mem(dve):
            for r in range(4):
                dve.wait_ge(vmt_full, r + 1)
                bank = psA if r % 2 == 0 else psY
                dve.tensor_copy(vm[:, r // 2, (r % 2) * 512:(r % 2) * 512 + 512], bank[:]).then_inc(vmt_copied, 1)
        pe_prog.append(pe_mem); act_prog.append(act_mem); dve_prog.append(dve_mem)
        edge("edge_mem")

        mh = ExitStack()
        ms2 = lambda n, s, d=F32: stage_sb(mh, n, s, d)
        kc = ms2("kc", [P, NB, 2, MEM])
        vc = ms2("vc", [P, NB, 2, MEM])
        qh2 = ms2("qh", [P, 2, 2, T])
        vh = ms2("vh", [P, 2, MEM])
        mp = ms2("mp", [P, 3, MEM])
        mpt = ms2("mpt", [P, 2, SEQ])
        apart = ms2("apart", [P, 2, NB * (TS + DT)])
        mo = ms2("mo", [TS, MEM])
        mfix = ms2("mfix", [P, 2, TS])
        mnm, msum, mrc = ms2("mnm", [P, 3]), ms2("msum", [P, 3]), ms2("mrc", [P, 3])
        mh.close(); mm_.close()
        n_qm = take(KT)
        h_v, h_s, h_max, h_exp, h_norm, h_a, h_ac = (sem(f"h_{k}") for k in ("v", "s", "max", "exp", "norm", "a", "ac"))
        h_pv, h_hi, h_lo, kc_in, vc_in = (sem(f"h_{k}") for k in ("pv", "hi", "lo", "kc", "vc"))
        h_hi2, h_apart = sem("h_hi2"), sem("h_apart")
        NQ, AHEAD = CH + 1, 2

        def h_bank(i):
            return (psL, psE, psY[:])[i % 3]

        def pe_scores_h(pe, h, q, i):
            bank = h_bank(i)
            pe.wait_ge(h_exp, h * NQ + max(i - 2, 0))
            if i == 2:
                pe.wait_ge(h_lo, h * 2)
            if i < CH:
                for kt in range(2):
                    mm = pe.matmul(bank[:, 0:MEM], qh2[:, q, kt, i * P:(i + 1) * P],
                                   cols(flat(km), h * (2 * MEM) + kt * MEM, MEM), start=(kt == 0), stop=(kt == 1))
            else:
                pe.wait_ge(h_apart, h + 1)
                pe.wait_ge(kc_in, h * 16 + 16)
                for b in range(NB):
                    for kt in range(2):
                        mm = pe.matmul(bank[0:TS, 0:MEM], apart[:, kt, b * TS:(b + 1) * TS], kc[:, b, kt, :],
                                       start=(b == 0 and kt == 0), stop=(b == NB - 1 and kt == 1))
            mm.then_inc(h_s, 1)

        def turn(pe, h, i):
            m = P if i < CH else TS
            pe.wait_ge(h_ac, h * 7 + i)
            pe.wait_ge(h_norm, h * NQ + (i + 1))
            for kk in range(2):
                mm = pe.matmul(psA[:, kk * P:kk * P + m], mp[0:m, i % 3, kk * P:(kk + 1) * P],
                               cst[0:m, CST["ident"][0]:CST["ident"][0] + m], start=True, stop=True)
            mm.then_inc(h_a, 1)

        def pe_head(pe, h, q, ahead):
            for u in range(2):
                par, k0 = slot(n_qm, u, h, 2)
                pe.wait_ge(dense_free[par], k0 + 1)
            for i in range(AHEAD):
                pe_scores_h(pe, h, q, i)
            for i in range(NQ):
                if i + AHEAD < NQ:
                    pe_scores_h(pe, h, q, i + AHEAD)
                turn(pe, h, i)
                if ahead and i in (0, 2):
                    pe_dense(pe, slot(n_qm, i // 2, h + 1, 2), xn_hi, xn_lo)
            pe.wait_ge(h_ac, h * 7 + 5)
            pe.wait_ge(h_v, h + 1)
            for dt in range(2):
                if dt:
                    pe.wait_ge(h_lo, h * 2 + 1)
                for kt in range(2):
                    mm = pe.matmul(psY[:], vh[:, kt, dt * P:(dt + 1) * P], mpt[:, kt, 0:SEQ], start=(kt == 0), stop=(kt == 1))
                mm.then_inc(h_pv, 1)
                if dt:
                    continue
                pe.wait_ge(vc_in, h * 16 + 16)
                for b in range(NB):
                    for kt in range(2):
                        mm = pe.matmul(psA[0:TS, 0:MEM], apart[:, kt, b * TS:(b + 1) * TS], vc[:, b, kt, :],
                                       start=(b == 0 and kt == 0), stop=(b == NB - 1 and kt == 1))
                mm.then_inc(h_a, 1)
            pe.wait_ge(h_ac, h * 7 + 6)
            for d2 in range(2):
                mm = pe.matmul(psA[:, d2 * TS:(d2 + 1) * TS], mo[:, d2 * P:(d2 + 1) * P], cst[0:TS, CST["ident"][0]:CST["ident"][0] + TS],
                               start=True, stop=True)
            mm.then_inc(h_a, 1)

        def pe_h(pe):
            with pe.Fori(0, 2) as j:
                for u in range(2):
                    pe_dense(pe, slot(n_qm, u, j * 2, 2), xn_hi, xn_lo)
                for q in range(2):
                    pe_head(pe, j * 2 + q, q, q == 0)

        def untile(act, h, i):
            act.wait_ge(h_a, h * 7 + (i + 1))
            turned = psA[:, 0:2 * P].rearrange("p (k q) -> p k q", k=2)
            dst = mpt[:, :, i * P:(i + 1) * P] if i < CH else apart_own
            src = turned if i < CH else turned[:, :, 0:TS].rearrange("p k (b t) -> p k b t", b=NB)
            act.activation(dst, src, ACT.Copy).then_inc(h_ac, 1)

        apart_own = apart[:].rearrange("p k (b w) -> p k b w", b=NB)[:, :, :, 0:DT]

        def act_load(act, h, buf, src, landed):
            act.dma_start(buf[:], src[bass.ds(h * P, P), :].rearrange("p (b k t) -> p b k t", b=NB, k=2)).then_inc(landed, 16)

        def act_queries_h(act, h, q, u):
            par, k0 = slot(n_qm, u, h, 2)
            act.wait_ge(dense_full[par], k0 + 1)
            act.activation(two(qh2[:, q, u, :]), dps[:, par, :, 0:HALF], ACT.Copy, scale=0.0625).then_inc(dense_free[par], 1)

        def act_exp_h(act, h, i):
            m = P if i < CH else TS
            act.wait_ge(h_max, h * NQ + (i + 1))
            act.activation(mp[0:m, i % 3, :], h_bank(i)[0:m, 0:MEM], ACT.Exp, bias=mnm[0:m, i % 3:i % 3 + 1],
                           accum_out=msum[0:m, i % 3:i % 3 + 1]).then_inc(h_exp, 1)

        def act_head(act, h, q, ahead):
            act.wait_ge(h_a, h * 7)
            for u in range(2):
                par, k0 = slot(n_qm, u, h, 2)
                act.wait_ge(dense_free[par], k0 + 1)
            act.activation(apart_own, qh2[:, q, :, SEQ:T].rearrange("p k (b t) -> p k b t", b=NB), ACT.Copy).then_inc(h_apart, 1)
            for i in range(AHEAD):
                act_exp_h(act, h, i)
            for i in range(NQ):
                if i + AHEAD < NQ:
                    act_exp_h(act, h, i + AHEAD)
                untile(act, h, i)
                if ahead and i + AHEAD == CH:
                    act_load(act, h + 1, kc, io["mem_kt"], kc_in)
                if i == 0:
                    act.wait_ge(h_pv, h * 2)
                    act.activation(vh[:], vm[:, :, bass.ds(h * MEM, MEM)], ACT.Copy).then_inc(h_v, 1)
                if ahead and i in (1, 3):
                    act_queries_h(act, h + 1, 1 - q, i // 2)
            for dt in range(2):
                act.wait_ge(h_pv, h * 2 + (dt + 1))
                act.activation(cols(flat(y_hi), (h * 2 + dt) * T, SEQ), psY[:], ACT.Copy).then_inc(h_hi, 1)
                if dt:
                    continue
                act.wait_ge(h_a, h * 7 + 6)
                act.activation(mo[:], psA[0:TS, 0:MEM], ACT.Copy).then_inc(h_ac, 1)
                if ahead:
                    act_load(act, h + 1, vc, io["mem_v"], vc_in)
            act.wait_ge(h_a, h * 7 + 7)
            act.activation(mfix[:], psA[:, 0:2 * TS].rearrange("p (k t) -> p k t", k=2), ACT.Copy).then_inc(h_ac, 1)
            act.wait_ge(h_ac, h * 7 + 7)
            for d2 in range(2):
                act.activation(cols(flat(y_hi), (h * 2 + d2) * T + SEQ, TS), mfix[:, d2, :], ACT.Copy).then_inc(h_hi2, 1)

        def act_h(act):
            with act.Fori(0, 2) as j:
                act.wait_ge(h_a, j * 14)
                act_load(act, j * 2, kc, io["mem_kt"], kc_in)
                act_load(act, j * 2, vc, io["mem_v"], vc_in)
                for u in range(2):
                    act_queries_h(act, j * 2, 0, u)
                for q in range(2):
                    act_head(act, j * 2 + q, q, q == 0)

        def dve_max_h(dve, h, i):
            m = P if i < CH else TS
            dve.wait_ge(h_s, h * NQ + (i + 1))
            if i >= 3:
                dve.wait_ge(h_exp, h * NQ + (i - 2))
            dve.tensor_reduce(mnm[0:m, i % 3:i % 3 + 1], h_bank(i)[0:m, 0:MEM], AX, ALU.max, negate=True).then_inc(h_max, 1)

        def dve_h(dve):
            link = chains["dve"]
            with dve.Fori(0, 2) as j:
                link.enter(j, 2 * (NQ + 2))
                for q in range(2):
                    h = j * 2 + q
                    for i in range(AHEAD):
                        dve_max_h(dve, h, i)
                    for i in range(NQ):
                        m = P if i < CH else TS
                        if i + AHEAD < NQ:
                            dve_max_h(dve, h, i + AHEAD)
                        dve.wait_ge(h_exp, h * NQ + (i + 1))
                        link(dve.reciprocal(mrc[0:m, i % 3:i % 3 + 1], msum[0:m, i % 3:i % 3 + 1]))
                        dve.tensor_scalar(mp[0:m, i % 3, :], mp[0:m, i % 3, :], mrc[0:m, i % 3:i % 3 + 1], None, ALU.mult).then_inc(h_norm, 1)
                    for dt in range(2):
                        dve.wait_ge(h_hi, h * 2 + (dt + 1))
                        o = (h * 2 + dt) * T
                        dve.tensor_tensor(cols(flat(y_lo), o, SEQ), psY[:], cols(flat(y_hi), o, SEQ).bitcast(F32), ALU.subtract).then_inc(h_lo, 1)
                    for dt in range(2):
                        dve.wait_ge(h_hi2, h * 2 + (dt + 1))
                        o = (h * 2 + dt) * T + SEQ
                        link(dve.tensor_tensor(cols(flat(y_lo), o, TS), mfix[:, dt, :], cols(flat(y_hi), o, TS).bitcast(F32), ALU.subtract))
            link.leave(2)
        dve_prog.append(lambda dve: chains["dve"](dve.memset(apart[:], 0.0)))
        edge("edge_apart")
        pe_prog.append(pe_h); act_prog.append(act_h); dve_prog.append(dve_h)
        edge("edge_h")
        merge_stage("m2", False)
        edge("edge_m2")

        hs = ExitStack()
        h_res = stage_sb(hs, "h_res", [P, KT, T])
        ftails = stage_sb(hs, "ftails", [P, 2 * FT, FPAD + NB * FPAD])
        h_in, mg_hi, wo_done = sem("h_in"), sem("mg_hi"), sem("wo_done")
        n_wo = take(KT)

        def pe_residual(pe, n0, hi, lo, nk):
            with pe.Fori(0, KT // 2) as i:
                for u in range(2):
                    pe_dense(pe, slot(n0, u, i, 2), hi, lo, nk=nk)

        def dve_residual(dve, n0):
            with dve.Fori(0, KT // 2) as i:
                for u in range(2):
                    par, k0 = slot(n0, u, i, 2)
                    dve.wait_ge(dense_full[par], k0 + 1)
                    hv = two(cols(flat(h_res), (i * 2 + u) * T, T))
                    dve.tensor_tensor(hv, hv, dps[:, par, :, 0:HALF], ALU.add).then_inc(dense_free[par], 1)

        def act_wo(act):
            act.dma_start(h_res[:], io["x_t"]).then_inc(h_in, 16)
            for k in range(KT):
                act.activation(xn_hi[:, k, :], merged[:, k, :], ACT.Copy, scale=0.5).then_inc(mg_hi, 1)

        def dve_wo(dve):
            link = chains["dve"]
            for k in range(KT):
                dve.wait_ge(mg_hi, k + 1)
                dve.scalar_tensor_tensor(xn_lo[:, k, :], merged[:, k, :], 0.5, xn_hi[:, k, :].bitcast(F32), ALU.mult, ALU.subtract).then_inc(wo_done, 1)
            dve.wait_ge(h_in, 16)
        act_prog.append(act_wo); dve_prog.append(dve_wo)
        pe_prog.append(lambda pe: pe.wait_ge(wo_done, KT))
        pe_prog.append(lambda pe: pe_residual(pe, n_wo, xn_hi, xn_lo, KT))
        dve_prog.append(lambda dve: dve_residual(dve, n_wo))
        edge("edge_wo")

        norm_stage("norm2", h_res, "norm2", xn_hi, xn_lo)
        edge("edge_norm2")
        fs = ExitStack()
        ff = lambda n, s, d=F32: stage_sb(fs, n, s, d)
        fin = ff("fin", [P, 2, FW])
        fout = ff("fout", [P, 2, FW])
        fth = ff("fth", [P, FW])
        fg = ff("fg", [P, FW])
        fa = ff("fa", [P, T])
        fs.close()
        f_in, f_conv, f_th, f_a, f_hi = sem("f_in"), sem("f_conv"), sem("f_th"), sem("f_a"), sem("f_hi")
        dve_prog.append(lambda dve: chains["dve"](dve.memset(fin[:, :, 0:FPAD], 0.0)))
        FO = FW - FPAD

        f_lo = sem("f_lo")

        def pe_pair(pe, n0, i):
            for u in range(2):
                pe_dense(pe, slot(n0, u, i, 2), xn_hi, xn_lo)

        def act_front(act, n0, i, j):
            for u in range(2):
                par, k0 = slot(n0, u, i, 2)
                act.wait_ge(dense_full[par], k0 + 1)
                act.wait_ge(f_conv, j * 2 + u)
                fb = fin[:, u, :]
                k = FPAD + NB * FPAD
                tl = cols(flat(ftails), j * k + u * FT * k, k)
                sample = by_seq(dps[:, par, 1, SEQ - HALF:HALF])
                act.activation(fb[:, FPAD:FPAD + HALF], dps[:, par, 0, 0:HALF], ACT.Copy)
                act.activation(fb[:, FPAD + HALF:FPB], dps[:, par, 1, 0:SEQ - HALF], ACT.Copy)
                act.activation(by_seq(tl[:, FPAD:k]), sample[:, :, DT - FPAD:DT], ACT.Copy)
                act.activation(tl[:, 0:FPAD], dps[:, par, 1, SEQ - HALF - FPAD:SEQ - HALF], ACT.Copy)
                act.activation(by_seq(fb[:, FPB:FW])[:, :, FPAD:FSB], sample, ACT.Copy).then_inc(dense_free[par], 1)
            act.wait_ge(f_conv, j * 2 + 1)
            act.wait_ge(f_a, j)
            act.activation(fth[:, 0:FO], fout[:, 0, 0:FO], ACT.Tanh).then_inc(f_th, 1)

        def act_back(act, j, at):
            act.wait_ge(f_a, j + 1)
            act.activation(cols(flat(y_hi), at * T, T), fa[:], ACT.Copy).then_inc(f_hi, 1)

        def dve_front(dve, link, n0, i, j):
            for u in range(2):
                par, k0 = slot(n0, u, i, 2)
                dve.wait_ge(dense_free[par], k0 + 1)
                fb, fo = fin[:, u, :], fout[:, u, 0:FO]
                w = lambda k: cols(fea, j * FCONV + (FEA["fconvw"][0] + u * FT * FCONV + k))
                link(dve.tensor_copy(by_seq(fb[:, FPB:FW])[:, :, 0:FPAD],
                                     by_seq(cols(fea, j * (NB * FPAD) + (FEA["fhist"][0] + u * FT * NB * FPAD), NB * FPAD))))
                link(dve.tensor_scalar(fo, fb[:, 0:FO], w(0), cols(fea, j + (FEA["fconvb"][0] + u * FT)), ALU.mult, ALU.add))
                for k in range(1, FCONV):
                    ins = dve.scalar_tensor_tensor(fo, fb[:, k:k + FO], w(k), fo, ALU.mult, ALU.add)
                    if k < FCONV - 1:
                        link(ins)
                ins.then_inc(f_conv, 1)
            dve.wait_ge(f_conv, j * 2 + 2)
            dve.wait_ge(f_th, j + 1)
            link(dve.scalar_tensor_tensor(fg[:, 0:FO], fth[:, 0:FO], 1.0, fout[:, 0, 0:FO], ALU.add, ALU.mult))
            seqs = lambda a: by_seq(a[:, FPB:FW])[:, :, 0:DT]
            dve.wait_ge(f_hi, j)
            dve.tensor_tensor(fa[:, 0:SEQ], fg[:, 0:SEQ], fout[:, 1, 0:SEQ], ALU.mult)
            dve.tensor_tensor(by_seq(fa[:, SEQ:T]), seqs(fg), seqs(fout[:, 1, :]), ALU.mult).then_inc(f_a, 1)

        def dve_back(dve, j, at):
            dve.wait_ge(f_hi, j + 1)
            dve.tensor_tensor(cols(flat(y_lo), at * T, T), fa[:], cols(flat(y_hi), at * T, T).bitcast(F32), ALU.subtract).then_inc(f_lo, 1)
            dve.wait_ge(f_lo, j + 1)

        def ffn_part(j0, count, first, ahead):
            skip = 0 if first else 1
            n_up = take(2 * (count - skip))
            n_ahead = take(2) if ahead else None
            n_down = take(KT)
            loops = count - skip

            def pe_f(pe):
                with pe.Fori(0, loops) as i:
                    pe_pair(pe, n_up, i)
                if ahead:
                    pe_pair(pe, n_ahead, 0)
                pe.wait_ge(f_lo, j0 + count)
                pe_residual(pe, n_down, y_hi, y_lo, count)

            def act_f(act):
                with act.Fori(0, loops) as i:
                    act_front(act, n_up, i, i + (j0 + skip))
                    act_back(act, i + (j0 + skip), i + skip)
                if ahead:
                    act_front(act, n_ahead, 0, j0 + count)
                    for u in range(2):
                        par, k0 = slot(n_down, KT - 2 + u)
                        act.wait_ge(dense_full[par], k0 + 1)
                    act_back(act, j0 + count, 0)

            def dve_f(dve):
                link = chains["dve"]
                with dve.Fori(0, loops) as i:
                    link.enter(i, 2 * FCONV + 1)
                    dve_front(dve, link, n_up, i, i + (j0 + skip))
                    dve_back(dve, i + (j0 + skip), i + skip)
                    link.leave(loops)
                if ahead:
                    dve_front(dve, link, n_ahead, 0, j0 + count)
                dve_residual(dve, n_down)
                if ahead:
                    dve_back(dve, j0 + count, 0)
            pe_prog.append(pe_f); act_prog.append(act_f); dve_prog.append(dve_f)

        j0 = 0
        for part, count in enumerate(FFN_PIECES):
            ffn_part(j0, count, part == 0, part < len(FFN_PIECES) - 1)
            j0 += count
        edge("edge_ffn")

        fo_ = ExitStack()
        yt = stage_sb(fo_, "yt", [P, KT, T])
        y_count = norm_stage("normf", h_res, "final", None, None, plain=yt)
        fo_.close()
        hs.close()

        def act_out(act):
            act.dma_start(io["ftails"], ftails[:].rearrange("p n k -> p (n k)")).then_inc(out_done, 16)
            act.wait_ge(norm_sems[4], y_count)
            act.dma_start(io["y_t"], yt[:]).then_inc(out_done, 16)
        act_prog.append(act_out)
        final_waits += [(ssm_out, GROUPS * 32), (kv_out, 32), (memkv_out, 32), (out_done, 48)]
        block = ctx.enter_context(nc.Block())
        n_tiles = nstream[0]

        @block.sync
        def _(sp):
            def load(par, k, n):
                sp.wait_ge(w_split[par], k)
                sp.dma_start(w_raw[:, par, :], io["wstream"][n, :, :] if isinstance(n, int) else
                             io["wstream"][bass.ds(n, 1), :, :].rearrange("o p c -> (o p) c")).then_inc(w_landed[par], 16)
            first = (n_pages_at + 2) // 2
            first = min(first, n_tiles // 2)
            with sp.Fori(0, first) as i:
                for par in range(2):
                    load(par, i, i * 2 + par)
            tail = n_tiles % 2 and first == n_tiles // 2
            if tail:
                load(0, n_tiles // 2, n_tiles - 1)
            if sp_pages[0]:
                sp_pages[0](sp)
            if first < n_tiles // 2:
                with sp.Fori(first, n_tiles // 2) as i:
                    for par in range(2):
                        load(par, i, i * 2 + par)
            if n_tiles % 2 and not tail:
                load(0, n_tiles // 2, n_tiles - 1)
            for s_, v_ in final_waits:
                sp.wait_ge(s_, v_)

        @block.gpsimd
        def _(pool):
            turns = pool.alloc_register("turns")
            pool.reg_mov(turns, 0)

            def split(par, k, n):
                pool.wait_ge(dense_full[par], k)
                pool.wait_ge(w_landed[par], k * 16 + 16)
                pool.sem_inc(w_taken, 1)
                pool.tensor_scalar(w_hi[:, par, :], w_raw[:, par, :], 1.0, 1.0, ALU.mult, ALU.mult).then_inc(w_hi_done, 1)
                pool.wait_ge(w_hi_done, n + 1)
                pool.tensor_tensor(w_lo[:, par, :], w_raw[:, par, :], w_hi[:, par, :].bitcast(F32), ALU.subtract).then_inc(w_split[par], 1)
            first = min((n_pages_at + 2) // 2, n_tiles // 2)
            with pool.Fori(0, first) as i:
                for par in range(2):
                    split(par, i, i * 2 + par)
            if n_tiles % 2 and first == n_tiles // 2:
                split(0, n_tiles // 2, n_tiles - 1)
            if sp_pages[0]:
                pool_values(pool)
            if first < n_tiles // 2:
                with pool.Fori(first, n_tiles // 2) as i:
                    for par in range(2):
                        split(par, i, i * 2 + par)
                if n_tiles % 2:
                    split(0, n_tiles // 2, n_tiles - 1)

        @block.tensor
        def _(pe):
            for f in pe_prog:
                f(pe)

        @block.scalar
        def _(act):
            chains["act"] = Chain(act, act_step)
            for f in act_prog:
                f(act)

        @block.vector
        def _(dve):
            chains["dve"] = Chain(dve, dve_step)
            for f in dve_prog:
                f(dve)


def weight_stream(w_in, w_ssd_out, w_attn_out, w_mem_kv, w_mem_out, w_o, w_up, w_down):
    tiles = []

    def add(w, column, row=0):
        tile = np.zeros((D, P), w.dtype)
        block = w[row:row + D, column:column + P]
        tile[:block.shape[0], :block.shape[1]] = block
        tiles.append(tile.reshape(KT, P, P).transpose(1, 0, 2).reshape(P, D))

    inner = 2 * D
    x_at, b_at, c_at, dt_at = inner, 2 * inner, 2 * inner + D, 2 * inner + 2 * D
    q_at = dt_at + HEADS
    k_at, v_at = q_at + D, q_at + D + 256
    qm_at = v_at + 256
    gate_at = qm_at + D

    def groups(which):
        for g in which:
            for column in (x_at + g * 256, x_at + g * 256 + P, b_at + g * P, c_at + g * P, g * 256, g * 256 + P):
                add(w_in, column)

    def branch(number, w, row=0):
        for m in range(KT):
            add(w_in, gate_at + number * D + m * P)
            add(w, m * P, row)

    add(w_in, dt_at)
    groups(range(5))
    for m in range(KT):
        add(w_ssd_out, m * P)
    groups(range(5, GROUPS))
    branch(0, w_ssd_out, D)
    for column in (k_at, k_at + P, v_at, v_at + P):
        add(w_in, column)
    for m in range(KT):
        add(w_in, q_at + m * P)
    branch(1, w_attn_out)
    for m in range(2 * KT):
        add(w_mem_kv, m * P)
    for m in range(KT):
        add(w_in, qm_at + m * P)
    branch(2, w_mem_out)
    for m in range(KT):
        add(w_o, m * P)
    j = 0
    for piece, count in enumerate(FFN_PIECES):
        first, last = piece == 0, piece == len(FFN_PIECES) - 1
        for _ in range(count + first - last):
            add(w_up, j * P)
            add(w_up, (FT + j) * P)
            j += 1
        for m in range(KT):
            add(w_down, m * P, piece * D)
    return np.stack(tiles)


def constants():
    out = np.zeros((P, CST_W), np.float32)

    def put(name, a):
        at, _ = CST[name]
        out[:a.shape[0], at:at + a.shape[1]] = a

    i, s, e, b = np.arange(P), np.arange(TS), np.arange(DT), np.arange(NB)
    same = s[:, None] // DT == s[None] // DT
    put("ident", np.eye(P))
    put("ones", np.ones((P, P)))
    put("upto_p", i[:, None] <= i[None])
    put("after_p", i[:, None] > i[None])
    put("upto_s", same & (s[:, None] <= s[None]))
    put("after_s", same & (s[:, None] > s[None]))
    put("same_b", s[:, None] // DT == b[None])
    rot, swap = np.zeros((P, P)), np.zeros((P, P))
    for head in (0, 64):
        rot[head + 8 + e, head + e] = -1
        rot[head + e, head + 8 + e] = 1
    swap[i, (i + 64) % P] = 1
    put("rot", rot)
    put("swap", swap)
    put("causal", np.where(i[:, None] >= i[None], 0, NEG))
    at = np.arange(2 * TS - DT)[None] - (TS - DT)
    put("own", np.where((at >= 0) & (at < DT) & (i[:, None] % DT >= at), 0, NEG))
    put("blk_lt", np.tile((b[None] < b[:, None]).reshape(1, NB * NB), (P, 1)))
    position = np.concatenate([np.arange(SEQ), np.tile(PAST + e, NB)]).astype(np.float32)
    inverse = np.float32(500000.0) ** (-e.astype(np.float32) * np.float32(2) / np.float32(16))
    angle = (inverse.astype(np.float32)[:, None] * position[None]).astype(np.float32)
    cos, sin = np.ones((P, T)), np.zeros((P, T))
    for row in (0, 8, 64, 72):
        cos[row:row + 8], sin[row:row + 8] = np.cos(angle), np.sin(angle)
    put("cos", cos)
    put("sin", sin)
    return out


def features_down(a):
    return np.ascontiguousarray(a.T.reshape(-1, P, a.shape[0]).transpose(1, 0, 2))


def tokens_down(a):
    return a.transpose(2, 1, 0).reshape(a.shape[2], -1)


def per_feature(inp):
    out = np.zeros((P, FEA_W), np.float32)

    def put(name, a):
        at, _ = FEA[name]
        a = a.reshape(a.shape[0], -1)
        out[:a.shape[0], at:at + a.shape[1]] = a

    def column(a):
        return a.reshape(-1, P).T

    def rows(a, tiles):
        return a.reshape(-1, tiles, P).transpose(2, 1, 0)

    put("norm1", column(inp["norm1_w"][0]))
    put("norm2", column(inp["norm2_w"][0]))
    put("memn", column(inp["mem_norm_w"][0]))
    put("final", column(inp["final_norm_w"]))
    put("ssdn", column(inp["ssd_norm_w"][0]))
    put("dskip", column(np.repeat(inp["d_skip"][0], 64)))
    put("dtb", inp["dt_bias"][0][:, None])
    put("alog", inp["a_log"][0][:, None])
    put("convw", rows(inp["ssd_conv_w"][0], NCV))
    put("convb", column(inp["ssd_conv_b"][0]))
    put("hist", rows(inp["state_conv"][0].reshape(NB * PAD, -1), NCV))
    put("fconvw", rows(inp["ffn_conv_w"][0], 2 * FT))
    put("fconvb", column(inp["ffn_conv_b"][0]))
    put("fhist", rows(inp["state_ffn_conv"][0].reshape(NB * FPAD, -1), 2 * FT))
    return out


def kernel(**inputs):
    import concourse.bacc as _bacc
    from concourse.bass_utils import run_bass_kernel_spmd as _run

    inp = {name: np.asarray(a) for name, a in inputs.items()}
    data = {
        "wstream": weight_stream(*(inp[name][0] for name in ("w_in", "w_ssd_out", "w_attn_out", "w_mem_kv", "w_mem_out",
                                                             "w_o", "w_up", "w_down"))),
        "x_t": features_down(np.concatenate([inp["x_prompt"][0], inp["x_sample"].reshape(TS, D)], 0)),
        "cst": constants(),
        "fea": per_feature(inp),
        "state_t": inp["state_ssm"][0].reshape(NB, GROUPS, GH, 64, P).transpose(1, 4, 0, 2, 3).reshape(GROUPS * P, -1),
        "mem_t": features_down(inp["mem_prompt"][0]),
        "k_pages": inp["cache_k"][0].reshape(-1, PAGE, 2, P).transpose(0, 3, 2, 1).reshape(-1, P, 2 * PAGE),
        "v_pages": inp["cache_v"][0].reshape(-1, PAGE, 2 * P),
        "mem_kt": inp["cache_mem_k"][0].reshape(NB, MEM, 4, 2, P).transpose(2, 4, 0, 3, 1).reshape(4 * P, -1),
        "mem_v": inp["cache_mem_v"][0].reshape(NB, 2, P, 4, MEM).transpose(3, 2, 0, 1, 4).reshape(4 * P, -1),
        "page_table": inp["page_table"].reshape(1, -1),
    }
    outs = {"y_t": (P, KT, T), "kv_t": (P, 4, T), "memkv_t": (P, 2 * KT, MEM), "ssm_p": (GROUPS * P, 256),
            "ssm_s": (GROUPS * P, NB * 256), "tails": (P, NCV * (PAD + NB * PAD)),
            "ftails": (P, 2 * FT * (FPAD + NB * FPAD))}

    nc = _bacc.Bacc("TRN2", target_bir_lowering=False, num_devices=1)
    arrays, io = {}, {}
    for name, a in data.items():
        a = np.ascontiguousarray(a)
        arrays[f"{name}_dram"] = a
        io[name] = nc.dram_tensor(f"{name}_dram", a.shape, mybir.dt.from_np(a.dtype), kind="ExternalInput").ap()
    for name, shape in outs.items():
        io[name] = nc.dram_tensor(f"{name}_dram", shape, F32, kind="ExternalOutput").ap()
    build_program(nc, io)
    result = _run(nc, [arrays], core_ids=[0]).results[0]
    got = {name: np.asarray(result[f"{name}_dram"]) for name in outs}

    def parts(a, rows):
        return a[:rows], a[rows:]

    y_p, y_s = parts(tokens_down(got["y_t"]), SEQ)
    k_p, k_s = parts(tokens_down(got["kv_t"][:, 0:2]), SEQ)
    v_p, v_s = parts(tokens_down(got["kv_t"][:, 2:4]), SEQ)
    mem_k, mem_v = (tokens_down(got["memkv_t"][:, j * KT:(j + 1) * KT]).reshape(1, 1, MEM, 4, 256) for j in range(2))
    ssm_p = got["ssm_p"].reshape(GROUPS, P, GH, 64).transpose(0, 2, 3, 1).reshape(1, 1, HEADS, 64, P)
    ssm_s = got["ssm_s"].reshape(GROUPS, P, NB, GH, 64).transpose(2, 0, 3, 4, 1).reshape(1, NB, HEADS, 64, P)
    conv_p, conv_s = parts(tokens_down(got["tails"].reshape(P, NCV, -1)), PAD)
    ffn_p, ffn_s = parts(tokens_down(got["ftails"].reshape(P, 2 * FT, -1)), FPAD)
    return tuple(np.ascontiguousarray(a) for a in (
        y_p.reshape(1, SEQ, D), y_s.reshape(NB, DT, D),
        k_p.reshape(1, 1, SEQ, 4, 64), v_p.reshape(1, 1, SEQ, 4, 64), mem_k, mem_v, ssm_p,
        conv_p.reshape(1, 1, PAD, -1), ffn_p.reshape(1, 1, FPAD, -1),
        k_s.reshape(1, NB, DT, 4, 64), v_s.reshape(1, NB, DT, 4, 64), ssm_s,
        conv_s.reshape(1, NB, PAD, -1), ffn_s.reshape(1, NB, FPAD, -1)))
```

```python
from collections import namedtuple
from contextlib import ExitStack

import numpy as np

import concourse.bass as bass
from concourse import mybir

F32 = mybir.dt.float32
F32R = mybir.dt.float32r
ALU = mybir.AluOpType
ACT = mybir.ActivationFunctionType
AX = mybir.AxisListType.X

P = 128
D = 1024
KT = D // P
SEQ = 512
NB, DT = 8, 8
TS = NB * DT
T = SEQ + TS
HALF = T // 2
CH = SEQ // P
HEADS = 32
GROUPS = 8
GH = HEADS // GROUPS
SCONV, FCONV = 4, 3
NCV = 32
FT = 22
PAD = SCONV - 1
PBUF = SEQ + PAD
SB1 = DT + PAD
CW = PBUF + NB * SB1
FPAD = FCONV - 1
FPB = SEQ + FPAD
FSB = DT + FPAD
FW = FPB + NB * FSB
PAST, PAGE = 2048, 128
NPG = PAST // PAGE
MEM = 256
EPS = 1e-6
NEG = -1e30


def offsets(parts):
    at, out = 0, {}
    for name, width in parts:
        out[name] = (at, width)
        at += width
    return out, at


CST, CST_W = offsets([
    ("ident", P), ("ones", P), ("upto_p", P), ("after_p", P), ("upto_s", TS), ("after_s", TS),
    ("same_b", NB), ("rot", P), ("swap", P), ("causal", P), ("own", 2 * TS - DT), ("blk_lt", 64),
    ("cos", T), ("sin", T)])
FEA, FEA_W = offsets([
    ("norm1", KT), ("norm2", KT), ("memn", KT), ("final", KT), ("ssdn", 16), ("dskip", 16),
    ("dtb", 1), ("alog", 1), ("convw", NCV * SCONV), ("convb", NCV), ("hist", NCV * NB * PAD),
    ("fconvw", 2 * FT * FCONV), ("fconvb", 2 * FT), ("fhist", 2 * FT * NB * FPAD)])

N_DT = 1
N_GRP = 6
FFN_PIECES = (8, 8, 6)


class Chain:

    def __init__(self, eng, sem):
        self.e, self.sem, self.base, self.i, self.per, self.local = eng, sem, 0, None, 0, 0

    def value(self):
        v = self.base + self.local
        return v if self.i is None else self.i * self.per + v

    def __call__(self, ins):
        ins.then_inc(self.sem, 1)
        self.local += 1
        self.e.wait_ge(self.sem, self.value())

    def enter(self, i, per):
        self.base, self.local, self.i, self.per = self.base + self.local, 0, i, per

    def leave(self, trips):
        assert self.local == self.per, f"links of a turn: {self.local}, not {self.per}"
        self.base, self.local, self.i = self.base + trips * self.per, 0, None


Stage = namedtuple("Stage", "pe act dve")


def build_program(nc, io):
    ctx = ExitStack()
    with ctx:
        def sb(name, shape, dt=F32):
            return ctx.enter_context(nc.sbuf_tensor(name, shape, dt))

        def stage_sb(stack, name, shape, dt=F32):
            return stack.enter_context(nc.sbuf_tensor(name, shape, dt))

        def sem(name):
            return ctx.enter_context(nc.semaphore(name))

        cst = sb("cst", [P, CST_W])
        fea = sb("fea", [P, FEA_W])
        xn_hi, xn_lo = sb("xn_hi", [P, KT, T], F32R), sb("xn_lo", [P, KT, T], F32R)
        y_hi, y_lo = sb("y_hi", [P, KT, T], F32R), sb("y_lo", [P, KT, T], F32R)
        merged = sb("merged", [P, KT, T])
        w_raw = sb("w_raw", [P, 2, D])
        w_hi, w_lo = sb("w_hi", [P, 2, D], F32R), sb("w_lo", [P, 2, D], F32R)
        w_taken = sem("w_taken")
        era = ExitStack()
        dt_tok = stage_sb(era, "dt_tok", [P, 2, CH + 1, HEADS])
        dec = stage_sb(era, "dec", [P, CH + 1, HEADS])
        tot = stage_sb(era, "tot", [P, CH * HEADS + NB * HEADS])

        tails = stage_sb(era, "tails", [P, NCV, PAD + NB * PAD])

        def c_(name, p=P):
            at, w = CST[name]
            return cst[0:p, at:at + w]

        def f_(name, i=0, n=1, p=P):
            at, _ = FEA[name]
            return fea[0:p, at + i * n:at + i * n + n]

        ident, ones = c_("ident"), c_("ones")

        dps = ctx.enter_context(nc.psum_tensor("dps", [P, 2, 2, 512], F32))
        psA = ctx.enter_context(nc.psum_tensor("psA", [P, 512], F32))
        psLE = ctx.enter_context(nc.psum_tensor("psLE", [P, 2, 512], F32))
        psL, psE = psLE[:, 0, :], psLE[:, 1, :]
        psY = ctx.enter_context(nc.psum_tensor("psY", [P, 512], F32))

        w_landed = [sem("w_landed0"), sem("w_landed1")]
        w_hi_done = sem("w_hi_done")
        w_split = [sem("w_split0"), sem("w_split1")]
        dense_full = [sem("dense_full0"), sem("dense_full1")]
        dense_free = [sem("dense_free0"), sem("dense_free1")]
        cst_in, fea_in, x_in = sem("cst_in"), sem("fea_in"), [sem("x_in0"), sem("x_in1")]
        out_done = sem("out_done")
        dve_step, act_step = sem("dve_step"), sem("act_step")
        stage_done = [sem("pe_stage"), sem("act_stage"), sem("dve_stage")]

        chains = {}

        def stage_end(e, own, count):
            e.drain().then_inc(stage_done[own], 1)
            for other in range(3):
                e.wait_ge(stage_done[other], count)

        def from_one(count):
            return count + 1

        def two(ap):
            return ap.rearrange("p (h c) -> p h c", h=2)

        def slot(n0, u, i=0, nb=0):
            return (n0 + u) % 2, (n0 + u) // 2 + i * (nb // 2)

        def pe_dense(pe, tile, hi, lo, nk=KT, width=T, ready=None):
            par, k0 = tile
            pe.wait_ge(w_split[par], from_one(k0 + 1))
            pe.wait_ge(dense_free[par], k0)
            spans = [(0, 0, width)] if width <= 512 and width != T else [(0, 0, HALF), (1, HALF, HALF)]
            for k in range(nk):
                if ready:
                    pe.wait_ge(ready[0], ready[1] + k)
                wh, wl = w_hi[:, par, k * P:(k + 1) * P], w_lo[:, par, k * P:(k + 1) * P]
                for j, (w, a) in enumerate(((wh, hi), (wh, lo), (wl, hi))):
                    for b, c0, cw in spans:
                        mm = pe.matmul(dps[:, par, b, 0:cw], w, a[:, k, c0:c0 + cw],
                                       start=(k == 0 and j == 0), stop=(k == nk - 1 and j == 2))
            mm.then_inc(dense_full[par], 1)

        nstream = [0]

        def take(count):
            n = nstream[0]
            nstream[0] += count
            return n

        norm_sems = [sem(f"norm_{k}") for k in ("sq_ready", "sq_used", "sum", "mean", "root", "t_ready", "hi_ready")]
        norm_lo = sem("norm_lo")
        norm_count = [0]

        def norm_stage(name, src, wname, hi, lo, width=T, ready={}, plain=None, summed=None, meanwhile=None):
            st = ExitStack()
            sq = stage_sb(st, f"{name}_sq", [P, 2, width])
            acc = summed or stage_sb(st, f"{name}_acc", [P, width])
            rs = stage_sb(st, f"{name}_rs", [P, width])
            t = stage_sb(st, f"{name}_t", [P, 2, width])
            st.close()
            sq_ready, sq_used, sum_full, mean_ready, root_ready, t_ready, hi_ready = norm_sems
            norms = norm_count[0]
            norm_count[0] += 1
            done, kts = norms * KT, KT
            if width == T:
                sp = lambda ap: two(ap)
                ps = psLE[:, :, 0:HALF]
                spans = [(0, 0, HALF), (1, HALF, HALF)]
            else:
                sp = lambda ap: ap
                ps = psLE[:, 0, 0:width]
                spans = [(0, 0, width)]

            def pe_f(pe):
                pe.wait_ge(sq_used, done + kts)
                for b, c0, cw in spans:
                    mm = pe.matmul(psLE[:, b, 0:cw], ones, acc[:, c0:c0 + cw], start=True, stop=True)
                mm.then_inc(sum_full, 1)

            def act_f(act):
                for k in range(kts if summed is None else 0):
                    for s, v in ready.get(k, ()):
                        act.wait_ge(s, v)
                    if k >= 2:
                        act.wait_ge(sq_used, done + k - 1)
                    act.activation(sq[:, k % 2, :], src[:, k, :], ACT.Square).then_inc(sq_ready, 1)
                act.wait_ge(mean_ready, norms + 1)
                act.activation(rs[:], rs[:], ACT.Sqrt).then_inc(root_ready, 1)
                if hi is not None:
                    for k in range(kts):
                        act.wait_ge(t_ready, done + k + 1)
                        act.activation(hi[:, k, 0:width], t[:, k % 2, :], ACT.Copy).then_inc(hi_ready, 1)

            def dve_f(dve):
                link = chains["dve"]
                for waits in ready.values():
                    for s, v in waits:
                        dve.wait_ge(s, v)
                for k in range(kts if summed is None else 0):
                    dve.wait_ge(sq_ready, done + k + 1)
                    if k == 0:
                        dve.tensor_copy(acc[:], sq[:, 0, :]).then_inc(sq_used, 1)
                    else:
                        dve.tensor_tensor(acc[:], acc[:], sq[:, k % 2, :], ALU.add).then_inc(sq_used, 1)
                    dve.wait_ge(sq_used, done + k + 1)
                dve.wait_ge(sum_full, norms + 1)
                dve.tensor_scalar(sp(rs[:]), ps, 1.0 / D, EPS, ALU.mult, ALU.add).then_inc(mean_ready, 1)
                if meanwhile:
                    meanwhile(dve)
                dve.wait_ge(root_ready, norms + 1)
                link(dve.reciprocal(rs[:], rs[:]))
                if hi is None:
                    for k in range(kts):
                        dve.scalar_tensor_tensor(plain[:, k, :], src[:, k, :], f_(wname, k), rs[:],
                                                 ALU.mult, ALU.mult).then_inc(t_ready, 1)
                    return
                for k in range(kts + 1):
                    if k < kts:
                        dve.scalar_tensor_tensor(t[:, k % 2, :], src[:, k, :], f_(wname, k), rs[:],
                                                 ALU.mult, ALU.mult).then_inc(t_ready, 1)
                    if k:
                        dve.wait_ge(hi_ready, done + k)
                        dve.tensor_tensor(lo[:, k - 1, 0:width], t[:, (k - 1) % 2, :], hi[:, k - 1, 0:width].bitcast(F32),
                                          ALU.subtract).then_inc(norm_lo, 1)
                        dve.wait_ge(norm_lo, done + k)
            return Stage(pe_f, act_f, dve_f)

        s0 = ExitStack()
        x_t = stage_sb(s0, "x_t", [P, KT, T])

        def act_load(act):
            for j in range(2):
                half = slice(j * KT // 2, (j + 1) * KT // 2)
                act.dma_start(x_t[:, half, :], io["x_t"][:, half, :]).then_inc(x_in[j], 16)
            act.dma_start(cst[:], io["cst"]).then_inc(cst_in, 16)
            act.dma_start(fea[:], io["fea"]).then_inc(fea_in, 16)


        def dve_scale(dve):
            link = chains["dve"]
            dve.wait_ge(fea_in, 16)
            for name, w in (("convw", NCV * SCONV), ("convb", NCV), ("ssdn", 16),
                            ("fconvw", FT * FCONV), ("fconvb", FT)):
                a, _ = FEA[name]
                link(dve.tensor_scalar(fea[:, a:a + w], fea[:, a:a + w], 0.5, None, ALU.mult))
        norm1 = norm_stage("norm1", x_t, "norm1", xn_hi, xn_lo, ready={0: ((x_in[0], 16),), KT // 2: ((x_in[1], 16),)},
                           meanwhile=dve_scale)
        s0.close()

        ssd_stack = ExitStack()
        ss = lambda n, s, d=F32: stage_sb(ssd_stack, n, s, d)
        cbuf = ss("cbuf", [P, 2, CW])
        cout = ss("cout", [P, 2, CW])
        cth = ss("cth", [P, CW])
        feat = ss("feat", [P, 2, 6, T])
        xg2, bg2, cg2, zg2 = feat[:, :, 0:2, :], feat[:, :, 2, :], feat[:, :, 3, :], feat[:, :, 4:6, :]
        yg = ss("yg", [P, 2, T])
        rhs_a = ss("rhs_a", [P, GH, P])
        cbm = ss("cbm", [P, P])
        btok = ss("btok", [P, P])
        xdt, xdtd = ss("xdt", [P, 256]), ss("xdtd", [P, 256])
        l_exp, e_exp = ss("l_exp", [P, 512]), ss("e_exp", [P, 512])
        state = ss("state", [P, 256])
        st_in = ss("st_in", [P, NB, 256])
        bm = ss("bm", [TS, NB, P])
        acol = ss("acol", [HEADS, 1])
        rstd = ss("rstd", [P, T])
        ssd_stack.close()
        era.close()

        conv_ready = sem("conv_ready")
        th_ready, feat_ready = sem("th_ready"), sem("feat_ready")
        zth_ready = sem("zth_ready")
        a_full, a_free, le_full, exp_ready = sem("a_full"), sem("a_free"), sem("le_full"), sem("exp_ready")
        rhs_ready, m_ready, y_full, y_free = sem("rhs_ready"), sem("m_ready"), sem("y_full"), sem("y_free")
        n_full, n_free = sem("n_full"), sem("n_free")
        st_landed = sem("st_landed")
        gsq_ready, gsum_full, gmean_ready, groot_ready = sem("gsq_ready"), sem("gsum_full"), sem("gmean_ready"), sem("groot_ready")
        gate_ready, gt_ready, ghi_ready = sem("gate_ready"), sem("gt_ready"), sem("ghi_ready")
        ssm_ready, ssm_out = sem("ssm_ready"), sem("ssm_out")

        def cols(ap2, off, w=1):
            return ap2[:, bass.ds(off, w)]

        def flat(t3):
            return t3[:].rearrange("p k t -> p (k t)")

        def by_seq(ap):
            return ap.rearrange("p (b t) -> p b t", b=NB)

        def per_head(ap):
            return ap.rearrange("p (h d) -> p h d", h=GH)

        def spread(ap, m, w):
            return ap.rearrange("p (h o) -> p h o", o=1).to_broadcast([m, GH, w])

        def over_heads(ap, m, w):
            return ap.rearrange("p (o i) -> p o i", o=1).to_broadcast([m, GH, w])

        def tile_of(N, u):
            late = (KT if N > 4 else 0) if isinstance(N, int) else 0
            return (N_DT + late + u) % 2, (N_DT + late + u) // 2 + N * (N_GRP // 2)

        def tail_at(N, u):
            return N * 2 + u if u < 2 else N + (16 if u == 2 else 24)

        def act_copy(act, N, u):
            par, k0 = tile_of(N, u)
            act.wait_ge(dense_full[par], from_one(k0 + 1))
            if u >= 2:
                act.wait_ge(conv_ready, N * 4 + u - 1)
            cb = cbuf[:, u % 2, :]
            n_tail = PAD + NB * PAD
            tl = cols(flat(tails), tail_at(N, u) * n_tail, n_tail)
            sample = by_seq(dps[:, par, 1, SEQ - HALF:HALF])
            act.activation(cb[:, PAD:PAD + HALF], dps[:, par, 0, 0:HALF], ACT.Copy)
            act.activation(cb[:, PAD + HALF:PBUF], dps[:, par, 1, 0:SEQ - HALF], ACT.Copy)
            act.activation(by_seq(tl[:, PAD:n_tail]), sample[:, :, DT - PAD:DT], ACT.Copy)
            act.activation(tl[:, 0:PAD], dps[:, par, 1, SEQ - HALF - PAD:SEQ - HALF], ACT.Copy)
            act.activation(by_seq(cb[:, PBUF:CW])[:, :, PAD:SB1], sample, ACT.Copy).then_inc(dense_free[par], 1)

        def act_tanh(act, N, u):
            act.wait_ge(conv_ready, N * 4 + u + 1)
            act.wait_ge(feat_ready, N * 4 + u)
            act.activation(cth[:, 0:CW - PAD], cout[:, u % 2, 0:CW - PAD], ACT.Tanh).then_inc(th_ready, 1)

        def act_z(act, N, q, j):
            par, k0 = tile_of(N, 4 + j)
            act.wait_ge(dense_full[par], from_one(k0 + 1))
            act.activation(two(zg2[:, q, j, :]), dps[:, par, :, 0:HALF], ACT.Tanh, scale=0.5).then_inc(zth_ready, 1)

        GROUP_LINKS = 58

        def dve_conv(dve, link, N, u):
            tix = tail_at(N, u)
            cb, co = cbuf[:, u % 2, :], cout[:, u % 2, 0:CW - PAD]
            par, k0 = tile_of(N, u)
            dve.wait_ge(dense_free[par], k0 + 1)
            link(dve.tensor_copy(by_seq(cb[:, PBUF:CW])[:, :, 0:PAD], by_seq(cols(fea, tix * (NB * PAD) + FEA["hist"][0], NB * PAD))))
            w = lambda j: cols(fea, tix * SCONV + (FEA["convw"][0] + j))
            if u >= 2:
                dve.wait_ge(th_ready, N * 4 + u - 1)
            link(dve.tensor_scalar(co, cb[:, 0:CW - PAD], w(0), cols(fea, tix + FEA["convb"][0]), ALU.mult, ALU.add))
            for j in range(1, SCONV):
                ins = dve.scalar_tensor_tensor(co, cb[:, j:j + CW - PAD], w(j), co, ALU.mult, ALU.add)
                if j < SCONV - 1:
                    link(ins)
            ins.then_inc(conv_ready, 1)
            dve.wait_ge(conv_ready, N * 4 + u + 1)

        def dve_silu(dve, N, q, u):
            dst = (xg2[:, q, 0, :], xg2[:, q, 1, :], bg2[:, q, :], cg2[:, q, :])[u]
            co, th = cout[:, u % 2, :], cth
            seqs = lambda a: by_seq(a[:, PBUF:CW])[:, :, 0:DT]
            dve.wait_ge(th_ready, N * 4 + u + 1)
            dve.scalar_tensor_tensor(dst[:, 0:SEQ], th[:, 0:SEQ], 1.0, co[:, 0:SEQ], ALU.add, ALU.mult)
            dve.scalar_tensor_tensor(by_seq(dst[:, SEQ:T]), seqs(th), 1.0, seqs(co), ALU.add, ALU.mult).then_inc(feat_ready, 1)
            dve.wait_ge(feat_ready, N * 4 + u + 1)

        def dve_z(dve, N, q, j):
            dve.wait_ge(zth_ready, N * 2 + j + 1)
            par, k0 = tile_of(N, 4 + j)
            dve.scalar_tensor_tensor(two(zg2[:, q, j, :]), two(zg2[:, q, j, :]), 1.0, dps[:, par, :, 0:HALF],
                                     ALU.add, ALU.mult).then_inc(dense_free[par], 1)
            dve.wait_ge(dense_free[par], k0 + 1)

        def dve_rhs(dve, G, c):
            m = P if c < CH else TS
            up = c_("upto_p") if c < CH else c_("upto_s", TS)
            dve.tensor_tensor(rhs_a[0:m, :, 0:m], over_heads(up, m, m), spread(cols(dt_tok[0:m, 1, c, :], G * GH, GH), m, m),
                              ALU.mult).then_inc(rhs_ready, 1)

        def next_group(G, u):
            return tile_of(G + 1, u)

        n_gate = N_DT + GROUPS * N_GRP + KT

        def gates_of(G, u):
            return slot(n_gate, u)

        def act_gate(act, G, u):
            par, k0 = gates_of(G, u)
            act.wait_ge(dense_full[par], from_one(k0 + 1))
            act.activation(two(feat[:, 0, u, :]), dps[:, par, :, 0:HALF], ACT.Tanh, scale=0.5).then_inc(dense_free[par], 1)

        def pe_group(pe, G, q, ahead):
            xg, bg, cg, zg = xg2[:, q], bg2[:, q], cg2[:, q], zg2[:, q]
            pe.wait_ge(feat_ready, G * 4 + 4)
            for c in range(CH + 1):
                last = c == CH
                m = P if not last else TS
                lo_, hi_ = c * P, c * P + m
                pe.wait_ge(a_free, from_one(G * 5 + c))
                pe.matmul(psA[0:m, 384:384 + m], bg[:, lo_:hi_], cg[:, lo_:hi_], start=True, stop=True)
                for j in range(2):
                    pe.transpose(psA[0:m, j * P:(j + 1) * P], xg[:, j, lo_:hi_], ident)
                pe.transpose(psA[0:m, 256:384], bg[:, lo_:hi_], ident).then_inc(a_full, 1)
                pe.wait_ge(rhs_ready, G * 5 + c + 1)
                if c == 0:
                    pe.wait_ge(gmean_ready, from_one(G))
                rv = rhs_a[0:m, :, 0:m]
                if c > 0:
                    pe.matmul(per_head(psE[:, 0:GH * m]), cst[0:m, CST["ones"][0]:CST["ones"][0] + P], rv, start=True, stop=True)
                pe.matmul(per_head(psL[0:m, 0:GH * m]), c_("after_p") if not last else c_("after_s", TS), rv,
                          start=True, stop=True).then_inc(le_full, 1)
                if ahead:
                    pe_dense(pe, ahead(G, c), xn_hi, xn_lo)
                pe.wait_ge(m_ready, G * 5 + c + 1)
                pe.wait_ge(y_free, from_one(G * 5 + c))
                lv, ev = per_head(l_exp[0:m, 0:GH * m]), per_head(e_exp[:, 0:GH * m])
                if last:
                    pe.wait_ge(st_landed, G * 16 + 16)
                    for b in range(NB):
                        for j in range(2):
                            o = 2 * m + (b * 2 + j) * 16
                            pe.matmul(psY[:, o:o + 16].rearrange("p (h t) -> p h t", h=2),
                                      st_in[:, b, j * P:(j + 1) * P], ev[:, 2 * j:2 * j + 2, b * DT:(b + 1) * DT],
                                      start=True, stop=True)
                for h in range(GH):
                    o = psY[(h % 2) * 64:(h % 2) * 64 + 64, (h // 2) * m:(h // 2 + 1) * m]
                    carried = 0 < c < CH
                    mm = pe.matmul(o, xdt[0:m, h * 64:h * 64 + 64], lv[:, h, :], start=True, stop=not carried)
                    if carried:
                        pe.matmul(o, state[:, h * 64:h * 64 + 64], ev[:, h, :], start=False, stop=True)
                if not last:
                    pe.matmul(psY[:, 256:512], btok[:], xdtd[:], start=True, stop=True).then_inc(y_full, 1)
                else:
                    mm.then_inc(y_full, 1)
            for r in range(4):
                if r == 2 and ahead:
                    pe_dense(pe, ahead(G, 5), xn_hi, xn_lo)
                if r > 1:
                    pe.wait_ge(n_free, G * 4 + r - 1)
                bank = psL if r % 2 == 0 else psE
                for b in (2 * r, 2 * r + 1):
                    mm = pe.matmul(bank[:, (b % 2) * 256:(b % 2) * 256 + 256], bm[:, b, :], xdtd[0:TS, :],
                                   start=True, stop=True)
                mm.then_inc(n_full, 1)
            pe.wait_ge(n_free, G * 4 + 4)
            pe.wait_ge(gsq_ready, G + 1)
            for hf, bank in ((0, psL), (1, psE)):
                for j in range(2):
                    mm = pe.matmul(bank[:, 0:HALF], ones, zg[:, j, hf * HALF:(hf + 1) * HALF], start=(j == 0), stop=(j == 1))
            mm.then_inc(gsum_full, 1)

        def act_norm(act, G, q, first_y):
            act.wait_ge(gmean_ready, from_one(G + 1))
            act.activation(rstd[:], rstd[:], ACT.Sqrt).then_inc(groot_ready, 1)
            for j in range(2):
                act.wait_ge(gt_ready, G * 2 + (j + 1))
                yh = cols(flat(y_hi), (G * 2 - first_y + j) * T, T)
                act.activation(yh, zg2[:, q, j, :], ACT.Copy).then_inc(ghi_ready, 1)

        def act_group(act, G, q, first_y, ahead, before):
            zg = zg2[:, q]
            for c in range(CH + 1):
                act.wait_ge(le_full, G * 5 + c + 1)
                m = P if c < CH else TS
                ins = act.activation(l_exp[0:m, 0:GH * m], psL[0:m, 0:GH * m], ACT.Exp)
                if c > 0:
                    ins = act.activation(e_exp[:, 0:GH * m], psE[:, 0:GH * m], ACT.Exp)
                ins.then_inc(exp_ready, 1)
                if c == 1:
                    act.wait_ge(ssm_out, from_one(G * 32))
                    act.dma_start(st_in[:], io["state_t"][bass.ds(G * P, P), :].rearrange("n (b q) -> n b q", b=NB)).then_inc(st_landed, 16)
                if ahead == gates_of:
                    act_gate(act, G, c)
                elif ahead:
                    N = G + 1
                    if c < 4:
                        act_copy(act, N, c)
                    else:
                        act_z(act, N, 1 - q, 0)
                    if c >= 1:
                        act_tanh(act, N, c - 1)
                if before and c == 0:
                    act_norm(act, G - 1, 1 - q, first_y)
            act.wait_ge(gate_ready, G + 1)
            for j in range(2):
                ins = act.activation(zg[:, j, :], yg[:, j, :], ACT.Square)
            ins.then_inc(gsq_ready, 1)
            if ahead == gates_of:
                act_gate(act, G, 5)
            elif ahead:
                act_z(act, N, 1 - q, 1)
            act.wait_ge(ssm_ready, G + 1)
            act.dma_start(io["ssm_s"][bass.ds(G * P, P), :].rearrange("n (b q) -> n b q", b=NB), st_in[:]).then_inc(ssm_out, 16)
            act.dma_start(io["ssm_p"][bass.ds(G * P, P), :], state[:]).then_inc(ssm_out, 16)

        def dve_norm_group(dve, link, G, q, first_y):
            zg = zg2[:, q]
            dve.wait_ge(groot_ready, G + 1)
            link(dve.reciprocal(rstd[:], rstd[:]))
            for j in range(2):
                dve.scalar_tensor_tensor(zg[:, j, :], yg[:, j, :], cols(fea, G * 2 + (FEA["ssdn"][0] + j)), rstd[:], ALU.mult, ALU.mult).then_inc(gt_ready, 1)
            for j in range(2):
                dve.wait_ge(ghi_ready, G * 2 + j + 1)
                off = (G * 2 - first_y + j) * T
                link(dve.tensor_tensor(cols(flat(y_lo), off, T), zg[:, j, :], cols(flat(y_hi), off, T).bitcast(F32), ALU.subtract))

        def dve_group(dve, link, G, q, first_y, ahead, before):
            xg, bg, cg, zg = xg2[:, q], bg2[:, q], cg2[:, q], zg2[:, q]
            ahead = ahead == next_group
            N = G + 1
            for c in range(CH + 1):
                last = c == CH
                m = P if not last else TS
                lo_, hi_ = c * P, c * P + m
                up = c_("upto_p") if not last else c_("upto_s", TS)
                dve.wait_ge(a_full, G * 5 + c + 1)
                link(dve.tensor_tensor(per_head(xdt[0:m, :]), per_head(psA[0:m, 0:256]), spread(cols(dt_tok[0:m, 0, c, :], G * GH, GH), m, 64), ALU.mult))
                link(dve.tensor_copy(btok[0:m, :], psA[0:m, 256:384]))
                dve.tensor_tensor(cbm[0:m, 0:m], psA[0:m, 384:384 + m], up, ALU.mult).then_inc(a_free, 1)
                dve.wait_ge(a_free, from_one(G * 5 + c + 1))
                link(dve.tensor_tensor(per_head(xdtd[0:m, :]), per_head(xdt[0:m, :]), spread(cols(dec[0:m, c, :], G * GH, GH), m, 64), ALU.mult))
                if last:
                    link(dve.tensor_tensor(bm[:], btok[0:TS, :].rearrange("p (o n) -> p o n", o=1).to_broadcast([TS, NB, P]),
                                           c_("same_b", TS).rearrange("p (b o) -> p b o", o=1).to_broadcast([TS, NB, P]), ALU.mult))
                dve.wait_ge(exp_ready, G * 5 + c + 1)
                lv, ev = per_head(l_exp[0:m, 0:GH * m]), per_head(e_exp[:, 0:GH * m])
                ins = dve.tensor_tensor(lv, lv, over_heads(cbm[0:m, 0:m], m, m), ALU.mult)
                if c > 0:
                    ins = dve.tensor_tensor(ev, ev, over_heads(cg[:, lo_:hi_], P, m), ALU.mult)
                ins.then_inc(m_ready, 1)
                dve.wait_ge(m_ready, G * 5 + c + 1)
                if not last:
                    dve_rhs(dve, G, c + 1)
                if before and c == 0:
                    dve_norm_group(dve, link, G - 1, 1 - q, first_y)
                if ahead and c >= 1:
                    dve_conv(dve, link, N, c - 1)
                if ahead and c >= 2:
                    dve_silu(dve, N, 1 - q, c - 2)
                dve.wait_ge(y_full, G * 5 + c + 1)
                for j in range(2):
                    dsk = cols(fea, G * 2 + (FEA["dskip"][0] + j))
                    link(dve.scalar_tensor_tensor(yg[:, j, lo_:hi_], xg[:, j, lo_:hi_], dsk, psY[:, j * m:(j + 1) * m], ALU.mult, ALU.add))
                if not last:
                    if c > 0:
                        link(dve.tensor_tensor(per_head(state[:]), per_head(state[:]), spread(cols(tot, G * GH + c * HEADS, GH), P, 64), ALU.mult))
                        ins = dve.tensor_tensor(state[:], state[:], psY[:, 256:512], ALU.add)
                    else:
                        dve.wait_ge(ssm_out, from_one(G * 32))
                        ins = dve.tensor_copy(state[:], psY[:, 256:512])
                    ins.then_inc(y_free, 1)
                    dve.wait_ge(y_free, from_one(G * 5 + c + 1))
            for hh in range(2):
                r0, r1 = hh * 64, hh * 64 + 64
                yv = yg[r0:r1, :, SEQ:T].rearrange("p q (b t) -> p b q t", b=NB)
                ov = psY[r0:r1, 128:384].rearrange("p (b q h t) -> p b q h t", b=NB, q=2, h=2)[:, :, :, hh, :]
                ins = dve.tensor_tensor(yv, yv, ov, ALU.add)
                if hh == 0:
                    link(ins)
            ins.then_inc(y_free, 1)
            dve.wait_ge(y_free, from_one(G * 5 + 5))
            dve.tensor_tensor(yg[:], yg[:], zg, ALU.mult).then_inc(gate_ready, 1)
            for b in range(NB):
                link(dve.tensor_tensor(per_head(st_in[:, b, :]), per_head(st_in[:, b, :]), spread(cols(tot, G * GH + (CH + b) * HEADS, GH), P, 64), ALU.mult))
            for r in range(4):
                bank = psL if r % 2 == 0 else psE
                dve.wait_ge(n_full, G * 4 + r + 1)
                sv = st_in[:, 2 * r:2 * r + 2, :].rearrange("p b q -> p (b q)")
                dve.tensor_tensor(sv, sv, bank, ALU.add).then_inc(n_free, 1)
            dve.wait_ge(n_free, G * 4 + 4)
            dve.sem_inc(ssm_ready, 1)
            if ahead:
                dve_silu(dve, N, 1 - q, 3)
                dve_z(dve, N, 1 - q, 0)
                dve_rhs(dve, N, 0)
            dve.wait_ge(gsum_full, G + 1)
            link(dve.tensor_scalar(rstd[:, 0:HALF], psL[:, 0:HALF], 1.0 / 1024, EPS, ALU.mult, ALU.add))
            dve.tensor_scalar(rstd[:, HALF:T], psE[:, 0:HALF], 1.0 / 1024, EPS, ALU.mult, ALU.add).then_inc(gmean_ready, 1)
            if ahead:
                dve_z(dve, N, 1 - q, 1)
        take(N_DT)
        dtv = [feat[0:HEADS, 1, i, :] for i in range(6)]
        da_b = xdt[0:TS, :].rearrange("p (b h) -> p b h", b=NB)
        dt_e, dt_l, dt_t, dt_f = (sem(f"dt_{k}") for k in ("exp", "ln", "tr", "full"))
        dt_n, dt_u, a_neg, dt_tokd = sem("dt_n"), sem("dt_u"), sem("dt_a"), sem("dt_tokd")
        dtx, dtr, dtn, dte, dtu, dtl = dtv

        def pe_dt(pe):
            for u in range(2):
                pe_dense(pe, tile_of(0, u), xn_hi, xn_lo)
            pe.wait_ge(dt_f, 1)
            for j, v in enumerate((dtx, dtr)):
                for c in range(CH + 1):
                    m = P if c < CH else TS
                    o = (j * (CH + 1) + c) * HEADS
                    tr = pe.transpose(psA[0:m, o:o + HEADS], v[:, c * P:c * P + m], cst[0:HEADS, CST["ident"][0]:CST["ident"][0] + HEADS])
            tr.then_inc(dt_t, 1)
            pe_dense(pe, tile_of(0, 2), xn_hi, xn_lo)
            pe.wait_ge(dt_tokd, 1)
            da = dt_tok[:, 1, 0:CH, :].rearrange("p c h -> p (c h)")
            pe.matmul(psL[:, 0:CH * HEADS], c_("after_p"), da, start=True, stop=True)
            pe.matmul(psL[0:TS, 128:160], c_("after_s", TS), dt_tok[0:TS, 1, CH, :], start=True, stop=True)
            pe.matmul(psE[:, 0:CH * HEADS], ones, da, start=True, stop=True)
            pe.matmul(psE[:, 128:384], cst[0:TS, CST["ones"][0]:CST["ones"][0] + P],
                      xdt[0:TS, :], start=True, stop=True).then_inc(dt_t, 1)
            for u in range(3, N_GRP):
                pe_dense(pe, tile_of(0, u), xn_hi, xn_lo)

        def act_dt(act):
            link = chains["act"]
            act.wait_ge(dense_full[0], from_one(1))
            act.activation(two(dtx), dps[0:HEADS, 0, :, 0:HALF], ACT.Identity, bias=f_("dtb", p=HEADS)).then_inc(dense_free[0], 1)
            act.activation(acol[:], f_("alog", p=HEADS), ACT.Exp).then_inc(a_neg, 1)
            act.wait_ge(dt_n, 1)
            act.activation(dte, dtn, ACT.Exp).then_inc(dt_e, 1)
            act.wait_ge(dt_u, 1)
            act.activation(dtl, dtu, ACT.Ln).then_inc(dt_l, 1)
            for u in range(2):
                act_copy(act, 0, u)
            act.wait_ge(dt_t, 2)
            link(act.activation(dec[:, 0:CH, :].rearrange("p c h -> p (c h)"), psL[:, 0:128], ACT.Exp))
            link(act.activation(dec[0:TS, CH, :], psL[0:TS, 128:160], ACT.Exp))
            link(act.activation(tot[:], psE[:, 0:384], ACT.Exp))
            act_tanh(act, 0, 0)
            for u in range(2, 4):
                act_copy(act, 0, u)
                act_tanh(act, 0, u - 1)
            act_tanh(act, 0, 3)
            for j in range(2):
                act_z(act, 0, 0, j)

        def dve_dt(dve):
            link = chains["dve"]
            tt = lambda o, a, b, op: link(dve.tensor_tensor(o, a, b, op))
            ts = lambda o, a, s, op: link(dve.tensor_scalar(o, a, s, None, op))
            dve.wait_ge(dense_free[0], 1)
            ts(dtr, dtx, 0.0, ALU.max)
            ts(dtn, dtx, -1.0, ALU.mult)
            dve.tensor_tensor(dtn, dtn, dtx, ALU.min).then_inc(dt_n, 1)
            dve.wait_ge(dt_e, 1)
            dve.tensor_scalar(dtu, dte, 1.0, None, ALU.add).then_inc(dt_u, 1)
            dve.wait_ge(dt_l, 1)
            ts(dtu, dtu, 1.0, ALU.subtract)
            ts(dtn, dtu, 0.0, ALU.is_equal)
            tt(dtl, dtl, dtn, ALU.add)
            tt(dtu, dtu, dtn, ALU.add)
            link(dve.reciprocal(dtu, dtu))
            tt(dtl, dtl, dtu, ALU.mult)
            tt(dtl, dtl, dte, ALU.mult)
            tt(dtx, dtl, dtr, ALU.add)
            dve.wait_ge(a_neg, 1)
            link(dve.tensor_scalar(acol[:], acol[:], -1.0, None, ALU.mult))
            dve.tensor_scalar(dtr, dtx, acol[:], None, ALU.mult).then_inc(dt_f, 1)
            dve.wait_ge(dt_t, 1)
            link(dve.tensor_copy(dt_tok[:, :, 0:CH, :], psA[:, 0:320].rearrange("p (j c h) -> p j c h", j=2, c=CH + 1)[:, :, 0:CH, :]))
            link(dve.tensor_copy(dt_tok[0:TS, :, CH, :], psA[0:TS, 0:320].rearrange("p (j c h) -> p j c h", j=2, c=CH + 1)[:, :, CH, :]))
            dve.tensor_tensor(da_b, dt_tok[0:TS, 1:2, CH, :].to_broadcast([TS, NB, HEADS]),
                              c_("same_b", TS).rearrange("p (b o) -> p b o", o=1).to_broadcast([TS, NB, HEADS]),
                              ALU.mult).then_inc(dt_tokd, 1)
            for u in range(4):
                dve_conv(dve, link, 0, u)
                if u >= 1:
                    dve_silu(dve, 0, 0, u - 1)
            dve_silu(dve, 0, 0, 3)
            for j in range(2):
                dve_z(dve, 0, 0, j)
            dve_rhs(dve, 0, 0)


        def pe_half0(pe):
            with pe.Fori(0, 2) as i:
                for q in range(2):
                    pe_group(pe, i * 2 + q, q, next_group)

        def act_half0(act):
            with act.Fori(0, 2) as i:
                for q in range(2):
                    act_group(act, i * 2 + q, q, 0, next_group, q == 1)
                act_norm(act, i * 2 + 1, 1, 0)

        def dve_half0(dve):
            link = chains["dve"]
            with dve.Fori(0, 2) as i:
                link.enter(i, 2 * GROUP_LINKS)
                for q in range(2):
                    dve_group(dve, link, i * 2 + q, q, 0, next_group, q == 1)
                dve_norm_group(dve, link, i * 2 + 1, 1, 0)
                link.leave(2)

        take(5 * N_GRP)

        n0c = take(KT)

        def pe_c(pe):
            with pe.Fori(0, KT // 2) as i:
                for u in range(2):
                    pe_dense(pe, slot(n0c, u, i, 2), y_hi, y_lo)

        def act_c(act):
            with act.Fori(0, KT // 2) as i:
                for u in range(2):
                    par, k0 = slot(n0c, u, i, 2)
                    act.wait_ge(dense_full[par], from_one(k0 + 1))
                    act.activation(two(flat(merged)[:, bass.ds((i * 2 + u) * T, T)]),
                                   dps[:, par, :, 0:HALF], ACT.Copy).then_inc(dense_free[par], 1)
        def pe_half1(pe):
            for G in range(4, GROUPS):
                pe_group(pe, G, G % 2, next_group if G < GROUPS - 1 else gates_of)

        def act_half1(act):
            for G in range(4, GROUPS):
                act_group(act, G, G % 2, KT, next_group if G < GROUPS - 1 else gates_of, G > 4)
            act_norm(act, GROUPS - 1, 1, KT)

        def dve_half1(dve):
            for G in range(4, GROUPS):
                dve_group(dve, chains["dve"], G, G % 2, KT, next_group if G < GROUPS - 1 else gates_of, G > 4)
            dve_norm_group(dve, chains["dve"], GROUPS - 1, 1, KT)
        take(4 * N_GRP)


        def act_states_out(act):
            act.dma_start(io["tails"], flat(tails)).then_inc(out_done, 16)
            act.wait_ge(ssm_out, from_one(GROUPS * 32))
            act.wait_ge(out_done, 16)

        merged_done, merges = sem("merged_done"), [0]

        def merge_stage(name):
            st = ExitStack()
            gth = stage_sb(st, f"{name}_gth", [P, 2, T])
            tmp = stage_sb(st, f"{name}_tmp", [P, 2, T])
            st.close()
            n0 = take(2 * KT)
            before = merges[0] * KT
            merges[0] += 1

            def pe_f(pe):
                with pe.Fori(0, KT // 2) as i:
                    for u in range(4):
                        gate = u % 2 == 0
                        pe_dense(pe, slot(n0, u, i, 4), xn_hi if gate else y_hi, xn_lo if gate else y_lo)

            def act_f(act):
                with act.Fori(0, KT // 2) as i:
                    for u in (0, 2):
                        par, k0 = slot(n0, u, i, 4)
                        act.wait_ge(merged_done, i * 2 + before)
                        act.wait_ge(dense_full[par], from_one(k0 + 1))
                        act.activation(two(gth[:, u // 2, :]), dps[:, par, :, 0:HALF], ACT.Tanh, scale=0.5).then_inc(dense_free[par], 1)

            def dve_f(dve):
                link = chains["dve"]
                with dve.Fori(0, KT // 2) as i:
                    link.enter(i, 2)
                    for j in range(2):
                        gp, gk = slot(n0, 2 * j, i, 4)
                        par, k0 = slot(n0, 2 * j + 1, i, 4)
                        mv = merged[:].rearrange("p k t -> p (k t)")[:, bass.ds((i * 2 + j) * T, T)]
                        dve.wait_ge(dense_free[gp], gk + 1)
                        dve.wait_ge(dense_full[par], from_one(k0 + 1))
                        ps = dps[:, par, :, 0:HALF]
                        dve.scalar_tensor_tensor(two(tmp[:, j, :]), two(gth[:, j, :]), 1.0, ps, ALU.add, ALU.mult).then_inc(dense_free[par], 1)
                        dve.wait_ge(dense_free[par], k0 + 1)
                        link(dve.tensor_tensor(mv, mv, tmp[:, j, :], ALU.add))
                        dve.sem_inc(merged_done, 1)
                link.leave(KT // 2)
            return Stage(pe_f, act_f, dve_f)

        def merge_first():
            READY = N_GRP
            st = ExitStack()
            gth = stage_sb(st, "m0_gth", [P, KT - READY, T])
            tmp = stage_sb(st, "m0_tmp", [P, 2, T])
            st.close()
            n0, n1 = take(READY), take(2 * (KT - READY))
            merges[0] += 1

            def pe_f(pe):
                with pe.Fori(0, READY // 2) as i:
                    for u in range(2):
                        pe_dense(pe, slot(n0, u, i, 2), y_hi, y_lo)
                for u in range(2 * (KT - READY)):
                    gate = u % 2 == 0
                    pe_dense(pe, slot(n1, u), xn_hi if gate else y_hi, xn_lo if gate else y_lo)

            def act_f(act):
                for j in range(KT - READY):
                    par, k0 = slot(n1, 2 * j)
                    act.wait_ge(dense_full[par], from_one(k0 + 1))
                    act.activation(two(gth[:, j, :]), dps[:, par, :, 0:HALF], ACT.Tanh, scale=0.5).then_inc(dense_free[par], 1)

            def merge(dve, tile, gate, j, mv):
                par, k0 = tile
                dve.wait_ge(dense_full[par], from_one(k0 + 1))
                dve.tensor_tensor(two(tmp[:, j, :]), two(mv), dps[:, par, :, 0:HALF], ALU.add).then_inc(dense_free[par], 1)
                dve.wait_ge(dense_free[par], k0 + 1)
                dve.scalar_tensor_tensor(mv, gate, 1.0, tmp[:, j, :], ALU.add, ALU.mult).then_inc(merged_done, 1)

            def dve_f(dve):
                with dve.Fori(0, READY // 2) as i:
                    for j in range(2):
                        merge(dve, slot(n0, j, i, 2), cols(feat[:, 0].rearrange("p k t -> p (k t)"), (i * 2 + j) * T, T), j,
                              cols(flat(merged), (i * 2 + j) * T, T))
                for j in range(KT - READY):
                    gp, gk = slot(n1, 2 * j)
                    dve.wait_ge(dense_free[gp], gk + 1)
                    merge(dve, slot(n1, 2 * j + 1), gth[:, j, :], j, merged[:, READY + j, :])
            return Stage(pe_f, act_f, dve_f)

        merge0 = merge_first()

        att = ExitStack()
        as_ = lambda n, s, d=F32: stage_sb(att, n, s, d)
        ks = as_("ks", [P, 2, T])
        v_new = as_("v_new", [TS, 256])
        qbd = as_("qbd", [P, 2, NB, P])
        ys = as_("ys", [64, 16, TS])
        pro = ExitStack()
        ps_ = lambda n, s, d=F32: stage_sb(pro, n, s, d)
        ksw = ps_("ksw", [P, 2, T])
        v_tok = ps_("v_tok", [P, CH, 256])
        raw, ropet = ps_("raw", [P, T]), ps_("ropet", [P, T])
        keys_only = ExitStack()
        vs = stage_sb(keys_only, "vs", [P, 2, T])
        keys_only.close()
        qk2 = ps_("qk", [P, 2, T])
        kcur2 = ps_("kcur", [P, 2, SEQ])
        vcur2 = ps_("vcur", [P, 2, CH, 64])
        prob = ps_("prob", [P, 4, SEQ])
        prob_t = ps_("prob_t", [P, CH, SEQ])
        nmax, psum_, prec = ps_("nmax", [P, 4]), ps_("psum_", [P, 4]), ps_("prec", [P, 4])
        pro.close()

        raw_ready, rot_full, rope_done = sem("raw_ready"), sem("rot_full"), sem("rope_done")
        sw_full, sw_copied = sem("sw_full"), sem("sw_copied")
        vt_full, vt_copied = sem("vt_full"), sem("vt_copied")
        kv_out = sem("kv_out")
        n_kv = take(4)

        def rope(dve, link, dst, n_done, n_rot, banks=psLE):
            dve.wait_ge(rot_full, n_rot)
            dve.tensor_tensor(two(ropet[:]), two(c_("sin")), banks[:, :, 0:HALF], ALU.mult)
            link(dve.tensor_tensor(dst, raw[:], c_("cos"), ALU.mult))
            dve.tensor_tensor(dst, dst, ropet[:], ALU.add).then_inc(rope_done, 1)
            dve.wait_ge(rope_done, n_done)

        def pe_rot(pe, src, mat, done, banks=psLE):
            for b in range(2):
                mm = pe.matmul(banks[:, b, 0:HALF], mat, src[:, b * HALF:(b + 1) * HALF], start=True, stop=True)
            mm.then_inc(done, 1)

        def pe_kv(pe):
            for u in range(2):
                pe_dense(pe, slot(n_kv, u), xn_hi, xn_lo)
            for j in range(2):
                pe.wait_ge(raw_ready, j + 1)
                pe_rot(pe, raw, c_("rot"), rot_full)
                pe.wait_ge(rope_done, j + 1)
            for u in range(2, 4):
                pe_dense(pe, slot(n_kv, u), xn_hi, xn_lo)
            for j in range(2):
                if j:
                    pe.wait_ge(sw_copied, 1)
                pe_rot(pe, ks[:, j, :], c_("swap"), sw_full)
            par, k0 = slot(n_kv, 3)
            pe.wait_ge(dense_free[par], k0 + 1)
            for c in range(CH):
                bank = psA if c < 2 else psY
                for j in range(2):
                    mm = pe.transpose(bank[:, (c % 2) * 256 + j * P:(c % 2) * 256 + (j + 1) * P], vs[:, j, c * P:(c + 1) * P], ident)
            mm.then_inc(vt_full, 1)
            pe.wait_ge(vt_copied, 1)
            for j in range(2):
                mm = pe.transpose(psA[0:TS, j * P:(j + 1) * P], vs[:, j, SEQ:T], ident)
            mm.then_inc(vt_full, 1)

        def act_kv(act):
            for u in range(4):
                par, k0 = slot(n_kv, u)
                act.wait_ge(dense_full[par], from_one(k0 + 1))
                if u == 0:
                    act.activation(two(raw[:]), dps[:, par, :, 0:HALF], ACT.Copy).then_inc(dense_free[par], 1)
                    act.wait_ge(dense_free[par], k0 + 1)
                    act.sem_inc(raw_ready, 1)
                elif u == 1:
                    act.wait_ge(rope_done, 1)
                    act.activation(two(raw[:]), dps[:, par, :, 0:HALF], ACT.Copy).then_inc(dense_free[par], 1)
                    act.wait_ge(dense_free[par], k0 + 1)
                    act.sem_inc(raw_ready, 1)
                else:
                    act.activation(two(vs[:, u - 2, :]), dps[:, par, :, 0:HALF], ACT.Copy).then_inc(dense_free[par], 1)
            act.wait_ge(dense_free[par], k0 + 1)
            act.dma_start(io["kv_t"][:, 2:4, :], vs[:]).then_inc(kv_out, 16)
            for j in range(2):
                act.wait_ge(sw_full, j + 1)
                act.activation(two(ksw[:, j, :]), psLE[:, :, 0:HALF], ACT.Copy).then_inc(sw_copied, 1)
            act.wait_ge(rope_done, 2)
            act.dma_start(io["kv_t"][:, 0:2, :], ks[:]).then_inc(kv_out, 16)
            act.wait_ge(kv_out, 32)

        def dve_kv(dve):
            link = chains["dve"]
            dve.memset(qbd[:], 0.0)
            for j in range(2):
                dve.wait_ge(raw_ready, j + 1)
                rope(dve, link, ks[:, j, :], j + 1, j + 1)
            dve.wait_ge(vt_full, 1)
            dve.tensor_copy(v_tok[:, 0:2, :], psA[:].rearrange("p (c f) -> p c f", c=2))
            dve.tensor_copy(v_tok[:, 2:4, :], psY[:].rearrange("p (c f) -> p c f", c=2)).then_inc(vt_copied, 1)
            dve.wait_ge(vt_full, 2)
            dve.tensor_copy(v_new[:], psA[0:TS, 0:256]).then_inc(vt_copied, 1)

        n_q = take(KT)
        s_full, s_max, s_exp, p_norm = sem("s_full"), sem("s_max"), sem("s_exp"), sem("p_norm")
        t_full, t_copied, pv_full = sem("t_full"), sem("t_copied"), sem("pv_full")
        yhi_ready, ylo_ready, qsw_full, qbd_done, kv_cur = sem("yhi_ready"), sem("ylo_ready"), sem("qsw_full"), sem("qbd_done"), sem("kv_cur")

        ROUNDS, LOOK = 2 * CH, 3

        def q_bank(tt, r):
            par, _ = slot(n_q, tt)
            return (psL, psE, dps[:, par, 0, :], dps[:, par, 1, :])[r % 4]

        def pe_prep(pe, j, tt, step):
            par, _ = slot(n_q, tt)
            t = j * 4 + tt
            if step == "project":
                pe_dense(pe, slot(n_q, tt, j, 4), xn_hi, xn_lo)
            if step == "rotate":
                pe.wait_ge(raw_ready, t + 3)
                pe_rot(pe, raw, c_("rot"), rot_full, dps[:, par])
            if step == "swap":
                pe.wait_ge(rope_done, t + 3)
                pe.matmul(dps[:, par, 0, 0:TS], c_("swap"), qk2[:, tt % 2, SEQ:T], start=True, stop=True).then_inc(qsw_full, 1)

        def pe_scores_q(pe, t, tt, r):
            hh, i = r // CH, r % CH
            qk, kcur = qk2[:, tt % 2, :], kcur2[:, tt // 2, :]
            pe.wait_ge(s_exp, t * 8 + (r + 1))
            rows = slice(hh * 64, hh * 64 + 64)
            bank = q_bank(tt, r)
            pe.matmul(bank[:, 0:(i + 1) * P], qk[rows, i * P:(i + 1) * P], kcur[rows, 0:(i + 1) * P], start=True, stop=False)
            pe.matmul(bank[:, i * P:(i + 1) * P], ident, c_("causal"), start=False, stop=True).then_inc(s_full, 1)

        def pe_products_q(pe, t, tt, hh):
            pe.wait_ge(t_copied, from_one(t * 8 + (hh * CH + CH)))
            if hh == 0:
                pe.wait_ge(ylo_ready, from_one(t))
            for kt in range(CH):
                mm = pe.matmul(psY[hh * 64:hh * 64 + 64, kt * P:SEQ], vcur2[:, tt // 2, kt, :], prob_t[:, kt, kt * P:SEQ],
                               start=(kt == 0), stop=(kt == CH - 1))
            mm.then_inc(pv_full, 1)

        def pe_q(pe):
            with pe.Fori(0, 2) as j:
                for step in ("project", "rotate", "swap"):
                    pe_prep(pe, j, 0, step)
                for tt in range(4):
                    t = j * 4 + tt
                    pe.wait_ge(qbd_done, t + 1)
                    if tt % 2 == 0:
                        pe.wait_ge(kv_cur, j * 2 + (tt // 2 + 1))
                    for r in range(LOOK):
                        pe_scores_q(pe, t, tt, r)
                    if tt:
                        pe_products_q(pe, j * 4 + (tt - 1), tt - 1, 1)
                    for r in range(ROUNDS):
                        if r + LOOK < ROUNDS:
                            pe_scores_q(pe, t, tt, r + LOOK)
                        pe.wait_ge(p_norm, t * 8 + (r + 1))
                        pe.wait_ge(t_copied, from_one(t * 8 + r))
                        for kt in range(r % CH + 1):
                            mm = pe.transpose(psA[:, kt * P:(kt + 1) * P], prob[:, r % 4, kt * P:(kt + 1) * P], ident)
                        mm.then_inc(t_full, 1)
                        if r == CH:
                            pe_products_q(pe, t, tt, 0)
                        if tt < 3 and r in (1, 3, 6):
                            pe_prep(pe, j, tt + 1, {1: "project", 3: "rotate", 6: "swap"}[r])
                pe_products_q(pe, j * 4 + 3, 3, 1)

        def act_prep(act, j, tt):
            t = j * 4 + tt
            par, k0 = slot(n_q, tt, j, 4)
            act.wait_ge(dense_full[par], from_one(k0 + 1))
            act.wait_ge(rope_done, t + 2)
            act.activation(two(raw[:]), dps[:, par, :, 0:HALF], ACT.Copy, scale=0.125).then_inc(dense_free[par], 1)
            act.wait_ge(dense_free[par], k0 + 1)
            act.sem_inc(raw_ready, 1)
            if tt % 2 == 0:
                g = tt // 2
                act.wait_ge(pv_full, from_one(j * 8))
                for hf in range(2):
                    rows = slice(hf * 64, hf * 64 + 64)
                    act.activation(kcur2[rows, g, :], flat(ks if hf == g else ksw)[rows, bass.ds(j * T, SEQ)], ACT.Copy)
                act.activation(vcur2[:, g], v_tok[:, :, bass.ds(j * P + g * 64, 64)], ACT.Copy).then_inc(kv_cur, 1)

        def act_exp_q(act, t, tt, r):
            w = (r % CH + 1) * P
            act.wait_ge(s_max, t * 8 + (r + 1))
            act.activation(prob[:, r % 4, 0:w], q_bank(tt, r)[:, 0:w], ACT.Exp, bias=nmax[:, r % 4:r % 4 + 1],
                           accum_out=psum_[:, r % 4:r % 4 + 1]).then_inc(s_exp, 1)

        def act_y_q(act, t):
            act.wait_ge(pv_full, from_one(t * 2 + 2))
            act.activation(cols(flat(y_hi), t * T, SEQ), psY[:], ACT.Copy).then_inc(yhi_ready, 1)

        def act_q(act):
            act.sem_inc(s_exp, 4)
            with act.Fori(0, 2) as j:
                act_prep(act, j, 0)
                for tt in range(4):
                    t = j * 4 + tt
                    for r in range(LOOK):
                        act_exp_q(act, t, tt, r)
                    if tt:
                        act_y_q(act, j * 4 + (tt - 1))
                    for r in range(ROUNDS):
                        i = r % CH
                        if r + LOOK < ROUNDS:
                            act_exp_q(act, t, tt, r + LOOK)
                        act.wait_ge(t_full, t * 8 + (r + 1))
                        if i == 0:
                            act.wait_ge(pv_full, from_one(t * 2 + r // CH))
                        act.activation(prob_t[:, 0:i + 1, i * P:(i + 1) * P], psA[:, 0:(i + 1) * P].rearrange("p (k q) -> p k q", q=P),
                                       ACT.Copy).then_inc(t_copied, 1)
                        if tt < 3 and r == 2:
                            act_prep(act, j, tt + 1)
                act_y_q(act, j * 4 + 3)

        def dve_queries_q(dve, link, j, tt):
            t = j * 4 + tt
            rope(dve, link, qk2[:, tt % 2, :], t + 3, t + 3, dps[:, slot(n_q, tt)[0]])

        def dve_sample_q(dve, j, tt):
            t = j * 4 + tt
            g, r0 = tt // 2, (tt % 2) * 2
            par, _ = slot(n_q, tt)
            dve.wait_ge(qsw_full, t + 1)
            rows = slice(g * 64, g * 64 + 64)
            for hf in range(2):
                src = qk2[rows, tt % 2, SEQ:T] if hf == g else dps[rows, par, 0, 0:TS]
                col = g * 32 + (r0 + hf) * DT
                ap = qbd[rows, bass.ds(j, 1), :, bass.ds(j * 64 + col, DT)].rearrange("p o b c -> p (o b) c")
                ins = dve.tensor_copy(ap, by_seq(src))
            ins.then_inc(qbd_done, 1)

        def dve_max_q(dve, t, tt, r):
            dve.wait_ge(s_full, t * 8 + (r + 1))
            dve.wait_ge(s_exp, t * 8 + (r + 1))
            dve.tensor_reduce(nmax[:, r % 4:r % 4 + 1], q_bank(tt, r)[:, 0:(r % CH + 1) * P], AX, ALU.max, negate=True).then_inc(s_max, 1)

        def dve_y_q(dve, t):
            dve.wait_ge(yhi_ready, t + 1)
            dve.tensor_tensor(cols(flat(y_lo), t * T, SEQ), psY[:], cols(flat(y_hi), t * T, SEQ).bitcast(F32), ALU.subtract).then_inc(ylo_ready, 1)
            dve.wait_ge(ylo_ready, from_one(t + 1))

        def dve_q(dve):
            link = chains["dve"]
            with dve.Fori(0, 2) as j:
                link.enter(j, PER_Q)
                dve_queries_q(dve, link, j, 0)
                dve_sample_q(dve, j, 0)
                for tt in range(4):
                    t = j * 4 + tt
                    for r in range(LOOK):
                        dve_max_q(dve, t, tt, r)
                    for r in range(ROUNDS):
                        if r + LOOK < ROUNDS:
                            dve_max_q(dve, t, tt, r + LOOK)
                        w = (r % CH + 1) * P
                        dve.wait_ge(s_exp, t * 8 + (r + 5))
                        link(dve.reciprocal(prec[:, r % 4:r % 4 + 1], psum_[:, r % 4:r % 4 + 1]))
                        dve.tensor_scalar(prob[:, r % 4, 0:w], prob[:, r % 4, 0:w], prec[:, r % 4:r % 4 + 1], None, ALU.mult).then_inc(p_norm, 1)
                        if tt and r == 0:
                            dve_y_q(dve, j * 4 + (tt - 1))
                        if tt < 3 and r == 4:
                            dve_queries_q(dve, link, j, tt + 1)
                        if tt < 3 and r == 6:
                            dve_sample_q(dve, j, tt + 1)
                dve_y_q(dve, j * 4 + 3)
            link.leave(2)

        PER_Q = 36

        n_pages_at = nstream[0]
        sam = ExitStack()
        sa = lambda n, s, d=F32: stage_sb(sam, n, s, d)
        ptab = sa("ptab", [1, NB * NPG], mybir.dt.int32)
        kpg = sa("kpg", [P, 2, 4, 256])
        vpg = sa("vpg", [P, 4, 4, 256])
        sc = sa("sc", [P, 2, PAST + TS])
        pt_s = sa("pt_s", [P, NPG, P])
        pt_own = sa("pt_own", [TS, P])
        qb = sa("qb", [P, 2, P])
        gs, bmx, cmp1, cmp2 = sa("gs", [P, 8]), sa("bmx", [P, 9]), sa("cmp1", [P, 8, 8]), sa("cmp2", [P, 8, 8])
        rank, bias, nm, ssum = sa("rank", [P, 8]), sa("bias", [P, 9]), sa("nm", [P, 1]), sa("ssum", [P, 9])
        yf = pt_s[:, 0:CH, :].rearrange("p c (k t) -> p (c k) t", k=2)
        yo = sa("yo", [P, 64])
        sam.close(); att.close()
        k_landed, v_landed = ([sem(f"{k}_landed{slot_}") for slot_ in range(n)] for k, n in (("k", 2), ("v", 4)))
        pt_in, b_qb, b_s, b_sc, b_own, b_bias, b_exp, b_norm = (sem(f"b_{k}") for k in ("pt", "qb", "s", "sc", "own", "bias", "exp", "norm"))
        b_t, b_tc, b_pv, b_yo, b_vused, b_yt, b_ys = (sem(f"b_{k}") for k in ("t", "tc", "pv", "yo", "vused", "yt", "ys"))
        sw_s, sw_y = sem("sw_s"), sem("sw_y")
        sam_start = sem("sam_start")

        def load_pages(dma, b, c, buf, src, landed, used, count):
            _, pages = nc.values_load_multi_w_load_instructions(ptab[0:1, bass.ds(b * NPG + c * 4, 4)], engines=(dma.engine,),
                                                                min_val=0, max_val=src.shape[0] - 1)
            dma.wait_ge(used, count)
            for k in range(4):
                dma.dma_start(buf[:, c % len(landed), k, :], src[bass.ds(pages[k], 1), :, :].rearrange("o p f -> (o p) f")).then_inc(landed[c % len(landed)], 16)

        def sp_keys(sp):
            sp.wait_ge(sam_start, 1)
            sp.dma_start(ptab[:], io["page_table"]).then_inc(pt_in, 16)
            sp.wait_ge(pt_in, 16)
            with sp.Fori(0, NB) as b:
                for c in range(4):
                    load_pages(sp, b, c, kpg, io["k_pages"], k_landed, b_s, from_one(b * 5 + (c - 1 if c >= 2 else 0)))

        def pool_values(pool):
            pool.wait_ge(pt_in, 16)
            with pool.Fori(0, NB) as b:
                for c in range(4):
                    load_pages(pool, b, c, vpg, io["v_pages"], v_landed, b_vused, b * 4 + (c + 1))


        own_sc = dps[:, 1, 1, 0:TS]

        def pe_scores(pe, b, c):
            if c == CHUNKS:
                pe.wait_ge(b_own, b)
                for m in range(2):
                    mm = pe.matmul(own_sc, qb[:, m, :], ks[:, m, SEQ:T], start=(m == 0), stop=(m == 1))
                mm.then_inc(b_s, 1)
                return
            if c == 0:
                pe.wait_ge(b_qb, b + 1)
            pe.wait_ge(k_landed[c % 2], b * 128 + (c // 2 + 1) * 64)
            pe.wait_ge(b_sc, b * 4 + (c - 1 if c >= 2 else 0))
            for m in range(2):
                mm = pe.matmul(psLE[:, c % 2, :].rearrange("p (k t) -> p k t", k=4), qb[:, m, :],
                               kpg[:, c % 2, :, m * P:(m + 1) * P], start=(m == 0), stop=(m == 1))
            mm.then_inc(b_s, 1)

        def pe_turn(pe, b, q, c):
            if c == CHUNKS:
                pe.wait_ge(b_tc, b * 5 + 3)
                pe.matmul(psA[0:TS, 0:P], sc[:, q, PAST:], ident, start=True, stop=True).then_inc(b_t, 1)
                return
            if c == 0:
                pe.wait_ge(b_norm, b + 1)
            pe.wait_ge(b_tc, b * 5 + (c - 1 if c >= 2 else 0))
            bank = psA if c % 2 == 0 else psY
            for k in range(4):
                mm = pe.transpose(bank[:, k * P:(k + 1) * P], sc[:, q, (c * 4 + k) * P:(c * 4 + k + 1) * P], ident)
            mm.then_inc(b_t, 1)

        def pe_values(pe, b, c):
            out = dps[:, 0, 0, 0:256]
            pe.wait_ge(b_tc, b * 5 + (c + 1))
            if c == CHUNKS:
                pe.matmul(out, pt_own[:], v_new[:], start=False, stop=True).then_inc(b_pv, 1)
                return
            if c == 0:
                pe.wait_ge(b_yo, b)
            pe.wait_ge(v_landed[c], b * 64 + 64)
            for k in range(4):
                mm = pe.matmul(out, pt_s[:, c * 4 + k, :], vpg[:, c, k, :], start=(c == 0 and k == 0), stop=False)
            mm.then_inc(b_vused, 1)

        CHUNKS = NPG // 4
        out_t = dps[0:64, 1, 0, 0:P]

        def pe_out(pe, b):
            pe.wait_ge(b_yo, b + 1)
            pe.matmul(out_t, yo[:], ident, start=True, stop=True).then_inc(b_yt, 1)

        def pe_both(pe, b, q, ahead=True, first=False):
            for step in range(CHUNKS + 3):
                if step == 1 and not first:
                    pe_out(pe, b - 1)
                if ahead and step <= CHUNKS:
                    pe_scores(pe, b + 1, step)
                if 1 <= step <= CHUNKS + 1:
                    pe_turn(pe, b, q, step - 1)
                if step >= 2:
                    pe_values(pe, b, step - 2)

        def act_scores(act, b, q, c):
            act.wait_ge(b_s, from_one(b * 5 + (c + 1)))
            act.activation(sc[:, q, c * 512:(c + 1) * 512], psLE[:, c % 2, :], ACT.Copy).then_inc(b_sc, 1)

        def act_exp(act, b, q):
            act.wait_ge(b_bias, b + 1)
            for n in range(8):
                act.activation(sc[:, q, n * 256:(n + 1) * 256], sc[:, q, n * 256:(n + 1) * 256], ACT.Exp, bias=bias[:, n:n + 1],
                               accum_out=ssum[:, n:n + 1])
            act.activation(sc[:, q, PAST:], sc[:, q, PAST:], ACT.Exp, bias=nm[:, 0:1], accum_out=ssum[:, 8:9]).then_inc(b_exp, 1)

        def act_values(act, b, c):
            if c == 0:
                act.wait_ge(b_pv, b)
            act.wait_ge(b_t, b * 5 + (c + 1))
            if c < CHUNKS:
                bank = psA if c % 2 == 0 else psY
                act.activation(pt_s[:, 4 * c:4 * c + 4, :], bank[:].rearrange("p (k r) -> p k r", k=4), ACT.Copy).then_inc(b_tc, 1)
                return
            act.activation(pt_own[:], psA[0:TS, 0:P], ACT.Copy).then_inc(b_tc, 1)

        def act_both(act, b, q, ahead=True):
            act_exp(act, b, q)
            for step in range(CHUNKS + 2):
                if ahead and step < CHUNKS:
                    act_scores(act, b + 1, 1 - q, step)
                if step >= 1:
                    act_values(act, b, step - 1)

        def dve_queries(dve, b):
            dve.tensor_copy(qb[:], qbd[:].rearrange("p m b c -> p m (b c)")[:, :, bass.ds(b * P, P)]).then_inc(b_qb, 1)

        def dve_scores(dve, link, b, q):
            for c in range(4):
                dve.wait_ge(b_sc, b * 4 + (c + 1))
                blk = sc[:, q, c * 512:(c + 1) * 512].rearrange("p (n k) -> p n k", n=2)
                link(dve.tensor_reduce(gs[:, 2 * c:2 * c + 2], blk, AX, ALU.add))
                link(dve.tensor_reduce(bmx[:, 2 * c:2 * c + 2], blk, AX, ALU.max))
            dve.wait_ge(b_s, from_one(b * 5 + 5))
            mask = cols(cst, CST["own"][0] + (TS - DT) - b * DT, TS)
            dve.tensor_tensor(sc[:, q, PAST:], own_sc, mask, ALU.add).then_inc(b_own, 1)
            dve.wait_ge(b_own, b + 1)
            link(dve.tensor_reduce(bmx[:, 8:9], sc[:, q, PAST:], AX, ALU.max))
            gm = gs[:].rearrange("p (o m) -> p o m", o=1).to_broadcast([P, 8, 8])
            gn = gs[:].rearrange("p (n o) -> p n o", o=1).to_broadcast([P, 8, 8])
            link(dve.tensor_tensor(cmp1[:], gm, gn, ALU.is_gt))
            link(dve.tensor_tensor(cmp2[:], gm, gn, ALU.is_equal))
            link(dve.tensor_tensor(cmp2[:], cmp2[:], c_("blk_lt").rearrange("p (n m) -> p n m", n=8), ALU.mult))
            link(dve.tensor_tensor(cmp1[:], cmp1[:], cmp2[:], ALU.add))
            link(dve.tensor_reduce(rank[:], cmp1[:], AX, ALU.add))
            link(dve.tensor_scalar(bias[:, 0:8], rank[:], 3.0, NEG, ALU.is_ge, ALU.mult))
            link(dve.tensor_tensor(bmx[:, 0:8], bmx[:, 0:8], bias[:, 0:8], ALU.add))
            link(dve.tensor_reduce(nm[:], bmx[:], AX, ALU.max, negate=True))
            dve.tensor_scalar(bias[:, 0:8], bias[:, 0:8], nm[:, 0:1], None, ALU.add).then_inc(b_bias, 1)

        def dve_norm(dve, link, b, q):
            dve.wait_ge(b_exp, b + 1)
            link(dve.tensor_reduce(rank[:, 0:1], ssum[:], AX, ALU.add))
            link(dve.reciprocal(rank[:, 1:2], rank[:, 0:1]))
            dve.tensor_scalar(sc[:, q, :], sc[:, q, :], rank[:, 1:2], None, ALU.mult).then_inc(b_norm, 1)

        def dve_values(dve, b):
            dve.wait_ge(b_pv, b + 1)
            for g in range(4):
                rows = slice(g * 32, g * 32 + 32)
                ins = dve.tensor_copy(yo[rows, :], dps[rows, 0, 0, g * 64:g * 64 + 64])
            ins.then_inc(b_yo, 1)

        def dve_out(dve, b):
            dve.wait_ge(b_yt, b + 1)
            dve.tensor_copy(ys[:, :, bass.ds(b * DT, DT)], out_t.rearrange("p (h t) -> p h t", h=16)).then_inc(b_ys, 1)

        SCORE_LINKS, NORM_LINKS = 17, 2

        def pe_s(pe):
            pe.sem_inc(b_vused, 4)
            for c in range(CHUNKS + 1):
                pe_scores(pe, 0, c)
            pe_both(pe, 0, 0, first=True)
            with pe.Fori(0, NB // 2 - 1) as i:
                for q in (1, 0):
                    pe_both(pe, i * 2 + (2 - q), q)
            pe_both(pe, NB - 1, 1, ahead=False)
            pe_out(pe, NB - 1)
            pe.wait_ge(b_ys, NB)
            pe.matmul(per_tile(psL), c_("swap", 64), ys[:].rearrange("p (k s) t -> p k s t", s=2)[:, :, 1, :],
                      start=True, stop=True).then_inc(sw_s, 1)

        def per_tile(bank):
            return bank.rearrange("p (k t) -> p k t", k=KT)

        def act_s(act):
            act.sem_inc(sam_start, 1)
            for c in range(CHUNKS):
                act_scores(act, 0, 0, c)
            act_both(act, 0, 0)
            with act.Fori(0, NB // 2 - 1) as i:
                for q in (1, 0):
                    act_both(act, i * 2 + (2 - q), q)
            act_both(act, NB - 1, 1, ahead=False)
            act.wait_ge(sw_y, 1)
            act.activation(y_hi[:, :, SEQ:T], yf, ACT.Copy).then_inc(yhi_ready, 1)

        def dve_s(dve):
            link = chains["dve"]
            dve_queries(dve, 0)
            dve_scores(dve, link, 0, 0)
            dve_queries(dve, 1)
            dve_norm(dve, link, 0, 0)
            dve_scores(dve, link, 1, 1)
            dve_values(dve, 0)
            with dve.Fori(0, NB // 2 - 1) as i:
                link.enter(i, 2 * (SCORE_LINKS + NORM_LINKS))
                for q in (1, 0):
                    b = i * 2 + (2 - q)
                    dve_queries(dve, b + 1)
                    dve_norm(dve, link, b, q)
                    dve_out(dve, b - 1)
                    dve_scores(dve, link, b + 1, 1 - q)
                    dve_values(dve, b)
                link.leave(NB // 2 - 1)
            dve_norm(dve, link, NB - 1, 1)
            dve_out(dve, NB - 2)
            dve_values(dve, NB - 1)
            dve_out(dve, NB - 1)
            dve.wait_ge(b_ys, NB)
            dve.wait_ge(sw_s, 1)
            dve.tensor_copy(yf[0:64], ys[:].rearrange("p (k s) t -> p k s t", s=2)[:, :, 0, :])
            dve.tensor_copy(yf[64:P], per_tile(psL)[64:P]).then_inc(sw_y, 1)
            dve.wait_ge(sw_y, 1)
            dve.wait_ge(yhi_ready, KT + 1)
            link(dve.tensor_tensor(y_lo[:, :, SEQ:T], yf, y_hi[:, :, SEQ:T].bitcast(F32), ALU.subtract))
        merge1 = merge_stage("m1")

        mm_ = ExitStack()
        ms = lambda n, s, d=F32: stage_sb(mm_, n, s, d)
        km = ms("km", [P, KT, MEM])
        vm = ms("vm", [P, 2, D])
        mk = ExitStack()
        memx = stage_sb(mk, "memx", [P, KT, MEM])
        vmt = stage_sb(mk, "vmt", [P, KT, MEM])
        mem_in, memkv_out = sem("mem_in"), sem("memkv_out")
        normm = norm_stage("normm", memx, "memn", y_hi, y_lo, width=MEM, ready={0: ((mem_in, 16),)})
        mk.close()
        n_mem = take(2 * KT)
        mem_ready = (norm_lo, (norm_count[0] - 1) * KT + 1)
        vmt_full, vmt_copied = sem("vmt_full"), sem("vmt_copied")

        def pe_mem(pe):
            pe_dense(pe, slot(n_mem, 1), y_hi, y_lo, width=MEM)
            with pe.Fori(1, KT) as i:
                for u in range(2):
                    pe_dense(pe, slot(n_mem, u, i, 2), y_hi, y_lo, width=MEM)
            for par in range(2):
                pe.wait_ge(dense_free[par], (n_mem + 2 * KT) // 2 if (n_mem % 2 == 0) else (n_mem + 2 * KT + 1 - par) // 2)
            for kt in range(2):
                for j in range(KT):
                    r = kt * 2 + j // 4
                    if j % 4 == 0 and r >= 2:
                        pe.wait_ge(vmt_copied, r - 1)
                    bank = psA if r % 2 == 0 else psY
                    mm = pe.transpose(bank[:, (j % 4) * P:(j % 4 + 1) * P], vmt[:, j, kt * P:(kt + 1) * P], ident)
                    if j % 4 == 3:
                        mm.then_inc(vmt_full, 1)

        def act_mem(act):
            for dst in (km, vmt):
                base = n_mem if dst is km else n_mem + KT
                with act.Fori(0, KT // 2) as i:
                    for u in range(2):
                        par, k0 = slot(base, u, i, 2)
                        act.wait_ge(dense_full[par], from_one(k0 + 1))
                        act.activation(dst[:].rearrange("p k t -> p (k t)")[:, bass.ds((i * 2 + u) * MEM, MEM)],
                                       dps[:, par, 0, 0:MEM], ACT.Copy).then_inc(dense_free[par], 1)
            for par in range(2):
                act.wait_ge(dense_free[par], (n_mem + 2 * KT + 1 - par) // 2)
            act.dma_start(io["memkv_t"][:, 0:KT, :], km[:]).then_inc(memkv_out, 16)
            act.dma_start(io["memkv_t"][:, KT:2 * KT, :], vmt[:]).then_inc(memkv_out, 16)
            act.wait_ge(memkv_out, 32)

        def dve_mem(dve):
            for r in range(4):
                dve.wait_ge(vmt_full, r + 1)
                bank = psA if r % 2 == 0 else psY
                dve.tensor_copy(vm[:, r // 2, (r % 2) * 512:(r % 2) * 512 + 512], bank[:]).then_inc(vmt_copied, 1)

        mh = ExitStack()
        ms2 = lambda n, s, d=F32: stage_sb(mh, n, s, d)
        kc = ms2("kc", [P, NB, 2, MEM])
        vc = ms2("vc", [P, NB, 2, MEM])
        qh2 = ms2("qh", [P, 2, 2, T])
        vh = ms2("vh", [P, 2, MEM])
        mp = ms2("mp", [P, 3, MEM])
        mpt = ms2("mpt", [P, 2, SEQ])
        apart = ms2("apart", [P, 2, NB * (TS + DT)])
        mo = ms2("mo", [TS, MEM])
        mfix = ms2("mfix", [P, 2, TS])
        mnm, msum, mrc = ms2("mnm", [P, 3]), ms2("msum", [P, 3]), ms2("mrc", [P, 3])
        mh.close(); mm_.close()
        n_qm = take(KT)
        h_v, h_s, h_max, h_exp, h_norm, h_a, h_ac = (sem(f"h_{k}") for k in ("v", "s", "max", "exp", "norm", "a", "ac"))
        h_pv, h_hi, h_lo, kc_in, vc_in = (sem(f"h_{k}") for k in ("pv", "hi", "lo", "kc", "vc"))
        h_hi2, h_apart, apart_clear = sem("h_hi2"), sem("h_apart"), sem("apart_clear")
        NQ, AHEAD = CH + 1, 2

        def h_bank(i):
            return (psL, psE, psY[:])[i % 3]

        def pe_scores_h(pe, h, q, i):
            bank = h_bank(i)
            pe.wait_ge(h_exp, from_one(h * NQ + max(i - 2, 0)))
            if i == 2:
                pe.wait_ge(h_lo, from_one(h * 2))
            if i < CH:
                for kt in range(2):
                    mm = pe.matmul(bank[:, 0:MEM], qh2[:, q, kt, i * P:(i + 1) * P],
                                   cols(flat(km), h * (2 * MEM) + kt * MEM, MEM), start=(kt == 0), stop=(kt == 1))
            else:
                pe.wait_ge(h_apart, h + 1)
                pe.wait_ge(kc_in, h * 16 + 16)
                for b in range(NB):
                    for kt in range(2):
                        mm = pe.matmul(bank[0:TS, 0:MEM], apart[:, kt, b * TS:(b + 1) * TS], kc[:, b, kt, :],
                                       start=(b == 0 and kt == 0), stop=(b == NB - 1 and kt == 1))
            mm.then_inc(h_s, 1)

        def turn(pe, h, i):
            m = P if i < CH else TS
            pe.wait_ge(h_ac, from_one(h * 7 + i))
            pe.wait_ge(h_norm, h * NQ + (i + 1))
            for kk in range(2):
                mm = pe.matmul(psA[:, kk * P:kk * P + m], mp[0:m, i % 3, kk * P:(kk + 1) * P],
                               cst[0:m, CST["ident"][0]:CST["ident"][0] + m], start=True, stop=True)
            mm.then_inc(h_a, 1)

        def pe_head(pe, h, q, ahead):
            for u in range(2):
                par, k0 = slot(n_qm, u, h, 2)
                pe.wait_ge(dense_free[par], k0 + 1)
            for i in range(AHEAD):
                pe_scores_h(pe, h, q, i)
            for i in range(NQ):
                if i + AHEAD < NQ:
                    pe_scores_h(pe, h, q, i + AHEAD)
                turn(pe, h, i)
                if ahead and i in (0, 2):
                    pe_dense(pe, slot(n_qm, i // 2, h + 1, 2), xn_hi, xn_lo)
            pe.wait_ge(h_ac, from_one(h * 7 + 5))
            pe.wait_ge(h_v, h + 1)
            for dt in range(2):
                if dt:
                    pe.wait_ge(h_lo, from_one(h * 2 + 1))
                for kt in range(2):
                    mm = pe.matmul(psY[:], vh[:, kt, dt * P:(dt + 1) * P], mpt[:, kt, 0:SEQ], start=(kt == 0), stop=(kt == 1))
                mm.then_inc(h_pv, 1)
                if dt:
                    continue
                pe.wait_ge(vc_in, h * 16 + 16)
                for b in range(NB):
                    for kt in range(2):
                        mm = pe.matmul(psA[0:TS, 0:MEM], apart[:, kt, b * TS:(b + 1) * TS], vc[:, b, kt, :],
                                       start=(b == 0 and kt == 0), stop=(b == NB - 1 and kt == 1))
                mm.then_inc(h_a, 1)
            pe.wait_ge(h_ac, from_one(h * 7 + 6))
            for d2 in range(2):
                mm = pe.matmul(psA[:, d2 * TS:(d2 + 1) * TS], mo[:, d2 * P:(d2 + 1) * P], cst[0:TS, CST["ident"][0]:CST["ident"][0] + TS],
                               start=True, stop=True)
            mm.then_inc(h_a, 1)

        def pe_h(pe):
            with pe.Fori(0, 2) as j:
                for u in range(2):
                    pe_dense(pe, slot(n_qm, u, j * 2, 2), xn_hi, xn_lo)
                for q in range(2):
                    pe_head(pe, j * 2 + q, q, q == 0)

        def untile(act, h, i):
            act.wait_ge(h_a, from_one(h * 7 + (i + 1)))
            turned = psA[:, 0:2 * P].rearrange("p (k q) -> p k q", k=2)
            dst = mpt[:, :, i * P:(i + 1) * P] if i < CH else apart_own
            src = turned if i < CH else turned[:, :, 0:TS].rearrange("p k (b t) -> p k b t", b=NB)
            act.activation(dst, src, ACT.Copy).then_inc(h_ac, 1)

        apart_own = apart[:].rearrange("p k (b w) -> p k b w", b=NB)[:, :, :, 0:DT]

        def load_head(act, h, buf, src, landed):
            act.dma_start(buf[:], src[bass.ds(h * P, P), :].rearrange("p (b k t) -> p b k t", b=NB, k=2)).then_inc(landed, 16)

        def act_queries_h(act, h, q, u):
            par, k0 = slot(n_qm, u, h, 2)
            act.wait_ge(dense_full[par], from_one(k0 + 1))
            act.activation(two(qh2[:, q, u, :]), dps[:, par, :, 0:HALF], ACT.Copy, scale=0.0625).then_inc(dense_free[par], 1)

        def act_exp_h(act, h, i):
            m = P if i < CH else TS
            act.wait_ge(h_max, h * NQ + (i + 1))
            act.activation(mp[0:m, i % 3, :], h_bank(i)[0:m, 0:MEM], ACT.Exp, bias=mnm[0:m, i % 3:i % 3 + 1],
                           accum_out=msum[0:m, i % 3:i % 3 + 1]).then_inc(h_exp, 1)

        def act_head(act, h, q, ahead):
            act.wait_ge(h_a, from_one(h * 7))
            for u in range(2):
                par, k0 = slot(n_qm, u, h, 2)
                act.wait_ge(dense_free[par], k0 + 1)
            act.activation(apart_own, qh2[:, q, :, SEQ:T].rearrange("p k (b t) -> p k b t", b=NB), ACT.Copy).then_inc(h_apart, 1)
            for i in range(AHEAD):
                act_exp_h(act, h, i)
            for i in range(NQ):
                if i + AHEAD < NQ:
                    act_exp_h(act, h, i + AHEAD)
                untile(act, h, i)
                if ahead and i + AHEAD == CH:
                    load_head(act, h + 1, kc, io["mem_kt"], kc_in)
                if i == 0:
                    act.wait_ge(h_pv, from_one(h * 2))
                    act.activation(vh[:], vm[:, :, bass.ds(h * MEM, MEM)], ACT.Copy).then_inc(h_v, 1)
                if ahead and i in (1, 3):
                    act_queries_h(act, h + 1, 1 - q, i // 2)
            for dt in range(2):
                act.wait_ge(h_pv, from_one(h * 2 + (dt + 1)))
                act.activation(cols(flat(y_hi), (h * 2 + dt) * T, SEQ), psY[:], ACT.Copy).then_inc(h_hi, 1)
                if dt:
                    continue
                act.wait_ge(h_a, from_one(h * 7 + 6))
                act.activation(mo[:], psA[0:TS, 0:MEM], ACT.Copy).then_inc(h_ac, 1)
                if ahead:
                    load_head(act, h + 1, vc, io["mem_v"], vc_in)
            act.wait_ge(h_a, from_one(h * 7 + 7))
            act.activation(mfix[:], psA[:, 0:2 * TS].rearrange("p (k t) -> p k t", k=2), ACT.Copy).then_inc(h_ac, 1)
            act.wait_ge(h_ac, from_one(h * 7 + 7))
            for d2 in range(2):
                act.activation(cols(flat(y_hi), (h * 2 + d2) * T + SEQ, TS), mfix[:, d2, :], ACT.Copy).then_inc(h_hi2, 1)

        def act_h(act):
            with act.Fori(0, 2) as j:
                act.wait_ge(h_a, from_one(j * 14))
                load_head(act, j * 2, kc, io["mem_kt"], kc_in)
                load_head(act, j * 2, vc, io["mem_v"], vc_in)
                for u in range(2):
                    act_queries_h(act, j * 2, 0, u)
                for q in range(2):
                    act_head(act, j * 2 + q, q, q == 0)

        def dve_max_h(dve, h, i):
            m = P if i < CH else TS
            dve.wait_ge(h_s, h * NQ + (i + 1))
            if i >= 3:
                dve.wait_ge(h_exp, from_one(h * NQ + (i - 2)))
            dve.tensor_reduce(mnm[0:m, i % 3:i % 3 + 1], h_bank(i)[0:m, 0:MEM], AX, ALU.max, negate=True).then_inc(h_max, 1)

        def dve_h(dve):
            link = chains["dve"]
            with dve.Fori(0, 2) as j:
                link.enter(j, 2 * (NQ + 2))
                for q in range(2):
                    h = j * 2 + q
                    for i in range(AHEAD):
                        dve_max_h(dve, h, i)
                    for i in range(NQ):
                        m = P if i < CH else TS
                        if i + AHEAD < NQ:
                            dve_max_h(dve, h, i + AHEAD)
                        dve.wait_ge(h_exp, from_one(h * NQ + (i + 1)))
                        link(dve.reciprocal(mrc[0:m, i % 3:i % 3 + 1], msum[0:m, i % 3:i % 3 + 1]))
                        dve.tensor_scalar(mp[0:m, i % 3, :], mp[0:m, i % 3, :], mrc[0:m, i % 3:i % 3 + 1], None, ALU.mult).then_inc(h_norm, 1)
                    for dt in range(2):
                        dve.wait_ge(h_hi, h * 2 + (dt + 1))
                        o = (h * 2 + dt) * T
                        dve.tensor_tensor(cols(flat(y_lo), o, SEQ), psY[:], cols(flat(y_hi), o, SEQ).bitcast(F32), ALU.subtract).then_inc(h_lo, 1)
                    for dt in range(2):
                        dve.wait_ge(h_hi2, h * 2 + (dt + 1))
                        o = (h * 2 + dt) * T + SEQ
                        link(dve.tensor_tensor(cols(flat(y_lo), o, TS), mfix[:, dt, :], cols(flat(y_hi), o, TS).bitcast(F32), ALU.subtract))
            link.leave(2)
        merge2 = merge_stage("m2")

        hs = ExitStack()
        h_res = stage_sb(hs, "h_res", [P, KT, T])
        sq2, acc = stage_sb(hs, "sq2", [P, 2, T]), stage_sb(hs, "acc", [P, T])
        ftails = stage_sb(hs, "ftails", [P, 2 * FT, FPAD + NB * FPAD])
        h_in, mg_hi, wo_done = sem("h_in"), sem("mg_hi"), sem("wo_done")
        n_wo = take(KT)

        def pe_residual(pe, n0, hi, lo, nk):
            with pe.Fori(0, KT // 2) as i:
                for u in range(2):
                    pe_dense(pe, slot(n0, u, i, 2), hi, lo, nk=nk)

        def dve_residual(dve, n0, link=None, done=None):
            if link:
                link(dve.memset(acc[:], 0.0))
            with dve.Fori(0, KT // 2) as i:
                for u in range(2):
                    par, k0 = slot(n0, u, i, 2)
                    dve.wait_ge(dense_full[par], from_one(k0 + 1))
                    hv = two(cols(flat(h_res), (i * 2 + u) * T, T))
                    dve.tensor_tensor(hv, hv, dps[:, par, :, 0:HALF], ALU.add).then_inc(dense_free[par], 1)
                    if link:
                        dve.wait_ge(norm_sems[0], i * 2 + (done + u + 1))
                        dve.tensor_tensor(acc[:], acc[:], sq2[:, u, :], ALU.add).then_inc(norm_sems[1], 1)
                        dve.wait_ge(norm_sems[1], i * 2 + (done + u + 1))

        def act_squares(act, n0, done):
            with act.Fori(0, KT // 2) as i:
                for u in range(2):
                    par, k0 = slot(n0, u, i, 2)
                    act.wait_ge(norm_sems[1], i * 2 + (done + u - 1))
                    act.wait_ge(dense_free[par], k0 + 1)
                    act.activation(sq2[:, u, :], cols(flat(h_res), (i * 2 + u) * T, T), ACT.Square).then_inc(norm_sems[0], 1)

        def act_wo(act):
            act.dma_start(h_res[:], io["x_t"]).then_inc(h_in, 16)
            for k in range(KT):
                act.activation(xn_hi[:, k, :], merged[:, k, :], ACT.Copy, scale=0.5).then_inc(mg_hi, 1)

        def dve_wo(dve):
            link = chains["dve"]
            for k in range(KT):
                dve.wait_ge(mg_hi, k + 1)
                dve.scalar_tensor_tensor(xn_lo[:, k, :], merged[:, k, :], 0.5, xn_hi[:, k, :].bitcast(F32), ALU.mult, ALU.subtract).then_inc(wo_done, 1)
            dve.wait_ge(h_in, 16)
        done_wo = norm_count[0] * KT

        norm2 = norm_stage("norm2", h_res, "norm2", xn_hi, xn_lo, summed=acc)
        n_ffn, ffn_ready = nstream[0], (norm_lo, (norm_count[0] - 1) * KT + 1)
        fs = ExitStack()
        ff = lambda n, s, d=F32: stage_sb(fs, n, s, d)
        fin = ff("fin", [P, 2, FW])
        fout = ff("fout", [P, 2, FW])
        fth = ff("fth", [P, FW])
        fg = ff("fg", [P, FW])
        fa = ff("fa", [P, T])
        fs.close()
        f_conv, f_th, f_a, f_hi = sem("f_conv"), sem("f_th"), sem("f_a"), sem("f_hi")
        FO = FW - FPAD

        f_lo = sem("f_lo")

        def pe_pair(pe, n0, i):
            for u in range(2):
                pe_dense(pe, slot(n0, u, i, 2), xn_hi, xn_lo)

        def act_front(act, n0, i, j):
            for u in range(2):
                par, k0 = slot(n0, u, i, 2)
                act.wait_ge(dense_full[par], from_one(k0 + 1))
                act.wait_ge(f_conv, from_one(j * 2 + u))
                fb = fin[:, u, :]
                k = FPAD + NB * FPAD
                tl = cols(flat(ftails), j * k + u * FT * k, k)
                sample = by_seq(dps[:, par, 1, SEQ - HALF:HALF])
                act.activation(fb[:, FPAD:FPAD + HALF], dps[:, par, 0, 0:HALF], ACT.Copy)
                act.activation(fb[:, FPAD + HALF:FPB], dps[:, par, 1, 0:SEQ - HALF], ACT.Copy)
                act.activation(by_seq(tl[:, FPAD:k]), sample[:, :, DT - FPAD:DT], ACT.Copy)
                act.activation(tl[:, 0:FPAD], dps[:, par, 1, SEQ - HALF - FPAD:SEQ - HALF], ACT.Copy)
                act.activation(by_seq(fb[:, FPB:FW])[:, :, FPAD:FSB], sample, ACT.Copy).then_inc(dense_free[par], 1)
            act.wait_ge(f_conv, from_one(j * 2 + 1))
            act.wait_ge(f_a, from_one(j))
            act.activation(fth[:, 0:FO], fout[:, 0, 0:FO], ACT.Tanh).then_inc(f_th, 1)

        def act_back(act, j, at):
            act.wait_ge(f_a, from_one(j + 1))
            act.activation(cols(flat(y_hi), at * T, T), fa[:], ACT.Copy).then_inc(f_hi, 1)

        def dve_front(dve, link, n0, i, j):
            for u in range(2):
                par, k0 = slot(n0, u, i, 2)
                dve.wait_ge(dense_free[par], k0 + 1)
                fb, fo = fin[:, u, :], fout[:, u, 0:FO]
                w = lambda k: cols(fea, j * FCONV + (FEA["fconvw"][0] + u * FT * FCONV + k))
                link(dve.tensor_copy(by_seq(fb[:, FPB:FW])[:, :, 0:FPAD],
                                     by_seq(cols(fea, j * (NB * FPAD) + (FEA["fhist"][0] + u * FT * NB * FPAD), NB * FPAD))))
                link(dve.tensor_scalar(fo, fb[:, 0:FO], w(0), cols(fea, j + (FEA["fconvb"][0] + u * FT)), ALU.mult, ALU.add))
                for k in range(1, FCONV):
                    ins = dve.scalar_tensor_tensor(fo, fb[:, k:k + FO], w(k), fo, ALU.mult, ALU.add)
                    if k < FCONV - 1:
                        link(ins)
                ins.then_inc(f_conv, 1)
            dve.wait_ge(f_conv, from_one(j * 2 + 2))
            dve.wait_ge(f_th, j + 1)
            link(dve.scalar_tensor_tensor(fg[:, 0:FO], fth[:, 0:FO], 1.0, fout[:, 0, 0:FO], ALU.add, ALU.mult))
            seqs = lambda a: by_seq(a[:, FPB:FW])[:, :, 0:DT]
            dve.wait_ge(f_hi, from_one(j))
            dve.tensor_tensor(fa[:, 0:SEQ], fg[:, 0:SEQ], fout[:, 1, 0:SEQ], ALU.mult)
            dve.tensor_tensor(by_seq(fa[:, SEQ:T]), seqs(fg), seqs(fout[:, 1, :]), ALU.mult).then_inc(f_a, 1)

        def dve_back(dve, j, at):
            dve.wait_ge(f_hi, from_one(j + 1))
            dve.tensor_tensor(cols(flat(y_lo), at * T, T), fa[:], cols(flat(y_hi), at * T, T).bitcast(F32), ALU.subtract).then_inc(f_lo, 1)
            dve.wait_ge(f_lo, j + 1)

        def ffn_part(j0, count, first, ahead):
            skip = 0 if first else 1
            n_up = take(2 * (count - skip))
            n_ahead = take(2) if ahead else None
            n_down = take(KT)
            loops = count - skip
            done = norm_count[0] * KT

            def pe_f(pe):
                if first:
                    pe_dense(pe, slot(n_up, 1), xn_hi, xn_lo)
                with pe.Fori(int(first), loops) as i:
                    pe_pair(pe, n_up, i)
                if ahead:
                    pe_pair(pe, n_ahead, 0)
                pe.wait_ge(f_lo, j0 + count)
                pe_residual(pe, n_down, y_hi, y_lo, count)

            def act_f(act):
                with act.Fori(0, loops) as i:
                    act_front(act, n_up, i, i + (j0 + skip))
                    act_back(act, i + (j0 + skip), i + skip)
                if ahead:
                    act_front(act, n_ahead, 0, j0 + count)
                    for u in range(2):
                        par, k0 = slot(n_down, KT - 2 + u)
                        act.wait_ge(dense_full[par], from_one(k0 + 1))
                    act_back(act, j0 + count, 0)
                else:
                    act_squares(act, n_down, done)

            def dve_f(dve):
                link = chains["dve"]
                with dve.Fori(0, loops) as i:
                    link.enter(i, 2 * FCONV + 1)
                    dve_front(dve, link, n_up, i, i + (j0 + skip))
                    dve_back(dve, i + (j0 + skip), i + skip)
                    link.leave(loops)
                if ahead:
                    dve_front(dve, link, n_ahead, 0, j0 + count)
                dve_residual(dve, n_down, *(() if ahead else (link, done)))
                if ahead:
                    dve_back(dve, j0 + count, 0)
            return Stage(pe_f, act_f, dve_f)

        ffn = [ffn_part(sum(FFN_PIECES[:part]), count, part == 0, part < len(FFN_PIECES) - 1)
               for part, count in enumerate(FFN_PIECES)]

        fo_ = ExitStack()
        yt = stage_sb(fo_, "yt", [P, KT, T])
        normf = norm_stage("normf", h_res, "final", None, None, plain=yt, summed=acc)
        fo_.close()
        hs.close()
        y_from = (norm_count[0] - 1) * KT

        def act_out(act):
            act.dma_start(io["ftails"], ftails[:].rearrange("p n k -> p (n k)")).then_inc(out_done, 16)
            for part in range(4):
                act.wait_ge(norm_sems[5], y_from + 2 * part + 2)
                at = slice(2 * part, 2 * part + 2)
                act.dma_start(io["y_t"][:, at, :], yt[:, at, :]).then_inc(out_done, 16)
        final_waits = [(ssm_out, from_one(GROUPS * 32)), (kv_out, 32), (memkv_out, 32), (out_done, 96)]

        block = ctx.enter_context(nc.Block())
        n_tiles = nstream[0]
        ahead_of_pages = (n_pages_at + 2) // 2

        def load(sp, i, par):
            sp.wait_ge(w_split[par], from_one(i))
            sp.dma_start(w_raw[:, par, :], io["wstream"][bass.ds(i * 2 + par, 1), :, :].rearrange("o p c -> (o p) c")).then_inc(w_landed[par], 16)

        def split(pool, i, par):
            pool.wait_ge(dense_full[par], from_one(i))
            pool.wait_ge(w_landed[par], i * 16 + 16)
            pool.sem_inc(w_taken, 1)
            pool.tensor_scalar(w_hi[:, par, :], w_raw[:, par, :], 1.0, 1.0, ALU.mult, ALU.mult).then_inc(w_hi_done, 1)
            pool.wait_ge(w_hi_done, i * 2 + (par + 1))
            pool.tensor_tensor(w_lo[:, par, :], w_raw[:, par, :], w_hi[:, par, :].bitcast(F32), ALU.subtract).then_inc(w_split[par], 1)

        @block.sync
        def _(sp):
            with sp.Fori(0, ahead_of_pages) as i:
                for par in range(2):
                    load(sp, i, par)
            sp_keys(sp)
            with sp.Fori(ahead_of_pages, n_tiles // 2) as i:
                for par in range(2):
                    load(sp, i, par)
            if n_tiles % 2:
                load(sp, n_tiles // 2, 0)
            for written, count in final_waits:
                sp.wait_ge(written, count)

        @block.gpsimd
        def _(pool):
            pool.sem_inc(w_split[0], 1)
            pool.sem_inc(w_split[1], 1)
            with pool.Fori(0, ahead_of_pages) as i:
                for par in range(2):
                    split(pool, i, par)
            pool_values(pool)
            with pool.Fori(ahead_of_pages, n_tiles // 2) as i:
                for par in range(2):
                    split(pool, i, par)
            if n_tiles % 2:
                split(pool, n_tiles // 2, 0)

        @block.tensor
        def _(pe):
            pe.sem_inc(b_s, 1)
            pe.sem_inc(dense_full[0], 1)
            pe.sem_inc(dense_full[1], 1)
            pe.sem_inc(h_a, 1)
            pe.sem_inc(h_pv, 1)
            pe.sem_inc(pv_full, 1)
            pe.wait_ge(cst_in, 16)
            norm1.pe(pe)
            pe_dense(pe, slot(0, 0), xn_hi, xn_lo, ready=(norm_lo, 1))
            stage_end(pe, 0, 1)
            pe_dt(pe)
            pe_half0(pe)
            stage_end(pe, 0, 2)
            pe_c(pe)
            stage_end(pe, 0, 3)
            pe_half1(pe)
            stage_end(pe, 0, 4)
            merge0.pe(pe)
            stage_end(pe, 0, 5)
            pe_kv(pe)
            stage_end(pe, 0, 6)
            pe_q(pe)
            stage_end(pe, 0, 7)
            pe_s(pe)
            stage_end(pe, 0, 8)
            merge1.pe(pe)
            stage_end(pe, 0, 9)
            normm.pe(pe)
            pe_dense(pe, slot(n_mem, 0), y_hi, y_lo, width=MEM, ready=mem_ready)
            stage_end(pe, 0, 10)
            pe_mem(pe)
            stage_end(pe, 0, 11)
            pe_h(pe)
            stage_end(pe, 0, 12)
            merge2.pe(pe)
            stage_end(pe, 0, 13)
            pe.wait_ge(wo_done, KT)
            pe_residual(pe, n_wo, xn_hi, xn_lo, KT)
            stage_end(pe, 0, 14)
            norm2.pe(pe)
            pe_dense(pe, slot(n_ffn, 0), xn_hi, xn_lo, ready=ffn_ready)
            stage_end(pe, 0, 15)
            for part in ffn:
                part.pe(pe)
            stage_end(pe, 0, 16)
            normf.pe(pe)

        @block.scalar
        def _(act):
            act.sem_inc(f_hi, 1)
            act.sem_inc(h_ac, 1)
            act.sem_inc(h_exp, 1)
            act.sem_inc(ssm_out, 1)
            act.sem_inc(t_copied, 1)
            chains["act"] = Chain(act, act_step)
            act_load(act)
            norm1.act(act)
            stage_end(act, 1, 1)
            act_dt(act)
            act_half0(act)
            stage_end(act, 1, 2)
            act_c(act)
            stage_end(act, 1, 3)
            act_half1(act)
            act_states_out(act)
            stage_end(act, 1, 4)
            merge0.act(act)
            stage_end(act, 1, 5)
            act_kv(act)
            stage_end(act, 1, 6)
            act_q(act)
            stage_end(act, 1, 7)
            act_s(act)
            stage_end(act, 1, 8)
            merge1.act(act)
            stage_end(act, 1, 9)
            act.dma_start(memx[:], io["mem_t"]).then_inc(mem_in, 16)
            normm.act(act)
            stage_end(act, 1, 10)
            act_mem(act)
            stage_end(act, 1, 11)
            act.wait_ge(apart_clear, 1)
            act_h(act)
            stage_end(act, 1, 12)
            merge2.act(act)
            stage_end(act, 1, 13)
            act_wo(act)
            act_squares(act, n_wo, done_wo)
            stage_end(act, 1, 14)
            norm2.act(act)
            stage_end(act, 1, 15)
            for part in ffn:
                part.act(act)
            stage_end(act, 1, 16)
            normf.act(act)
            act_out(act)

        @block.vector
        def _(dve):
            dve.sem_inc(a_free, 1)
            dve.sem_inc(f_a, 1)
            dve.sem_inc(f_conv, 1)
            dve.sem_inc(gmean_ready, 1)
            dve.sem_inc(h_lo, 1)
            dve.sem_inc(y_free, 1)
            dve.sem_inc(ylo_ready, 1)
            chains["dve"] = Chain(dve, dve_step)
            norm1.dve(dve)
            stage_end(dve, 2, 1)
            chains["dve"](dve.memset(cbuf[:, :, 0:PAD], 0.0))
            dve_dt(dve)
            dve_half0(dve)
            stage_end(dve, 2, 2)
            stage_end(dve, 2, 3)
            dve_half1(dve)
            stage_end(dve, 2, 4)
            merge0.dve(dve)
            stage_end(dve, 2, 5)
            dve_kv(dve)
            stage_end(dve, 2, 6)
            dve_q(dve)
            stage_end(dve, 2, 7)
            dve_s(dve)
            stage_end(dve, 2, 8)
            merge1.dve(dve)
            stage_end(dve, 2, 9)
            normm.dve(dve)
            stage_end(dve, 2, 10)
            dve_mem(dve)
            stage_end(dve, 2, 11)
            dve.memset(apart[:], 0.0).then_inc(apart_clear, 1)
            dve_h(dve)
            stage_end(dve, 2, 12)
            merge2.dve(dve)
            stage_end(dve, 2, 13)
            dve_wo(dve)
            dve_residual(dve, n_wo, chains["dve"], done_wo)
            stage_end(dve, 2, 14)
            norm2.dve(dve)
            stage_end(dve, 2, 15)
            chains["dve"](dve.memset(fin[:, :, 0:FPAD], 0.0))
            for part in ffn:
                part.dve(dve)
            stage_end(dve, 2, 16)
            normf.dve(dve)


def weight_stream(w_in, w_ssd_out, w_attn_out, w_mem_kv, w_mem_out, w_o, w_up, w_down):
    tiles = []

    def add(w, column, row=0):
        tile = np.zeros((D, P), w.dtype)
        block = w[row:row + D, column:column + P]
        tile[:block.shape[0], :block.shape[1]] = block
        tiles.append(tile.reshape(KT, P, P).transpose(1, 0, 2).reshape(P, D))

    inner = 2 * D
    x_at, b_at, c_at, dt_at = inner, 2 * inner, 2 * inner + D, 2 * inner + 2 * D
    q_at = dt_at + HEADS
    k_at, v_at = q_at + D, q_at + D + 256
    qm_at = v_at + 256
    gate_at = qm_at + D

    def groups(which):
        for g in which:
            for column in (x_at + g * 256, x_at + g * 256 + P, b_at + g * P, c_at + g * P, g * 256, g * 256 + P):
                add(w_in, column)

    def branch(number, w, row=0, ahead=0):
        for m in range(ahead):
            add(w_in, gate_at + number * D + m * P)
        for m in range(KT):
            if m >= ahead:
                add(w_in, gate_at + number * D + m * P)
            add(w, m * P, row)

    add(w_in, dt_at)
    groups(range(5))
    for m in range(KT):
        add(w_ssd_out, m * P)
    groups(range(5, GROUPS))
    branch(0, w_ssd_out, D, N_GRP)
    for column in (k_at, k_at + P, v_at, v_at + P):
        add(w_in, column)
    for m in range(KT):
        add(w_in, q_at + m * P)
    branch(1, w_attn_out)
    for m in range(2 * KT):
        add(w_mem_kv, m * P)
    for m in range(KT):
        add(w_in, qm_at + m * P)
    branch(2, w_mem_out)
    for m in range(KT):
        add(w_o, m * P)
    j = 0
    for piece, count in enumerate(FFN_PIECES):
        first, last = piece == 0, piece == len(FFN_PIECES) - 1
        for _ in range(count + first - last):
            add(w_up, j * P)
            add(w_up, (FT + j) * P)
            j += 1
        for m in range(KT):
            add(w_down, m * P, piece * D)
    return np.stack(tiles)


def constants():
    out = np.zeros((P, CST_W), np.float32)

    def put(name, a):
        at, _ = CST[name]
        out[:a.shape[0], at:at + a.shape[1]] = a

    i, s, e, b = np.arange(P), np.arange(TS), np.arange(DT), np.arange(NB)
    same = s[:, None] // DT == s[None] // DT
    put("ident", np.eye(P))
    put("ones", np.ones((P, P)))
    put("upto_p", i[:, None] <= i[None])
    put("after_p", i[:, None] > i[None])
    put("upto_s", same & (s[:, None] <= s[None]))
    put("after_s", same & (s[:, None] > s[None]))
    put("same_b", s[:, None] // DT == b[None])
    rot, swap = np.zeros((P, P)), np.zeros((P, P))
    for head in (0, 64):
        rot[head + 8 + e, head + e] = -1
        rot[head + e, head + 8 + e] = 1
    swap[i, (i + 64) % P] = 1
    put("rot", rot)
    put("swap", swap)
    put("causal", np.where(i[:, None] >= i[None], 0, NEG))
    at = np.arange(2 * TS - DT)[None] - (TS - DT)
    put("own", np.where((at >= 0) & (at < DT) & (i[:, None] % DT >= at), 0, NEG))
    put("blk_lt", np.tile((b[None] < b[:, None]).reshape(1, NB * NB), (P, 1)))
    position = np.concatenate([np.arange(SEQ), np.tile(PAST + e, NB)]).astype(np.float32)
    inverse = np.float32(500000.0) ** (-e.astype(np.float32) * np.float32(2) / np.float32(16))
    angle = (inverse.astype(np.float32)[:, None] * position[None]).astype(np.float32)
    cos, sin = np.ones((P, T)), np.zeros((P, T))
    for row in (0, 8, 64, 72):
        cos[row:row + 8], sin[row:row + 8] = np.cos(angle), np.sin(angle)
    put("cos", cos)
    put("sin", sin)
    return out


def features_down(a):
    return np.ascontiguousarray(a.T.reshape(-1, P, a.shape[0]).transpose(1, 0, 2))


def tokens_down(a):
    return a.transpose(2, 1, 0).reshape(a.shape[2], -1)


def per_feature(inp):
    out = np.zeros((P, FEA_W), np.float32)

    def put(name, a):
        at, _ = FEA[name]
        a = a.reshape(a.shape[0], -1)
        out[:a.shape[0], at:at + a.shape[1]] = a

    def column(a):
        return a.reshape(-1, P).T

    def rows(a, tiles):
        return a.reshape(-1, tiles, P).transpose(2, 1, 0)

    put("norm1", column(inp["norm1_w"][0]))
    put("norm2", column(inp["norm2_w"][0]))
    put("memn", column(inp["mem_norm_w"][0]))
    put("final", column(inp["final_norm_w"]))
    put("ssdn", column(inp["ssd_norm_w"][0]))
    put("dskip", column(np.repeat(inp["d_skip"][0], 64)))
    put("dtb", inp["dt_bias"][0][:, None])
    put("alog", inp["a_log"][0][:, None])
    put("convw", rows(inp["ssd_conv_w"][0], NCV))
    put("convb", column(inp["ssd_conv_b"][0]))
    put("hist", rows(inp["state_conv"][0].reshape(NB * PAD, -1), NCV))
    put("fconvw", rows(inp["ffn_conv_w"][0], 2 * FT))
    put("fconvb", column(inp["ffn_conv_b"][0]))
    put("fhist", rows(inp["state_ffn_conv"][0].reshape(NB * FPAD, -1), 2 * FT))
    return out


def kernel(**inputs):
    import concourse.bacc as _bacc
    from concourse.bass_utils import run_bass_kernel_spmd as _run

    inp = {name: np.asarray(a) for name, a in inputs.items()}
    data = {
        "wstream": weight_stream(*(inp[name][0] for name in ("w_in", "w_ssd_out", "w_attn_out", "w_mem_kv", "w_mem_out",
                                                             "w_o", "w_up", "w_down"))),
        "x_t": features_down(np.concatenate([inp["x_prompt"][0], inp["x_sample"].reshape(TS, D)], 0)),
        "cst": constants(),
        "fea": per_feature(inp),
        "state_t": inp["state_ssm"][0].reshape(NB, GROUPS, GH, 64, P).transpose(1, 4, 0, 2, 3).reshape(GROUPS * P, -1),
        "mem_t": features_down(inp["mem_prompt"][0]),
        "k_pages": inp["cache_k"][0].reshape(-1, PAGE, 2, P).transpose(0, 3, 2, 1).reshape(-1, P, 2 * PAGE),
        "v_pages": inp["cache_v"][0].reshape(-1, PAGE, 2 * P),
        "mem_kt": inp["cache_mem_k"][0].reshape(NB, MEM, 4, 2, P).transpose(2, 4, 0, 3, 1).reshape(4 * P, -1),
        "mem_v": inp["cache_mem_v"][0].reshape(NB, 2, P, 4, MEM).transpose(3, 2, 0, 1, 4).reshape(4 * P, -1),
        "page_table": inp["page_table"].reshape(1, -1),
    }
    outs = {"y_t": (P, KT, T), "kv_t": (P, 4, T), "memkv_t": (P, 2 * KT, MEM), "ssm_p": (GROUPS * P, 256),
            "ssm_s": (GROUPS * P, NB * 256), "tails": (P, NCV * (PAD + NB * PAD)),
            "ftails": (P, 2 * FT * (FPAD + NB * FPAD))}

    nc = _bacc.Bacc("TRN2", target_bir_lowering=False, num_devices=1)
    arrays, io = {}, {}
    for name, a in data.items():
        a = np.ascontiguousarray(a)
        arrays[f"{name}_dram"] = a
        io[name] = nc.dram_tensor(f"{name}_dram", a.shape, mybir.dt.from_np(a.dtype), kind="ExternalInput").ap()
    for name, shape in outs.items():
        io[name] = nc.dram_tensor(f"{name}_dram", shape, F32, kind="ExternalOutput").ap()
    build_program(nc, io)
    result = _run(nc, [arrays], core_ids=[0]).results[0]
    got = {name: np.asarray(result[f"{name}_dram"]) for name in outs}

    def parts(a, rows):
        return a[:rows], a[rows:]

    y_p, y_s = parts(tokens_down(got["y_t"]), SEQ)
    k_p, k_s = parts(tokens_down(got["kv_t"][:, 0:2]), SEQ)
    v_p, v_s = parts(tokens_down(got["kv_t"][:, 2:4]), SEQ)
    mem_k, mem_v = (tokens_down(got["memkv_t"][:, j * KT:(j + 1) * KT]).reshape(1, 1, MEM, 4, 256) for j in range(2))
    ssm_p = got["ssm_p"].reshape(GROUPS, P, GH, 64).transpose(0, 2, 3, 1).reshape(1, 1, HEADS, 64, P)
    ssm_s = got["ssm_s"].reshape(GROUPS, P, NB, GH, 64).transpose(2, 0, 3, 4, 1).reshape(1, NB, HEADS, 64, P)
    conv_p, conv_s = parts(tokens_down(got["tails"].reshape(P, NCV, -1)), PAD)
    ffn_p, ffn_s = parts(tokens_down(got["ftails"].reshape(P, 2 * FT, -1)), FPAD)
    return tuple(np.ascontiguousarray(a) for a in (
        y_p.reshape(1, SEQ, D), y_s.reshape(NB, DT, D),
        k_p.reshape(1, 1, SEQ, 4, 64), v_p.reshape(1, 1, SEQ, 4, 64), mem_k, mem_v, ssm_p,
        conv_p.reshape(1, 1, PAD, -1), ffn_p.reshape(1, 1, FPAD, -1),
        k_s.reshape(1, NB, DT, 4, 64), v_s.reshape(1, NB, DT, 4, 64), ssm_s,
        conv_s.reshape(1, NB, PAD, -1), ffn_s.reshape(1, NB, FPAD, -1)))
```
